# Optimizing a Trainium2 kernel written in Bass

```python
import functools
import jax, jax.numpy as jnp
from jax import lax
import numpy as np

D_MODEL = 1024
BATCH = 1
SEQ = 1024
DEPTH = 1
DEC_BATCH = 8
DEC_SEQ = 4
PAST_LEN = 4096
PAGE_SIZE = 128

N_HEADS = 8
HEAD_DIM = 64
D_ATTN = N_HEADS * HEAD_DIM
Q_BLOCK = 128
FORGET_BIAS_MIN = 2.0
FORGET_BIAS_MAX = 12.0
D_GMLP = D_MODEL // 2
GMLP_GROUPS = 4
GMLP_GROUP_DIM = D_GMLP // GMLP_GROUPS
CHUNK = 128
N_GROUPS = 4
EXPERTS_PER_GROUP = 4
N_EXPERTS = N_GROUPS * EXPERTS_PER_GROUP
TOP_K = 2
D_EXPERT = D_MODEL // 4
ALPHA = (2.0 * DEPTH) ** 0.25
BETA = (8.0 * DEPTH) ** -0.25
LN_EPS = 1e-5
ADA_SCALE = 0.2
SPLIT_SIZES = (D_ATTN, D_ATTN, D_ATTN, N_HEADS, D_GMLP, D_GMLP, D_MODEL, D_MODEL)
SPLIT_POINTS = tuple(int(s) for s in np.cumsum(SPLIT_SIZES)[:-1])
D_IN = int(sum(SPLIT_SIZES))

kernel_name = 'fox_gmlp_hmoe_deepnorm_adaln_step'

def _layernorm(x, g, b):
    xf = x.astype(jnp.float32)
    mu = jnp.mean(xf, axis=-1, keepdims=True)
    var = jnp.mean(jnp.square(xf - mu), axis=-1, keepdims=True)
    return ((xf - mu) * lax.rsqrt(var + LN_EPS)).astype(x.dtype) * g + b

def _ada(c, w_ada, b_ada):
    m = jax.nn.silu(c) @ w_ada + b_ada
    return jnp.split(m[:, None, :], 6, axis=-1)

def _mixer_inputs(h, w_in, b_f, gln_g, gln_b):
    z = h @ w_in
    q, k, v, f, u, gv, ga, gg = jnp.split(z, SPLIT_POINTS, axis=-1)
    shp = h.shape[:-1] + (N_HEADS, HEAD_DIM)
    logf = jax.nn.log_sigmoid((f + b_f).astype(jnp.float32))
    u = jax.nn.gelu(u)
    gv = _layernorm(jax.nn.gelu(gv), gln_g, gln_b)
    return q.reshape(shp), k.reshape(shp), v.reshape(shp), logf, u, gv, ga, gg

def _fox_prompt(q, k, v, logf):
    b, s = q.shape[:2]
    nb = s // Q_BLOCK
    scale = HEAD_DIM ** -0.5
    cum = jnp.cumsum(logf, axis=1)
    cum_k = cum.transpose(0, 2, 1)[:, :, None, :]
    kpos = jnp.arange(s)

    def block(args):
        qb, cb, qpos = args
        sc = jnp.einsum('bqhd,bkhd->bhqk', qb, k).astype(jnp.float32) * scale
        sc = sc + cb.transpose(0, 2, 1)[..., None] - cum_k
        sc = jnp.where(kpos[None, :] <= qpos[:, None], sc, -jnp.inf)
        p = jax.nn.softmax(sc, axis=-1).astype(v.dtype)
        return jnp.einsum('bhqk,bkhd->bqhd', p, v)

    qb = q.reshape(b, nb, Q_BLOCK, N_HEADS, HEAD_DIM).transpose(1, 0, 2, 3, 4)
    cb = cum.reshape(b, nb, Q_BLOCK, N_HEADS).transpose(1, 0, 2, 3)
    qpos = kpos.reshape(nb, Q_BLOCK)
    o = lax.map(block, (qb, cb, qpos))
    return o.transpose(1, 0, 2, 3, 4).reshape(b, s, D_ATTN)

def _fox_sample(q, k, v, logf, k_past, v_past, logf_past):
    n = q.shape[1]
    p_len = k_past.shape[1]
    scale = HEAD_DIM ** -0.5
    lp = logf_past.astype(jnp.float32)
    suffix = lax.cumsum(lp, axis=1, reverse=True) - lp
    cn = jnp.cumsum(logf, axis=1)
    cn_t = cn.transpose(0, 2, 1)
    suf_t = suffix.transpose(0, 2, 1)
    s_past = jnp.einsum('bqhd,bkhd->bhqk', q, k_past).astype(jnp.float32) * scale
    s_past = s_past + cn_t[..., :, None] + suf_t[..., None, :]
    s_new = jnp.einsum('bqhd,bkhd->bhqk', q, k).astype(jnp.float32) * scale
    s_new = s_new + cn_t[..., :, None] - cn_t[..., None, :]
    causal = jnp.tril(jnp.ones((n, n), dtype=bool))
    s_new = jnp.where(causal, s_new, -jnp.inf)
    p = jax.nn.softmax(jnp.concatenate([s_past, s_new], axis=-1), axis=-1).astype(v.dtype)
    o = (jnp.einsum('bhqk,bkhd->bqhd', p[..., :p_len], v_past)
         + jnp.einsum('bhqk,bkhd->bqhd', p[..., p_len:], v))
    return o.reshape(q.shape[0], n, D_ATTN)

def _gmlp_prompt(u, gv, w_s, b_s):
    b, s, _ = gv.shape
    mask = jnp.tril(jnp.ones((CHUNK, CHUNK), dtype=bool))
    ws = jnp.where(mask, w_s, jnp.zeros_like(w_s))
    vg = gv.reshape(b, s // CHUNK, CHUNK, GMLP_GROUPS, GMLP_GROUP_DIM)
    sp = jnp.einsum('gts,bnsgc->bntgc', ws, vg) + b_s.T[:, :, None]
    return u * sp.reshape(b, s, D_GMLP)

def _gmlp_sample(u, gv, w_s, b_s):
    b, n, _ = gv.shape
    mask = jnp.tril(jnp.ones((n, n), dtype=bool))
    ws = w_s[:, :n, :n]
    ws = jnp.where(mask, ws, jnp.zeros_like(ws))
    vg = gv.reshape(b, n, GMLP_GROUPS, GMLP_GROUP_DIM)
    sp = jnp.einsum('gts,bsgc->btgc', ws, vg) + b_s[:, :n].T[:, :, None]
    return u * sp.reshape(b, n, D_GMLP)

def _moe(h, w_gr, b_gr, w_er, b_er, w_eg, w_eu, w_ed):
    shp = h.shape
    t = h.reshape(-1, D_MODEL)
    pg = jax.nn.softmax((t @ w_gr + b_gr).astype(jnp.float32), axis=-1)
    gi = jnp.argmax(pg, axis=-1)
    pg_top = jnp.take_along_axis(pg, gi[:, None], axis=-1)
    el = (t @ w_er + b_er).astype(jnp.float32).reshape(-1, N_GROUPS, EXPERTS_PER_GROUP)
    el = jnp.take_along_axis(el, gi[:, None, None], axis=1)[:, 0]
    tw, ti = lax.top_k(jax.nn.softmax(el, axis=-1), TOP_K)
    tw = tw / jnp.sum(tw, axis=-1, keepdims=True) * pg_top
    eid = gi[:, None] * EXPERTS_PER_GROUP + ti
    comb = jnp.sum(jax.nn.one_hot(eid, N_EXPERTS, dtype=jnp.float32) * tw[..., None], axis=1)
    comb = comb.astype(h.dtype)
    hg = jnp.einsum('nd,edf->nef', t, w_eg)
    hu = jnp.einsum('nd,edf->nef', t, w_eu)
    a = jax.nn.silu(hg) * hu * comb[..., None]
    out = jnp.einsum('nef,efd->nd', a, w_ed)
    return out.reshape(shp)

def _layer(x, c, fox_fn, gmlp_fn, w_ada, b_ada, w_in, b_f, gln_g, gln_b, w_ao, w_go, w_o,
           ln1_g, ln1_b, w_gr, b_gr, w_er, b_er, w_eg, w_eu, w_ed, ln2_g, ln2_b):
    sh1, sc1, g1, sh2, sc2, g2 = _ada(c, w_ada, b_ada)
    h = x * (1.0 + sc1) + sh1
    q, k, v, logf, u, gv, ga, gg = _mixer_inputs(h, w_in, b_f, gln_g, gln_b)
    a = fox_fn(q, k, v, logf)
    gm = gmlp_fn(u, gv)
    m = (jax.nn.sigmoid(ga) * (a @ w_ao) + jax.nn.sigmoid(gg) * (gm @ w_go)) @ w_o
    x = _layernorm(ALPHA * x + (1.0 + g1) * m, ln1_g, ln1_b)
    h2 = x * (1.0 + sc2) + sh2
    f = _moe(h2, w_gr, b_gr, w_er, b_er, w_eg, w_eu, w_ed)
    x = _layernorm(ALPHA * x + (1.0 + g2) * f, ln2_g, ln2_b)
    return x, k, v, logf, gv

def setup_inputs(seed: int = 0) -> dict:
    key = jax.random.key(seed)
    ks = iter(jax.random.split(key, 40))
    nrm = lambda shape: jax.random.normal(next(ks), shape, dtype=jnp.float32)
    n_pages = PAST_LEN // PAGE_SIZE
    n_pool = (5 * DEC_BATCH * n_pages) // 4
    page_table = jax.random.permutation(next(ks), n_pool)[:DEC_BATCH * n_pages]
    page_table = page_table.reshape(DEC_BATCH, n_pages).astype(jnp.int32)
    col_scale = jnp.concatenate([jnp.ones((2 * D_ATTN,), jnp.float32),
                                 jnp.full((D_ATTN,), BETA, jnp.float32),
                                 jnp.ones((D_IN - 3 * D_ATTN,), jnp.float32)])
    head_bias = jnp.linspace(FORGET_BIAS_MIN, FORGET_BIAS_MAX, N_HEADS, dtype=jnp.float32)
    return {
        'x_prompt': nrm((BATCH, SEQ, D_MODEL)),
        'x_sample': nrm((DEC_BATCH, DEC_SEQ, D_MODEL)),
        'c_prompt': nrm((BATCH, D_MODEL)),
        'c_sample': nrm((DEC_BATCH, D_MODEL)),
        'cache_k': nrm((DEPTH, n_pool, PAGE_SIZE, N_HEADS, HEAD_DIM)),
        'cache_v': nrm((DEPTH, n_pool, PAGE_SIZE, N_HEADS, HEAD_DIM)) * BETA,
        'cache_logf': jax.nn.log_sigmoid(head_bias + 0.5 * nrm((DEPTH, n_pool, PAGE_SIZE, N_HEADS))),
        'page_table': page_table,
        'w_ada': nrm((DEPTH, D_MODEL, 6 * D_MODEL)) * (ADA_SCALE * D_MODEL ** -0.5),
        'b_ada': nrm((DEPTH, 6 * D_MODEL)) * 0.01,
        'w_in': nrm((DEPTH, D_MODEL, D_IN)) * (D_MODEL ** -0.5) * col_scale,
        'b_f': head_bias[None, :] + 0.5 * nrm((DEPTH, N_HEADS)),
        'gmlp_ln_g': 1.0 + 0.05 * nrm((DEPTH, D_GMLP)),
        'gmlp_ln_b': 0.02 * nrm((DEPTH, D_GMLP)),
        'w_s': nrm((DEPTH, GMLP_GROUPS, CHUNK, CHUNK)) * (CHUNK ** -0.5),
        'b_s': 1.0 + 0.1 * nrm((DEPTH, GMLP_GROUPS, CHUNK)),
        'w_attn_out': nrm((DEPTH, D_ATTN, D_MODEL)) * (BETA * D_ATTN ** -0.5),
        'w_gmlp_out': nrm((DEPTH, D_GMLP, D_MODEL)) * (BETA * D_GMLP ** -0.5),
        'w_o': nrm((DEPTH, D_MODEL, D_MODEL)) * (BETA * D_MODEL ** -0.5),
        'ln1_g': 1.0 + 0.05 * nrm((DEPTH, D_MODEL)),
        'ln1_b': 0.02 * nrm((DEPTH, D_MODEL)),
        'w_group_router': nrm((DEPTH, D_MODEL, N_GROUPS)) * (D_MODEL ** -0.5),
        'b_group_router': 0.01 * nrm((DEPTH, N_GROUPS)),
        'w_expert_router': nrm((DEPTH, D_MODEL, N_EXPERTS)) * (D_MODEL ** -0.5),
        'b_expert_router': 0.01 * nrm((DEPTH, N_EXPERTS)),
        'w_exp_gate': nrm((DEPTH, N_EXPERTS, D_MODEL, D_EXPERT)) * (D_MODEL ** -0.5),
        'w_exp_up': nrm((DEPTH, N_EXPERTS, D_MODEL, D_EXPERT)) * (D_MODEL ** -0.5),
        'w_exp_down': nrm((DEPTH, N_EXPERTS, D_EXPERT, D_MODEL)) * (BETA * D_EXPERT ** -0.5),
        'ln2_g': 1.0 + 0.05 * nrm((DEPTH, D_MODEL)),
        'ln2_b': 0.02 * nrm((DEPTH, D_MODEL)),
    }

def reference(x_prompt, x_sample, c_prompt, c_sample, cache_k, cache_v, cache_logf, page_table,
              w_ada, b_ada, w_in, b_f, gmlp_ln_g, gmlp_ln_b, w_s, b_s, w_attn_out, w_gmlp_out,
              w_o, ln1_g, ln1_b, w_group_router, b_group_router, w_expert_router,
              b_expert_router, w_exp_gate, w_exp_up, w_exp_down, ln2_g, ln2_b):
    db = x_sample.shape[0]
    xp, xs = x_prompt, x_sample
    kp_l, vp_l, lfp_l, ks_l, vs_l, lfs_l, gvs_l = [], [], [], [], [], [], []
    for l in range(DEPTH):
        lw = (w_ada[l], b_ada[l], w_in[l], b_f[l], gmlp_ln_g[l], gmlp_ln_b[l], w_attn_out[l],
              w_gmlp_out[l], w_o[l], ln1_g[l], ln1_b[l], w_group_router[l], b_group_router[l],
              w_expert_router[l], b_expert_router[l], w_exp_gate[l], w_exp_up[l],
              w_exp_down[l], ln2_g[l], ln2_b[l])
        gp = functools.partial(_gmlp_prompt, w_s=w_s[l], b_s=b_s[l])
        xp, kp, vp, lfp, _ = _layer(xp, c_prompt, _fox_prompt, gp, *lw)
        k_past = cache_k[l][page_table].reshape(db, -1, N_HEADS, HEAD_DIM)
        v_past = cache_v[l][page_table].reshape(db, -1, N_HEADS, HEAD_DIM)
        lf_past = cache_logf[l][page_table].reshape(db, -1, N_HEADS)
        fs = functools.partial(_fox_sample, k_past=k_past, v_past=v_past, logf_past=lf_past)
        gs = functools.partial(_gmlp_sample, w_s=w_s[l], b_s=b_s[l])
        xs, ksn, vsn, lfs, gvs = _layer(xs, c_sample, fs, gs, *lw)
        kp_l.append(kp); vp_l.append(vp); lfp_l.append(lfp)
        ks_l.append(ksn); vs_l.append(vsn); lfs_l.append(lfs); gvs_l.append(gvs)
    return (xp, xs, jnp.stack(kp_l), jnp.stack(vp_l), jnp.stack(lfp_l),
            jnp.stack(ks_l), jnp.stack(vs_l), jnp.stack(lfs_l), jnp.stack(gvs_l))


_drawn_inputs = setup_inputs


def setup_inputs(seed=0):
    import zlib

    import numpy as np

    out = dict(_drawn_inputs(seed))
    spreads = {}
    factors = {'cache_k': 4.314,
     'cache_v': 3.675,
     'cache_logf': 3.27,
     'b_ada': 3.375,
     'gmlp_ln_b': 2.868,
     'b_s': 3.839,
     'b_group_router': 6.244,
     'b_expert_router': 8.0,
     'ln2_b': 2.932}
    for name, (base, spread) in spreads.items():
        noise = np.random.default_rng([zlib.crc32(name.encode()), seed]).standard_normal(out[name].shape)
        drawn = base * np.exp(spread * noise) if base else spread * noise
        out[name] = __import__('jax').numpy.asarray(drawn.astype(out[name].dtype))
    for name, factor in factors.items():
        out[name] = (out[name] * factor).astype(out[name].dtype)
    return out
```

```python
from contextlib import ExitStack

import numpy as np

import concourse.bass as bass
from concourse import mybir

F32 = mybir.dt.float32
I32 = mybir.dt.int32
ALU = mybir.AluOpType
ACT = mybir.ActivationFunctionType
AX = mybir.AxisListType

P = 128
D = 1024
KD = D // P
SEQ = 1024
DEC_B, DEC_S = 8, 4
NS = DEC_B * DEC_S
T = SEQ + NS
PT = SEQ // P
NT = PT + 1
BLK = T // 3
H, HD = 8, 64
DA = H * HD
DG = 512
NGRP = DG // P
PAGES = 32
NB = 1 + DEC_B
COL_Q, COL_K, COL_V = 0, DA, 2 * DA
COL_F = 3 * DA
COL_U = COL_F + H
COL_GV = COL_U + DG
COL_GA = COL_GV + DG
COL_GG = COL_GA + D
ALPHA = 2.0 ** 0.25
EPS = 1e-5
NEG = -1e30
NEXP, EPG, NG = 16, 4, 4
DE = 256
TILE_ROWS = [P] * PT + [NS]


START = 1


class Chain:

    def __init__(self, eng, sem):
        self.eng, self.sem, self.base, self.n = eng, sem, 0, 0

    def __call__(self, ins):
        ins.then_inc(self.sem, 1)
        self.n += 1
        self.eng.wait_ge(self.sem, self.base + self.n)

    def enter(self, it, per):
        self.before, self.per = self.base + self.n, per
        self.base, self.n = self.before + it * per, 0

    def leave(self, trips):
        assert self.n == self.per, (self.n, self.per)
        self.base, self.n = self.before + trips * self.per, 0


class Mem:

    def __init__(self, nc, ctx, tag):
        self.nc, self.ctx, self.tag, self.taken = nc, ctx, tag, []
        ctx.callback(self.release)

    def sb(self, name, shape, dt=F32):
        return self.ctx.enter_context(self.nc.sbuf_tensor(f"{self.tag}_{name}", shape, dt))

    def sem(self, name):
        self.taken.append(self.nc.alloc_semaphore(f"{self.tag}_{name}"))
        return self.taken[-1]

    def sems(self, name, n):
        return [self.sem(f"{name}{i}") for i in range(n)]

    def start(self, sems):
        for sem in sems:
            self.nc.gpsimd.sem_inc(sem, START)
        self.nc.all_engine_barrier()

    def release(self):
        if self.taken:
            self.nc.clear_and_free_semaphores(self.taken)
            self.nc.all_engine_barrier()


def modulate(nc, io, g, ps):
    with ExitStack() as ctx:
        m = Mem(nc, ctx, "mod")
        c_sb, cs = m.sb("c", [NB, D]), m.sb("cs", [NB, D])
        csT = m.sb("csT", [P, KD, NB])
        b_bc = m.sb("b_bc", [NB, 6 * D])
        ada = m.sb("ada", [NB, 6, D])
        ada_out = m.sem("ada_out")
        w = [g.arena[:, KD * T:KD * T + KD * D].rearrange("p (k n) -> p k n", k=KD), m.sb("w1", [P, KD, D])]
        x_sb, xs_sb = m.sb("x", [P, PT, D]), m.sb("xs", [NS, D])
        modT = m.sb("modT", [P, 2, KD, NB])
        hs = m.sb("hs", [P, KD, NS])
        ones = g.ones
        zero = m.sem("zero")
        consts = m.sem("consts")
        c_in, bias_in, x_in = m.sem("c_in"), m.sem("bias_in"), m.sem("x_in")
        w_in = m.sems("w_in", 2)
        silu_done, cT_done, cT_copied = m.sem("silu"), m.sem("cT_done"), m.sem("cT_copied")
        ada_mm, ada_copied = m.sems("ada_mm", 2), m.sems("ada_copied", 2)
        modT_done, modT_copied = m.sem("modT_done"), m.sem("modT_copied")
        xT_done, hT_done = m.sems("xT_done", 4), m.sems("hT_done", 4)
        own = m.sem("own")
        xsT_done = m.sem("xsT_done")
        w_v = io["w_ada"][0].rearrange("(k p) n -> p k n", p=P)

        m.start(ada_mm + ada_copied)

        with nc.Block() as block:
            @block.sync
            def _(sp):
                sp.dma_start(c_sb[0:1, :], io["c_prompt"]).then_inc(c_in, 16)
                sp.dma_start(c_sb[1:NB, :], io["c_sample"]).then_inc(c_in, 16)
                sp.dma_start(b_bc[:], io["b_ada"].partition_broadcast(NB).rearrange("p a n -> p (a n)")).then_inc(bias_in, 16)
                with sp.Fori(0, 3) as it:
                    for s in range(2):
                        sp.wait_ge(ada_mm[s], START + it)
                        sp.dma_start(w[s][:, :, :], w_v[:, :, bass.ds((2 * it + s) * D, D)]).then_inc(w_in[s], 16)
                for s in range(2):
                    sp.wait_ge(ada_copied[s], START + 3)
                sp.dma_start(g.ada_rows, ada[:]).then_inc(ada_out, 16)
                sp.wait_ge(ada_out, 16)

            @block.gpsimd
            def _(pool):
                pool.dma_start(x_sb[:], io["x_prompt"][0].rearrange("(t p) d -> p t d", p=P)).then_inc(x_in, 16)
                pool.dma_start(xs_sb[:], io["x_sample"].rearrange("b s d -> (b s) d")).then_inc(x_in, 16)
                nc.gpsimd.memset(g.ident[:], 0.0).then_inc(zero, 1)
                nc.gpsimd.memset(ones[:], 1.0).then_inc(zero, 1)
                nc.gpsimd.memset(g.causal[:], 0.0).then_inc(zero, 1)
                pool.wait_ge(zero, 3)
                nc.gpsimd.affine_select(out=g.ident[:], in_=g.ident[:], compare_op=ALU.not_equal, fill=1.0, base=0,
                                        pattern=[[-1, P]], channel_multiplier=1).then_inc(consts, 1)
                nc.gpsimd.affine_select(out=g.before[:], in_=ones[:, 0:P], compare_op=ALU.is_gt, fill=0.0, base=0,
                                        pattern=[[1, P]], channel_multiplier=-1).then_inc(consts, 1)
                nc.gpsimd.memset(g.after[:, 0:3 * P], 1.0).then_inc(consts, 1)
                nc.gpsimd.affine_select(out=g.after[:, 3 * P:4 * P], in_=ones[:, 0:P], compare_op=ALU.is_gt, fill=0.0,
                                        base=0, pattern=[[-1, P]], channel_multiplier=1).then_inc(consts, 1)
                nc.gpsimd.affine_select(out=g.causal[:], in_=g.causal[:], compare_op=ALU.is_ge, fill=NEG, base=0,
                                        pattern=[[-1, P]], channel_multiplier=1).then_inc(consts, 1)

            @block.scalar
            def _(act):
                act.wait_ge(c_in, 32)
                nc.scalar.activation(cs[:], c_sb[:], ACT.Silu).then_inc(silu_done, 1)
                act.wait_ge(modT_copied, 2)
                for k in range(0, KD, 2):
                    for half in range(2):
                        b = 2 * ((k // 2) % 2) + half
                        act.wait_ge(xT_done[b], k // 4 + 1)
                        nc.scalar.activation(g.hT[:, k, half * 512:half * 512 + 512], ps[:, b, :], ACT.Identity,
                                             scale=modT[:, 1, k, 0:1], bias=modT[:, 0, k, 0:1]).then_inc(hT_done[b], 1)

            @block.tensor
            def _(pe):
                pe.wait_ge(silu_done, 1)
                pe.wait_ge(consts, 1)
                for k in range(KD):
                    last = nc.tensor.transpose(ps[:, 0, 16 * k:16 * k + NB], cs[:, k * P:k * P + P], g.ident[0:NB, 0:NB])
                last.then_inc(cT_done, 1)
                pe.wait_ge(cT_copied, 1)
                with pe.Fori(0, 3) as it:
                    for s in range(2):
                        pe.wait_ge(w_in[s], 16 * it + 16)
                        pe.wait_ge(ada_copied[s], START + it)
                        for k in range(KD):
                            for j in range(4):
                                last = nc.tensor.matmul(ps[32 * j:32 * j + NB, 1 + s, 0:256], csT[:, k, :],
                                                        w[s][:, k, 256 * j:256 * j + 256],
                                                        start=(k == 0), stop=(k == KD - 1))
                        last.then_inc(ada_mm[s], 1)
                for s in range(2):
                    pe.wait_ge(ada_copied[s], START + 3)
                for r in range(2):
                    for k in range(KD):
                        last = nc.tensor.transpose(ps[:, 3, 16 * (KD * r + k):16 * (KD * r + k) + NB],
                                                   ada[:, r, k * P:k * P + P], g.ident[0:NB, 0:NB])
                last.then_inc(modT_done, 1)
                pe.wait_ge(modT_copied, 2)
                pe.wait_ge(x_in, 32)
                for k in range(KD):
                    for half in range(2):
                        b = (4 if k % 2 else 0) + 2 * ((k // 2) % 2) + half
                        if b < 4:
                            pe.wait_ge(hT_done[b], k // 4)
                        else:
                            pe.wait_ge(g.hT_odd[b - 4], k // 4)
                        for i in range(4):
                            last = nc.tensor.transpose(ps[:, b, i * P:i * P + P],
                                                       x_sb[:, 4 * half + i, k * P:k * P + P], g.ident[:])
                        last.then_inc(xT_done[b] if b < 4 else g.xT_odd[b - 4], 1)
                pe.wait_ge(hT_done[0], 2)
                for k in range(KD):
                    last = nc.tensor.transpose(ps[:, 0, NS * k:NS * k + NS], xs_sb[:, k * P:k * P + P],
                                               g.ident[0:NS, 0:NS])
                last.then_inc(xsT_done, 1)

            @block.vector
            def _(dve):
                link = Chain(dve, own)
                dve.wait_ge(cT_done, 1)
                nc.vector.tensor_copy(csT[:], ps[:, 0, 0:16 * KD].rearrange("p (k n) -> p k n", n=16)[:, :, 0:NB])\
                    .then_inc(cT_copied, 1)
                dve.wait_ge(bias_in, 16)
                with dve.Fori(0, 3) as it:
                    for s in range(2):
                        dve.wait_ge(ada_mm[s], START + it + 1)
                        for j in range(4):
                            last = nc.vector.tensor_tensor(
                                ada[:, bass.ds(2 * it + s, 1), 256 * j:256 * j + 256].rearrange("p a n -> p (a n)"),
                                ps[32 * j:32 * j + NB, 1 + s, 0:256],
                                b_bc[:, bass.ds((2 * it + s) * D + 256 * j, 256)], ALU.add)
                        last.then_inc(ada_copied[s], 1)
                dve.wait_ge(modT_done, 1)
                mT = ps[:, 3, 0:32 * KD].rearrange("p (r k n) -> p r k n", r=2, n=16)
                nc.vector.tensor_copy(modT[:, 0], mT[:, 0, :, 0:NB]).then_inc(modT_copied, 1)
                nc.vector.tensor_scalar(modT[:, 1], mT[:, 1, :, 0:NB], 1.0, None, ALU.add).then_inc(modT_copied, 1)
                dve.wait_ge(modT_copied, 2)
                for k in range(1, KD, 2):
                    for half in range(2):
                        b = 2 * ((k // 2) % 2) + half
                        dve.wait_ge(g.xT_odd[b], k // 4 + 1)
                        nc.vector.tensor_scalar(g.hT[:, k, half * 512:half * 512 + 512], ps[:, 4 + b, :],
                                                modT[:, 1, k, 0:1], modT[:, 0, k, 0:1], ALU.mult, ALU.add)\
                            .then_inc(g.hT_odd[b], 1)
                dve.wait_ge(xsT_done, 1)
                seqs = "p k (b s) -> p k b s"
                per_seq = [modT[:, r, :, 1:NB].unsqueeze(3).to_broadcast([P, KD, DEC_B, DEC_S]) for r in range(2)]
                link(nc.vector.tensor_tensor(hs[:].rearrange(seqs, s=DEC_S),
                                             ps[:, 0, 0:NS * KD].rearrange("p (k b s) -> p k b s", k=KD, s=DEC_S),
                                             per_seq[1], ALU.mult))
                link(nc.vector.tensor_tensor(g.hT[:, :, SEQ:T].rearrange(seqs, s=DEC_S),
                                             hs[:].rearrange(seqs, s=DEC_S), per_seq[0], ALU.add))


def project_in(nc, io, g, ps):
    with ExitStack() as ctx:
        m = Mem(nc, ctx, "pin")
        w = [m.sb(f"w{i}", [P, KD, 512]) for i in range(2)]
        w_f = m.sb("w_f", [P, KD, H])
        bf = m.sb("bf", [H, 1])
        f_x, f_e, f_u, f_l = (m.sb(n, [H, T]) for n in ("f_x", "f_e", "f_u", "f_l"))
        f_one = m.sb("f_one", [H, SEQ])
        logfT, ncumT, logf = m.sb("logfT", [H, T]), m.sb("ncumT", [H, T]), m.sb("logf", [P, NT, H])
        w_in, w_used = m.sems("w_in", 2), m.sems("w_used", 2)
        f_in = m.sem("f_in")
        full, free = m.sems("full", 6), m.sems("free", 6)
        u_w, u_full, u_free = m.sem("u_w"), m.sems("u_full", 6), m.sems("u_free", 6)
        f_full, own, act_own = m.sem("f_full"), m.sem("own"), m.sem("act_own")
        f_abs, f_exp, f_log, f_cum = m.sem("f_abs"), m.sem("f_exp"), m.sem("f_log"), m.sem("f_cum")
        fT_done = m.sem("fT_done")
        out = m.sem("out")
        w_v = io["w_in"][0].rearrange("(k p) n -> p k n", p=P)
        GROUPS = 2 * NT
        USES = GROUPS // 6

        m.start(w_used + free)

        with nc.Block() as block:
            @block.sync
            def _(sp):
                with nc.allow_non_contiguous_dma(reason="eight columns"):
                    sp.dma_start(w_f[:], w_v[:, :, COL_F:COL_F + H]).then_inc(f_in, 16)
                    sp.dma_start(bf[:], io["b_f"].rearrange("a h -> h a")).then_inc(f_in, 16)
                with sp.Fori(0, 2) as it:
                    for s, (at, by) in enumerate(((COL_Q, COL_V - COL_Q), (COL_K, COL_GV - COL_K))):
                        sp.wait_ge(w_used[s], START + it)
                        sp.dma_start(w[s][:], w_v[:, :, bass.ds(it * by + at, 512)]).then_inc(w_in[s], 16)
                sp.wait_ge(w_used[0], START + 2)
                sp.dma_start(w[0][:], w_v[:, :, COL_U:COL_U + DG]).then_inc(u_w, 16)

            @block.tensor
            def _(pe):
                pe.wait_ge(f_in, 32)
                for k in range(KD):
                    for j in range(3):
                        last = nc.tensor.matmul(ps[32 * j:32 * j + H, 6, 0:BLK], w_f[:, k, :],
                                                g.hT[:, k, j * BLK:(j + 1) * BLK], start=(k == 0), stop=(k == KD - 1))
                last.then_inc(f_full, 1)
                with pe.Fori(0, 2) as it:
                    for s in range(2):
                        pe.wait_ge(w_in[s], 16 * it + 16)
                        for t in range(NT):
                            n = s * NT + t
                            b, use, rows = n % 6, n // 6, TILE_ROWS[t]
                            pe.wait_ge(free[b], START + it * USES + use)
                            for k in range(KD):
                                last = nc.tensor.matmul(ps[0:rows, b, :], g.hT[:, k, t * P:t * P + rows], w[s][:, k, :],
                                                        start=(k == 0), stop=(k == KD - 1))
                            last.then_inc(full[b], 1)
                pe.wait_ge(u_w, 16)
                for i in range(NGRP):
                    for j in range(3):
                        n = 3 * i + j
                        b = n % 6
                        pe.wait_ge(free[b], START + 2 * USES)
                        pe.wait_ge(u_free[b], n // 6)
                        for k in range(KD):
                            last = nc.tensor.matmul(ps[:, b, 0:BLK], w[0][:, k, i * P:i * P + P],
                                                    g.hT[:, k, j * BLK:(j + 1) * BLK], start=(k == 0), stop=(k == KD - 1))
                        last.then_inc(u_full[b], 1)
                pe.wait_ge(f_cum, 1)
                for r, src in enumerate((logfT, ncumT)):
                    for t in range(NT):
                        rows = TILE_ROWS[t]
                        last = nc.tensor.transpose(ps[0:rows, 7, (r * NT + t) * H:(r * NT + t + 1) * H],
                                                   src[:, t * P:t * P + rows], g.ident[0:H, 0:H])
                last.then_inc(fT_done, 1)

            def evacuate(eng, copy, parity):
                with eng.Fori(0, 2) as it:
                    for n in range(GROUPS):
                        b, use, s, t = n % 6, n // 6, n // NT, n % NT
                        if b % 2 == parity:
                            eng.wait_ge(full[b], it * USES + use + 1)
                            if t == NT - 1:
                                eng.sem_inc(w_used[s], 1)
                            copy(g.z[0:TILE_ROWS[t], bass.ds(it, 1), s, t, :].rearrange("p a n -> p (a n)"),
                                 ps[0:TILE_ROWS[t], b, :]).then_inc(free[b], 1)

            @block.vector
            def _(dve):
                link = Chain(dve, own)
                dve.wait_ge(f_full, 1)
                dve.wait_ge(f_in, 32)
                for j in range(3):
                    last = nc.vector.tensor_scalar(f_x[:, j * BLK:(j + 1) * BLK], ps[32 * j:32 * j + H, 6, 0:BLK],
                                                   bf[:, 0:1], None, ALU.add)
                link(last)
                nc.vector.scalar_tensor_tensor(out=f_l[:], in0=f_x[:], scalar=-1.0, in1=f_x[:], op0=ALU.mult,
                                               op1=ALU.max).then_inc(f_abs, 1)
                evacuate(dve, nc.vector.tensor_copy, 0)
                dve.wait_ge(f_exp, 1)
                link(nc.vector.tensor_scalar(f_u[:], f_e[:], 1.0, None, ALU.add))
                link(nc.vector.memset(f_one[:], 1.0))
                nc.vector.scalar_tensor_tensor(out=f_e[:], in0=f_u[:], scalar=-1.0, in1=f_e[:], op0=ALU.add,
                                               op1=ALU.subtract).then_inc(f_abs, 1)
                dve.wait_ge(f_log, 1)
                link(nc.vector.reciprocal(f_u[:], f_u[:]))
                link(nc.vector.tensor_tensor(f_e[:], f_e[:], f_u[:], ALU.mult))
                link(nc.vector.tensor_tensor(f_l[:], f_e[:], f_l[:], ALU.subtract))
                link(nc.vector.scalar_tensor_tensor(out=logfT[:], in0=f_x[:], scalar=0.0, in1=f_l[:], op0=ALU.min,
                                                    op1=ALU.add))
                link(nc.vector.tensor_scalar(f_x[:], logfT[:], -1.0, None, ALU.mult))
                link(nc.vector.tensor_tensor_scan(ncumT[:, 0:SEQ], f_one[:], f_x[:, 0:SEQ], 0.0, ALU.mult, ALU.add))
                cs = ncumT[:, SEQ:T].rearrange("h (b s) -> h b s", s=DEC_S)
                xs = f_x[:, SEQ:T].rearrange("h (b s) -> h b s", s=DEC_S)
                link(nc.vector.tensor_copy(cs[:, :, 0], xs[:, :, 0]))
                for s in range(1, DEC_S):
                    last = nc.vector.tensor_tensor(cs[:, :, s], cs[:, :, s - 1], xs[:, :, s], ALU.add)
                    if s < DEC_S - 1:
                        link(last)
                last.then_inc(f_cum, 1)
                dve.wait_ge(f_cum, 1)
                nc.vector.tensor_copy(g.ncum_new[:], ncumT[:, SEQ:T])
                dve.wait_ge(fT_done, 1)
                for r, dst in enumerate((logf, g.ncum)):
                    nc.vector.tensor_copy(dst[:, 0:PT, :], ps[:, 7, r * NT * H:(r * NT + PT) * H]
                                          .rearrange("p (t h) -> p t h", h=H)).then_inc(f_abs, 1)
                    nc.vector.tensor_copy(dst[0:NS, PT, :], ps[0:NS, 7, (r * NT + PT) * H:(r + 1) * NT * H])\
                        .then_inc(f_abs, 1)

            @block.scalar
            def _(act):
                evacuate(act, nc.scalar.copy, 1)
                act.wait_ge(f_abs, 1)
                nc.scalar.activation(f_e[:], f_l[:], ACT.Exp, scale=-1.0).then_inc(f_exp, 1)
                act.wait_ge(f_abs, 2)
                nc.scalar.activation(f_l[:], f_u[:], ACT.Ln).then_inc(f_log, 1)
                for n in range(3 * NGRP):
                    i, j, b = n // 3, n % 3, n % 6
                    act.wait_ge(u_full[b], n // 6 + 1)
                    nc.scalar.activation(g.uT[:, i, j * BLK:(j + 1) * BLK], ps[:, b, 0:BLK], ACT.Gelu_apprx_tanh)\
                        .then_inc(u_free[b], 1)

            @block.gpsimd
            def _(pool):
                for b in range(6):
                    pool.wait_ge(free[b], START + 2 * USES)
                tok = "(t p) n -> p t n"
                for dst, dst_s, src in ((io["new_k_prompt"], io["new_k_sample"], g.z[:, 0, 1]),
                                        (io["new_v_prompt"], io["new_v_sample"], g.z[:, 1, 0])):
                    pool.dma_start(dst[0, 0].rearrange("s h d -> s (h d)").rearrange(tok, p=P), src[:, 0:PT, :])\
                        .then_inc(out, 16)
                    pool.dma_start(dst_s[0].rearrange("b s h d -> (b s) (h d)"), src[0:NS, PT, :]).then_inc(out, 16)
                pool.wait_ge(f_abs, 6)
                with nc.allow_non_contiguous_dma(reason="eight columns"):
                    pool.dma_start(io["new_logf_prompt"][0, 0].rearrange(tok, p=P), logf[:, 0:PT, :]).then_inc(out, 16)
                    pool.dma_start(io["new_logf_sample"][0].rearrange("b s h -> (b s) h"), logf[0:NS, PT, :])\
                        .then_inc(out, 16)
                pool.wait_ge(out, 6 * 16)


def gmlp(nc, io, g, ps):
    with ExitStack() as ctx:
        m = Mem(nc, ctx, "gm")
        ws, wsT = m.sb("ws", [P, NGRP, P]), m.sb("wsT", [P, NGRP, P])
        ws_new = m.sb("ws_new", [NS, NGRP, NS])
        upto = m.sb("upto", [P, P])
        bs = m.sb("bs", [P, NGRP, P])
        ln_g, ln_b = m.sb("ln_g", [P, DG]), m.sb("ln_b", [P, DG])
        stats, mv, rstd = m.sb("stats", [P, NT, 6]), m.sb("mv", [P, NT, 2]), m.sb("rstd", [P, NT])
        sp_b = [m.sb(f"sp{i}", [P, NGRP, P]) for i in range(2)]
        eps = m.sb("eps", [P, 1])
        loaded, cleared, new_in, masked = m.sem("loaded"), m.sem("cleared"), m.sem("new_in"), m.sem("masked")
        gelu, have_var, have_std, normed = m.sem("gelu"), m.sem("have_var"), m.sem("have_std"), m.sem("normed")
        wsT_done, wsT_ready = m.sem("wsT_done"), m.sem("wsT_ready")
        sp_full, sp_free = m.sems("sp_full", 2), m.sems("sp_free", 2)
        own, out, q_scaled = m.sem("own"), m.sem("out"), m.sem("q_scaled")
        gv = g.z[:, 1, 1]

        with nc.Block() as block:
            @block.sync
            def _(sp):
                sp.dma_start(ws[:], io["w_s"][0].rearrange("g t s -> t g s")).then_inc(loaded, 16)
                sp.dma_start(bs[:].rearrange("p g t -> p (g t)"),
                             io["b_s"].rearrange("a g t -> a (g t)").partition_broadcast(P)
                             .rearrange("p a n -> p (a n)")).then_inc(loaded, 16)
                sp.dma_start(ln_g[:], io["gmlp_ln_g"].partition_broadcast(P).rearrange("p a n -> p (a n)")).then_inc(loaded, 16)
                sp.dma_start(ln_b[:], io["gmlp_ln_b"].partition_broadcast(P).rearrange("p a n -> p (a n)")).then_inc(loaded, 16)
                sp.wait_ge(cleared, 1)
                with nc.allow_non_contiguous_dma(reason="4x4 corners of w_s, transposed"):
                    for b in range(DEC_B):
                        at = slice(b * DEC_S, (b + 1) * DEC_S)
                        for grp in range(NGRP):
                            sp.dma_start(ws_new[at, grp, at],
                                         io["w_s"][0, grp, 0:DEC_S, 0:DEC_S].rearrange("t s -> s t")).then_inc(new_in, 16)
                sp.wait_ge(q_scaled, 1)
                sp.dma_start(g.q_rows, g.z[0:NS, 0, 0, PT, :]).then_inc(out, 16)
                sp.wait_ge(normed, NT)
                sp.dma_start(io["new_gmlp_v_sample"][0].rearrange("b s n -> (b s) n"), gv[0:NS, PT, :]).then_inc(out, 16)
                sp.wait_ge(out, 32)

            @block.gpsimd
            def _(pool):
                nc.gpsimd.memset(ws_new[:], 0.0).then_inc(cleared, 1)
                nc.gpsimd.affine_select(out=upto[:], in_=g.ones[:, 0:P], compare_op=ALU.is_ge, fill=0.0, base=0,
                                        pattern=[[1, P]], channel_multiplier=-1).then_inc(masked, 1)
                nc.gpsimd.memset(mv[:], 1.0).then_inc(masked, 1)
                nc.gpsimd.memset(eps[:], EPS).then_inc(masked, 1)
                nc.gpsimd.tensor_scalar(g.z[:, 0, 0, 0:PT, :], g.z[:, 0, 0, 0:PT, :], HD ** -0.5, None, ALU.mult)
                nc.gpsimd.tensor_scalar(g.z[0:NS, 0, 0, PT, :], g.z[0:NS, 0, 0, PT, :], HD ** -0.5, None, ALU.mult)\
                    .then_inc(q_scaled, 1)

            @block.scalar
            def _(act):
                for t in range(NT):
                    at = gv[0:TILE_ROWS[t], t, :]
                    nc.scalar.activation(at, at, ACT.Gelu_apprx_tanh).then_inc(gelu, 1)
                act.wait_ge(have_var, 1)
                nc.scalar.activation(rstd[:], mv[:, :, 1], ACT.Sqrt, bias=eps[:, 0:1]).then_inc(have_std, 1)

            @block.tensor
            def _(pe):
                pe.wait_ge(loaded, 64)
                for i in range(NGRP):
                    last = nc.tensor.transpose(ps[:, 0, i * P:(i + 1) * P], ws[:, i, :], g.ident[:])
                last.then_inc(wsT_done, 1)
                pe.wait_ge(wsT_ready, 2)
                for t in range(NT):
                    rows, b = TILE_ROWS[t], t % 2
                    pe.wait_ge(normed, t + 1)
                    pe.wait_ge(sp_free[b], t // 2)
                    for i in range(NGRP):
                        last = nc.tensor.matmul(ps[:, 1 + b, i * rows:(i + 1) * rows], gv[0:rows, t, i * P:(i + 1) * P],
                                                wsT[:, i, :] if t < PT else ws_new[:, i, :], start=True, stop=True)
                    last.then_inc(sp_full[b], 1)

            @block.vector
            def _(dve):
                link = Chain(dve, own)
                dve.wait_ge(masked, 3)
                dve.wait_ge(wsT_done, 1)
                nc.vector.tensor_tensor(wsT[:], ps[:, 0, :].rearrange("p (g t) -> p g t", g=NGRP),
                                        upto[:].unsqueeze(1).to_broadcast([P, NGRP, P]), ALU.mult).then_inc(wsT_ready, 1)
                dve.wait_ge(new_in, 16 * DEC_B * NGRP)
                nc.vector.tensor_tensor(ws_new[:], ws_new[:], upto[0:NS, 0:NS].unsqueeze(1)
                                        .to_broadcast([NS, NGRP, NS]), ALU.mult).then_inc(wsT_ready, 1)
                for t in range(NT):
                    rows = TILE_ROWS[t]
                    dve.wait_ge(gelu, t + 1)
                    last = nc.vector.bn_stats(stats[0:rows, t, :], gv[0:rows, t, :])
                    link(last)
                for t in range(NT):
                    rows = TILE_ROWS[t]
                    last = nc.vector.bn_aggr(mv[0:rows, t, :], stats[0:rows, t, :])
                    if t < NT - 1:
                        link(last)
                last.then_inc(have_var, 1)
                dve.wait_ge(have_std, 1)
                link(nc.vector.reciprocal(rstd[:], rstd[:]))
                dve.wait_ge(loaded, 64)

                def norm(t):
                    rows = TILE_ROWS[t]
                    at = gv[0:rows, t, :]
                    link(nc.vector.scalar_tensor_tensor(out=at, in0=at, scalar=mv[0:rows, t, 0:1], in1=ln_g[0:rows, :],
                                                        op0=ALU.subtract, op1=ALU.mult))
                    nc.vector.scalar_tensor_tensor(out=at, in0=at, scalar=rstd[0:rows, t:t + 1], in1=ln_b[0:rows, :],
                                                   op0=ALU.mult, op1=ALU.add).then_inc(normed, 1)

                def gate(t):
                    b = t % 2
                    dve.wait_ge(sp_full[b], t // 2 + 1)
                    if t < PT:
                        u = g.uT[:, :, t * P:(t + 1) * P]
                        spt = sp_b[b][:]
                        nc.vector.tensor_tensor(spt, ps[:, 1 + b, :].rearrange("p (g t) -> p g t", g=NGRP), bs[:],
                                                ALU.add).then_inc(sp_free[b], 1)
                    else:
                        u = g.uT[:, :, SEQ:T]
                        spt = sp_b[b][:, :, 0:NS]
                        split = "p g (b s) -> p g b s"
                        nc.vector.tensor_tensor(spt.rearrange(split, s=DEC_S),
                                                ps[:, 1 + b, 0:NGRP * NS].rearrange("p (g b s) -> p g b s", g=NGRP, s=DEC_S),
                                                bs[:, :, 0:DEC_S].unsqueeze(2).to_broadcast([P, NGRP, DEC_B, DEC_S]),
                                                ALU.add).then_inc(sp_free[b], 1)
                    dve.wait_ge(sp_free[b], t // 2 + 1)
                    link(nc.vector.tensor_tensor(u, spt, u, ALU.mult))

                for t in range(NT + 1):
                    if t < NT:
                        norm(t)
                    if t:
                        gate(t - 1)


def attend_prompt(nc, io, g, ps):
    HA = HD + 2
    LAG, NPB = 3, 4
    UNITS = 2 * PT
    QB = 4

    groups, upto = [], {}
    for hh in range(2):
        for which in range(2):
            for half in range(2):
                groups.append(("qk", hh, which, half))
    for u in range(UNITS):
        i = u // 2
        for kb in range(0, i + 1, 4):
            groups.append(("p", u, kb, min(4, i + 1 - kb)))
        upto[u] = len(groups)
    USES = len(groups) // 2
    assert len(groups) % 2 == 0

    with ExitStack() as ctx:
        m = Mem(nc, ctx, "pat")
        qa, ka = m.sb("qa", [P, PT, 2, HA]), m.sb("ka", [P, PT, 2, HA])
        va = m.sb("va", [P, PT, 2 * HD])
        qkT = m.sb("qkT", [HA, 2, 2, SEQ])
        pr = [m.sb(f"pr{i}", [P, SEQ]) for i in range(NPB)]
        prT = [m.sb("prT", [P, PT, QB * P]), g.z[:, 1, 1, 0:PT, :]]
        nmax, rsum = m.sb("nmax", [P, NPB]), m.sb("rsum", [P, NPB])
        cum = m.sb("cum", [P, PT, H])
        one_set, cum_set = m.sem("one_set"), m.sem("cum_set")
        qk_staged, v_staged = m.sem("qk_staged"), m.sem("v_staged")
        t_full, t_free = m.sems("t_full", 2), m.sems("t_free", 2)
        s_full, masked, have_max = m.sems("s_full", 2), m.sem("masked"), m.sem("have_max")
        exped = m.sems("exped", NPB)
        have_recip, scaled = m.sem("have_recip"), m.sems("scaled", NPB)
        pv_done, pv_free = m.sems("pv_done", 2), m.sems("pv_free", 2)
        PER_BUF = UNITS // NPB

        def t_count(it, n):
            return [it * USES + (n + 1) // 2, it * USES + n // 2]

        m.start(t_full + pv_done + t_free + exped + pv_free)

        with nc.Block() as block:
            @block.gpsimd
            def _(pool):
                nc.gpsimd.memset(qa[:, :, :, HD:HD + 1], 1.0).then_inc(one_set, 1)
                nc.gpsimd.memset(ka[:, :, :, HD + 1:HA], 1.0).then_inc(one_set, 1)
                nc.gpsimd.tensor_scalar(cum[:], g.ncum[:, 0:PT, :], -1.0, None, ALU.mult).then_inc(cum_set, 1)
                pool.wait_ge(cum_set, 1)
                with pool.Fori(0, H // 2) as it:
                    for b in range(2):
                        pool.wait_ge(t_full[b], START + it * USES)
                    heads = "p t (h d) -> p t h d"
                    for dst, at in ((qa, 0), (ka, 1)):
                        nc.gpsimd.tensor_copy(dst[:, :, :, 0:HD], g.z[:, 0, at, 0:PT, bass.ds(it * 2 * HD, 2 * HD)]
                                              .rearrange(heads, h=2)).then_inc(qk_staged, 1)
                    nc.gpsimd.tensor_copy(ka[:, :, :, HD], g.ncum[:, 0:PT, bass.ds(2 * it, 2)]).then_inc(qk_staged, 1)
                    nc.gpsimd.tensor_copy(qa[:, :, :, HD + 1], cum[:, :, bass.ds(2 * it, 2)]).then_inc(qk_staged, 1)
                    pool.wait_ge(pv_done[1], START + it)
                    nc.gpsimd.tensor_copy(va[:], g.z[:, 1, 0, 0:PT, bass.ds(it * 2 * HD, 2 * HD)]).then_inc(v_staged, 1)

            @block.tensor
            def _(pe):
                pe.wait_ge(one_set, 2)
                with pe.Fori(0, H // 2) as it:
                    def group(n):
                        b, use = n % 2, n // 2
                        pe.wait_ge(t_free[b], START + it * USES + use)
                        what, *at = groups[n]
                        if what == "qk":
                            hh, which, half = at
                            for i in range(4):
                                last = nc.tensor.transpose(ps[0:HA, 4 + b, i * P:(i + 1) * P],
                                                           (qa, ka)[which][:, 4 * half + i, hh, :], g.ident[:])
                        else:
                            u, kb, n_kb = at
                            for i in range(n_kb):
                                last = nc.tensor.transpose(ps[:, 4 + b, i * P:(i + 1) * P],
                                                           pr[u % NPB][:, (kb + i) * P:(kb + i + 1) * P], g.ident[:])
                        last.then_inc(t_full[b], 1)

                    def scores(u):
                        i, hh = u // 2, u % 2
                        if u >= 2:
                            pe.wait_ge(exped[(u - 2) % NPB], START + it * PER_BUF + (u - 2) // NPB + 1)
                        else:
                            pe.wait_ge(exped[(u - 2) % NPB], START + it * PER_BUF)
                        for at in range(0, (i + 1) * P, 512):
                            n = min(512, (i + 1) * P - at)
                            last = nc.tensor.matmul(ps[:, 2 * (u % 2) + at // 512, 0:n], qkT[:, hh, 0, i * P:(i + 1) * P],
                                                    qkT[:, hh, 1, at:at + n], start=True, stop=True)
                        last.then_inc(s_full[u % 2], 1)

                    def values(qb):
                        for b, count in enumerate(t_count(it, upto[2 * QB * (qb + 1) - 1])):
                            pe.wait_ge(t_free[b], START + count)
                        pe.wait_ge(v_staged, it + 1)
                        pe.wait_ge(pv_free[qb], START + it)
                        for kb in range(QB * (qb + 1)):
                            q0 = max(0, kb - QB * qb) * P
                            for hh in range(2):
                                last = nc.tensor.matmul(ps[hh * HD:(hh + 1) * HD, 6 + qb, q0:QB * P],
                                                        va[:, kb, hh * HD:(hh + 1) * HD], prT[hh][:, kb, q0:QB * P],
                                                        start=(kb == 0), stop=(kb == QB * (qb + 1) - 1))
                        last.then_inc(pv_done[qb], 1)

                    pe.wait_ge(qk_staged, 4 * it + 4)
                    for n in range(8):
                        group(n)
                    for b, count in enumerate(t_count(it, 8)):
                        pe.wait_ge(t_free[b], START + count)
                    for n in range(UNITS + LAG):
                        if n < UNITS:
                            scores(n)
                        u = n - LAG
                        if u >= 0:
                            pe.wait_ge(scaled[u % NPB], it * PER_BUF + u // NPB + 1)
                            for k in range(upto[u - 1] if u else 8, upto[u]):
                                group(k)
                            if u % (2 * QB) == 2 * QB - 1:
                                values(u // (2 * QB))

            def copy_group(eng, copy, it, n):
                b, use = n % 2, n // 2
                eng.wait_ge(t_full[b], START + it * USES + use + 1)
                what, *at = groups[n]
                if what == "qk":
                    hh, which, half = at
                    ins = copy(qkT[:, hh, which, half * 512:(half + 1) * 512], ps[0:HA, 4 + b, :])
                else:
                    u, kb, n_kb = at
                    i, hh = u // 2, u % 2
                    if i < QB:
                        eng.wait_ge(pv_done[1], START + it)
                    else:
                        eng.wait_ge(pv_done[0], START + it + 1)
                    ins = copy(prT[hh][:, kb:kb + n_kb, (i % QB) * P:(i % QB + 1) * P],
                               ps[:, 4 + b, 0:n_kb * P].rearrange("p (k q) -> p k q", q=P))
                ins.then_inc(t_free[b], 1)

            def copy_values(eng, copy, it, qb):
                eng.wait_ge(pv_done[qb], START + it + 1)
                copy(g.aT[:, bass.ds(it, 1), qb * 512:(qb + 1) * 512].rearrange("p a n -> p (a n)"), ps[:, 6 + qb, :])\
                    .then_inc(pv_free[qb], 1)

            @block.vector
            def _(dve):
                with dve.Fori(0, H // 2) as it:
                    def row_max(u):
                        i, sb = u // 2, u % 2
                        keys = (i + 1) * P
                        dve.wait_ge(s_full[sb], it * (UNITS // 2) + u // 2 + 1)
                        diag = ps[:, 2 * sb + i // 4, (i % 4) * P:(i % 4 + 1) * P]
                        nc.vector.tensor_tensor(diag, diag, g.causal[:], ALU.add).then_inc(masked, 1)
                        dve.wait_ge(masked, it * UNITS + u + 1)
                        nc.vector.tensor_reduce(nmax[:, u % NPB:u % NPB + 1],
                                                ps[:, 2 * sb:2 * sb + 2, :].rearrange("p b n -> p (b n)")[:, 0:keys],
                                                AX.X, ALU.max, negate=True).then_inc(have_max, 1)

                    def scale(u):
                        k, keys = u % NPB, (u // 2 + 1) * P
                        dve.wait_ge(exped[k], START + it * PER_BUF + u // NPB + 1)
                        nc.vector.reciprocal(rsum[:, k:k + 1], rsum[:, k:k + 1]).then_inc(have_recip, 1)
                        dve.wait_ge(have_recip, it * UNITS + u + 1)
                        nc.vector.tensor_scalar(pr[k][:, 0:keys], pr[k][:, 0:keys], rsum[:, k:k + 1], None, ALU.mult)\
                            .then_inc(scaled[k], 1)

                    for n in range(0, 8, 2):
                        copy_group(dve, nc.vector.tensor_copy, it, n)
                    for n in range(UNITS + LAG):
                        if n < UNITS:
                            row_max(n)
                        if 1 <= n <= UNITS:
                            scale(n - 1)
                        u = n - LAG
                        if u >= 0:
                            for k in range(upto[u - 1] if u else 8, upto[u]):
                                if k % 2 == 0:
                                    copy_group(dve, nc.vector.tensor_copy, it, k)
                            if u == 2 * QB - 1:
                                copy_values(dve, nc.vector.tensor_copy, it, 0)

            @block.scalar
            def _(act):
                nc.scalar.preload_act_table(ACT.Exp)
                with act.Fori(0, H // 2) as it:
                    def exps(u):
                        k, keys = u % NPB, (u // 2 + 1) * P
                        act.wait_ge(have_max, it * UNITS + u + 1)
                        if u >= NPB:
                            for b, count in enumerate(t_count(it, upto[u - NPB])):
                                act.wait_ge(t_full[b], START + count)
                        else:
                            for b, count in enumerate(t_count(it, 0)):
                                act.wait_ge(t_full[b], START + count)
                        nc.scalar.activation(pr[k][:, 0:keys],
                                             ps[:, 2 * (u % 2):2 * (u % 2) + 2, :].rearrange("p b n -> p (b n)")[:, 0:keys],
                                             ACT.Exp, bias=nmax[:, k:k + 1], accum_out=rsum[:, k:k + 1])\
                            .then_inc(exped[k], 1)

                    for n in range(1, 8, 2):
                        copy_group(act, nc.scalar.copy, it, n)
                    for n in range(UNITS + LAG):
                        if n < UNITS:
                            exps(n)
                        u = n - LAG
                        if u >= 0:
                            for k in range(upto[u - 1] if u else 8, upto[u]):
                                if k % 2:
                                    copy_group(act, nc.scalar.copy, it, k)
                    copy_values(act, nc.scalar.copy, it, 1)


def attend_sample(nc, io, g, ps):
    UP, QUADS = 16, 4
    R = H * DEC_S
    KC = DA // P
    UNITS = 2 * DEC_B
    KS = 8

    with ExitStack() as ctx:
        m = Mem(nc, ctx, "sat")
        table = m.sb("table", [1, DEC_B * PAGES], I32)
        page_rows = m.sb("page_rows", [P, 2], I32)
        lfT = m.sb("lfT", [P, H, DEC_B * PAGES])
        quad_sum, later = m.sb("quad_sum", [P, H, 2 * UNITS * 2]), m.sb("later", [P, H, 2 * UNITS * 2])
        qT, kT_new = m.sb("qT", [P, KC, NS]), m.sb("kT_new", [P, KC, NS])
        q_diag = m.sb("q_diag", [P, KC, DEC_B, R])
        q_now = m.sb("q_now", [P, KC, R])
        lf_now, later_now = m.sb("lf_now", [P, 2, UP, R]), m.sb("later_now", [P, 2, QUADS, R])
        k_pg, v_pg = m.sb("k_pg", [P, KS, DA]), m.sb("v_pg", [P, UP, DA])
        kT = m.sb("kT", [P, KC, UP * P])
        lf_pages = kT[:, 0, :].rearrange("p (a n) -> p a n", a=2)
        pr, prT = m.sb("pr", [P, 2, 512]), m.sb("prT", [P, 512])
        nmax, rsum = m.sb("nmax", [P, 2]), m.sb("rsum", [P, 2])
        nmax_all, rsum_all = m.sb("nmax_all", [P, UNITS]), m.sb("rsum_all", [P, UNITS])
        own_head = m.sb("own_head", [P, H, HD])
        o_all = m.sb("o_all", [P, 512])
        o_head = m.sb("o_head", [P, UNITS, HD])
        row, row_mod = m.sb("row", [P, 1], I32), m.sb("row_mod", [P, 1], I32)
        own_seq = m.sb("own_seq", [R, DEC_B, NS])
        row_h = m.sb("row_h", [P, 1])
        row_q, key_q = m.sb("row_q", [R, 1]), m.sb("key_q", [R, DEC_B, NS])
        head_row = m.sb("head_row", [H, R])
        fold = m.sb("fold", [P, R])
        s_new, rsum_new, nmax_new = m.sb("s_new", [R, DEC_B, NS]), m.sb("rsum_new", [R, DEC_B]), m.sb("nmax_new", [R, DEC_B])
        p_newT = m.sb("p_newT", [NS, DEC_B * R])
        q_new, k_new, v_new = (m.sb(n, [NS, DA]) for n in ("q_new", "k_new", "v_new"))
        new_in = m.sem("new_in")
        parts_m, parts_l = m.sb("parts_m", [DEC_B, 9, R]), m.sb("parts_l", [DEC_B, 9, R])
        parts_w = m.sb("parts_w", [DEC_B, 9, R])
        top, total = m.sb("top", [DEC_B, R]), m.sb("total", [DEC_B, R])
        share, share_new = m.sb("share", [P, DEC_B, 2]), m.sb("share_new", [R, DEC_B])
        o_new = m.sb("o_new", [P, 2, HD])

        table_in, rows_in, lf_in = m.sem("table_in"), m.sem("rows_in"), m.sems("lf_in", 2)
        pool_own, own = m.sem("pool_own"), m.sem("own")
        lfT_done, lfT_copied = m.sems("lfT_done", 4), m.sem("lfT_copied")
        qk_done, qk_copied, diag_ready = m.sem("qk_done"), m.sem("qk_copied"), m.sem("diag_ready")
        later_ready, consts = m.sem("later_ready"), m.sem("consts")
        staged = m.sem("staged")
        k_in, v_in = m.sems("k_in", 2), m.sems("v_in", 4)
        t_done = [m.sems(f"t_done{e}", 2) for e in range(2)]
        t_copied = [m.sems(f"t_copied{e}", 2) for e in range(2)]
        s_done, have_max, exped = m.sems("s_done", 2), m.sems("have_max", 2), m.sems("exped", 2)
        prT_done, prT_copied = m.sem("prT_done"), m.sem("prT_copied")
        pv_done, o_read, o_masked = m.sems("pv_done", 4), m.sem("o_read"), m.sem("o_masked")
        kept = m.sem("kept")
        c_pe, c_dve, c_act, shifted = m.sem("c_pe"), m.sem("c_dve"), m.sem("c_act"), m.sem("shifted")

        k_pool = io["cache_k"][0].rearrange("n p h d -> n p (h d)")
        v_pool = io["cache_v"][0].rearrange("n p h d -> n p (h d)")
        n_pool = io["cache_k"].shape[1]

        m.start(t_copied[0] + t_copied[1] + pv_done + exped + s_done + [kept, prT_copied, o_read, prT_done])

        with nc.Block() as block:
            @block.sync
            def _(sp):
                sp.dma_start(table[:], io["page_table"].rearrange("b n -> (b n)").rearrange("(a n) -> a n", a=1))\
                    .then_inc(table_in, 16)
                sp.dma_start(q_new[:], g.q_rows).then_inc(new_in, 16)
                for dst, src in ((k_new, io["new_k_sample"]), (v_new, io["new_v_sample"])):
                    sp.dma_start(dst[:], src[0].rearrange("b s h d -> (b s) (h d)")).then_inc(new_in, 16)
                sp.wait_ge(table_in, 16)
                with sp.Fori(0, DEC_B) as b:
                    for half in range(2):
                        def page(n):
                            return sp.value_load(table[0:1, bass.ds(b * PAGES + half * UP + n, 1)],
                                                 min_val=0, max_val=n_pool - 1)

                        for j in range(QUADS):
                            use = 2 * half + j // 2
                            pages = [page(4 * j + pp) for pp in range(4)]
                            for e in range(2):
                                sp.wait_ge(t_copied[e][j % 2], START + 2 * (4 * b + use))
                            for pp in range(4):
                                sp.dma_start(k_pg[:, 4 * (j % 2) + pp, :],
                                             k_pool[bass.ds(pages[pp], 1)].rearrange("a p n -> (a p) n"))\
                                    .then_inc(k_in[j % 2], 16)
                        for pp in range(4):
                            pages = [page(4 * j + pp) for j in range(QUADS)]
                            sp.wait_ge(pv_done[pp], START + 2 * b + half)
                            for j in range(QUADS):
                                sp.dma_start(v_pg[:, 4 * pp + j, :],
                                             v_pool[bass.ds(pages[j], 1)].rearrange("a p n -> (a p) n"))\
                                    .then_inc(v_in[pp], 16)

            @block.gpsimd
            def _(pool):
                link = Chain(pool, pool_own)
                with nc.allow_non_contiguous_dma(reason="a page's number a partition"):
                    pool.dma_start(page_rows[:], io["page_table"].rearrange("b n -> (b n)").rearrange("(a p) -> p a", p=P))\
                        .then_inc(rows_in, 16)
                pool.wait_ge(rows_in, 16)
                for a in range(2):
                    pool.indirect_dma_start(lf_pages[:, a, :], None, io["cache_logf"][0].rearrange("n p h -> n (p h)"),
                                            bass.IndirectOffsetOnAxis(page_rows[:, a:a + 1], 0)).then_inc(lf_in[a], 16)
                nc.gpsimd.iota(row[:], pattern=[[0, 1]], base=0, channel_multiplier=1).then_inc(consts, 1)
                nc.gpsimd.iota(own_head[:], pattern=[[1, H], [0, HD]], base=0, channel_multiplier=0,
                               allow_small_or_imprecise_dtypes=True).then_inc(consts, 1)
                nc.gpsimd.iota(key_q[:], pattern=[[0, DEC_B * DEC_B], [1, DEC_S]], base=0, channel_multiplier=0,
                               allow_small_or_imprecise_dtypes=True).then_inc(consts, 1)
                link(nc.gpsimd.affine_select(out=head_row[:], in_=g.ones[0:H, 0:R], compare_op=ALU.is_ge, fill=0.0,
                                             base=0, pattern=[[1, R]], channel_multiplier=-DEC_S))
                nc.gpsimd.affine_select(out=head_row[:], in_=head_row[:], compare_op=ALU.is_ge, fill=0.0,
                                        base=DEC_S - 1, pattern=[[-1, R]], channel_multiplier=DEC_S).then_inc(consts, 1)
                link(nc.gpsimd.memset(own_seq[:], 0.0))
                link(nc.gpsimd.affine_select(out=own_seq[:], in_=own_seq[:], compare_op=ALU.is_ge, fill=NEG, base=0,
                                             pattern=[[-DEC_S, DEC_B], [1, NS]], channel_multiplier=0))
                nc.gpsimd.affine_select(out=own_seq[:], in_=own_seq[:], compare_op=ALU.is_ge, fill=NEG, base=DEC_S - 1,
                                        pattern=[[DEC_S, DEC_B], [-1, NS]], channel_multiplier=0).then_inc(consts, 1)
                nc.gpsimd.memset(q_diag[:], 0.0).then_inc(consts, 1)
                nc.gpsimd.memset(later[:], 0.0).then_inc(consts, 1)
                pool.wait_ge(diag_ready, 2 * KC)
                pool.wait_ge(later_ready, 1)
                pool.wait_ge(lfT_copied, 4)
                rep = [P, UP, H, DEC_S]
                with pool.Fori(0, DEC_B) as b:
                    for half in range(2):
                        pool.wait_ge(s_done[half], START + b)
                    nc.gpsimd.tensor_copy(q_now[:], q_diag[:, :, bass.ds(b, 1), :].rearrange("p c a r -> p c (a r)"))\
                        .then_inc(staged, 1)
                    for half in range(2):
                        for q in range(DEC_S):
                            nc.gpsimd.tensor_copy(
                                lf_now[:, half].rearrange("p n (h q) -> p n h q", q=DEC_S)[:, :, :, q],
                                lfT[:, :, bass.ds(b * PAGES + half * UP, UP)].rearrange("p h n -> p n h"))\
                                .then_inc(staged, 1)
                            nc.gpsimd.tensor_copy(
                                later_now[:, half].rearrange("p n (h q) -> p n h q", q=DEC_S)[:, :, :, q],
                                later[:, :, bass.ds(8 * b + 4 * half, 4)].rearrange("p h n -> p n h"))\
                                .then_inc(staged, 1)
                    pool.wait_ge(exped[0], START + b + 1)
                    pool.wait_ge(exped[1], START + b + 1)
                    nc.gpsimd.tensor_copy(nmax_all[:, bass.ds(2 * b, 2)], nmax[:]).then_inc(kept, 1)
                    nc.gpsimd.tensor_copy(rsum_all[:, bass.ds(2 * b, 2)], rsum[:]).then_inc(kept, 1)

            def copy_keys(eng, copy, e, b, half):
                for j in range(QUADS):
                    use = 2 * half + j // 2
                    for pp in range(e, 4, 2):
                        eng.wait_ge(t_done[e][j % 2], 2 * (4 * b + use) + pp // 2 + 1)
                        if j == 0 and pp == e:
                            eng.wait_ge(s_done[1 - half], START + b + half)
                        n = 4 * j + pp
                        copy(kT[:, :, n * P:(n + 1) * P], ps[:, 2 * (j % 2) + e, :].rearrange("p (c k) -> p c k", c=KC))\
                            .then_inc(t_copied[e][j % 2], 1)

            @block.tensor
            def _(pe):
                pe.wait_ge(new_in, 48)
                for which, src in enumerate((q_new, k_new)):
                    for c in range(KC):
                        last = nc.tensor.transpose(ps[:, 7, (which * KC + c) * NS:(which * KC + c + 1) * NS],
                                                   src[:, c * P:(c + 1) * P], g.ident[0:NS, 0:NS])
                last.then_inc(qk_done, 1)
                for a in range(2):
                    pe.wait_ge(lf_in[a], 16)
                    for h0 in range(0, H, 4):
                        b = 2 * a + h0 // 4
                        for h in range(h0, h0 + 4):
                            last = nc.tensor.transpose(ps[:, b, (h - h0) * P:(h - h0 + 1) * P],
                                                       lf_pages[:, a, :].rearrange("n (k h) -> n k h", h=H)[:, :, h],
                                                       g.ident[:])
                        last.then_inc(lfT_done[b], 1)
                pe.wait_ge(lfT_copied, 4)
                with pe.Fori(0, DEC_B) as b:
                    def transposes(half):
                        for j in range(QUADS):
                            use = 2 * half + j // 2
                            pe.wait_ge(k_in[j % 2], 64 * (4 * b + use) + 64)
                            for pp in range(4):
                                e = pp % 2
                                pe.wait_ge(t_copied[e][j % 2], START + 2 * (4 * b + use) + pp // 2)
                                for c in range(KC):
                                    last = nc.tensor.transpose(ps[:, 2 * (j % 2) + e, c * P:(c + 1) * P],
                                                               k_pg[:, 4 * (j % 2) + pp, c * P:(c + 1) * P], g.ident[:])
                                last.then_inc(t_done[e][j % 2], 1)

                    def scores(half):
                        for e in range(2):
                            for par in range(2):
                                pe.wait_ge(t_copied[e][par], START + 2 * (4 * b + 2 * half + 2))
                        pe.wait_ge(staged, 17 * b + 17)
                        pe.wait_ge(exped[half], START + b)
                        quads = [(j, slice(R * j, R * j + R)) for j in range(QUADS)]
                        for c in range(KC):
                            for j, at in quads:
                                nc.tensor.matmul(ps[at, 4 + half, :], q_now[:, c, :], kT[:, c, j * 512:(j + 1) * 512],
                                                 start=(c == 0), stop=False, skip_group_check=True)
                        for j, at in quads:
                            nc.tensor.matmul(ps[at, 4 + half, :], later_now[:, half, j, :], g.ones[:],
                                             start=False, stop=False, skip_group_check=True)
                        for pp in range(4):
                            for j, at in quads:
                                last = nc.tensor.matmul(ps[at, 4 + half, 0:(pp + 1) * P], lf_now[:, half, 4 * j + pp, :],
                                                        g.after[:, (3 - pp) * P:4 * P], start=False, stop=(pp == 3),
                                                        skip_group_check=True)
                        last.then_inc(s_done[half], 1)

                    def values(half):
                        u = 2 * b + half
                        pe.wait_ge(exped[half], START + b + 1)
                        pe.wait_ge(prT_copied, START + u)
                        for pp in range(4):
                            last = nc.tensor.transpose(ps[:, 7, pp * P:(pp + 1) * P], pr[:, half, pp * P:(pp + 1) * P],
                                                       g.ident[:])
                        last.then_inc(prT_done, 1)
                        pe.wait_ge(prT_copied, START + u + 1)
                        pe.wait_ge(o_read, START + u)
                        for pp in range(4):
                            pe.wait_ge(v_in[pp], 64 * u + 64)
                            for j in range(QUADS):
                                at = slice(R * j, R * j + R)
                                last = nc.tensor.matmul(ps[at, 6, :], prT[:, pp * P + R * j:pp * P + R * j + R],
                                                        v_pg[:, 4 * pp + j, :], start=(pp == 0), stop=(pp == 3))
                            last.then_inc(pv_done[pp], 1)

                    transposes(0)
                    scores(0)
                    transposes(1)
                    values(0)
                    scores(1)
                    values(1)

                pe.wait_ge(o_read, START + UNITS)
                pe.wait_ge(consts, 7)
                for b in range(DEC_B):
                    at = slice(b * NS, (b + 1) * NS)
                    for c in range(KC):
                        nc.tensor.matmul(ps[0:R, 0, at], q_diag[:, c, b, :], kT_new[:, c, :], start=(c == 0), stop=False,
                                         skip_group_check=True)
                    last = nc.tensor.matmul(ps[0:R, 0, at], head_row[:], g.ncum_new[:], start=False, stop=True,
                                            skip_group_check=True)
                last.then_inc(c_pe, 1)
                pe.wait_ge(kept, START + 2 * DEC_B)
                pe.wait_ge(c_dve, 1)
                for half in range(2):
                    for bank, src in ((1, nmax_all), (2, rsum_all)):
                        nc.tensor.transpose(ps[0:DEC_B, bank, half * P:(half + 1) * P],
                                            src[:].rearrange("p (b a) -> p b a", a=2)[:, :, half], g.ident[:])
                for bank, src in ((1, nmax_new), (2, rsum_new)):
                    last = nc.tensor.transpose(ps[0:DEC_B, bank, 2 * P:2 * P + R], src[:], g.ident[0:R, 0:R])
                last.then_inc(c_pe, 1)
                pe.wait_ge(c_dve, 2)
                flat = parts_w[:].rearrange("b n r -> b (n r)")
                for half in range(2):
                    nc.tensor.transpose(ps[:, 3, half * DEC_B:(half + 1) * DEC_B], flat[:, half * P:(half + 1) * P],
                                        g.ident[0:DEC_B, 0:DEC_B])
                nc.tensor.transpose(ps[0:R, 3, 2 * DEC_B:3 * DEC_B], flat[:, 2 * P:2 * P + R],
                                    g.ident[0:DEC_B, 0:DEC_B]).then_inc(c_pe, 1)
                pe.wait_ge(c_dve, 3)
                for b in range(DEC_B):
                    last = nc.tensor.transpose(ps[0:NS, 0, b * R:(b + 1) * R], s_new[:, b, :], g.ident[0:R, 0:R])
                last.then_inc(c_pe, 1)
                pe.wait_ge(c_dve, 4)
                for bh in range(2):
                    for j in range(4):
                        b = 4 * bh + j
                        last = nc.tensor.matmul(ps[R * j:R * j + R, 4 + bh, :], p_newT[:, b * R:(b + 1) * R], v_new[:],
                                                start=True, stop=True)
                last.then_inc(c_pe, 1)
                pe.wait_ge(c_dve, 5)
                for b in range(DEC_B):
                    at = slice(b * R, (b + 1) * R)
                    for half in range(2):
                        nc.tensor.matmul(ps[0:HD, 7, at], o_head[:, 2 * b + half, :], fold[:], start=(half == 0), stop=False,
                                         skip_group_check=True)
                    last = nc.tensor.matmul(ps[0:HD, 7, at], o_new[:, b // 4, :], g.ident[:, R * (b % 4):R * (b % 4) + R],
                                            start=False, stop=True, skip_group_check=True)
                last.then_inc(c_pe, 1)

            @block.vector
            def _(dve):
                link = Chain(dve, own)
                dve.wait_ge(qk_done, 1)
                qkv = ps[:, 7, 0:2 * KC * NS].rearrange("p (a c n) -> p a c n", a=2, c=KC)
                nc.vector.tensor_copy(qT[:], qkv[:, 0]).then_inc(qk_copied, 1)
                nc.vector.tensor_copy(kT_new[:], qkv[:, 1]).then_inc(qk_copied, 1)
                dve.wait_ge(qk_copied, 2)
                dve.wait_ge(consts, 7)
                for c in range(KC):
                    for hh in range(2):
                        at = slice(hh * HD, (hh + 1) * HD)
                        nc.vector.tensor_copy(
                            q_diag[at, c].rearrange("p b (h q) -> p b h q", q=DEC_S)[:, :, 2 * c + hh, :],
                            qT[at, c, :].rearrange("p (b q) -> p b q", q=DEC_S)).then_inc(diag_ready, 1)
                for b in range(4):
                    dve.wait_ge(lfT_done[b], 1)
                    nc.vector.tensor_copy(lfT[:, 4 * (b % 2):4 * (b % 2) + 4, (b // 2) * P:(b // 2 + 1) * P],
                                          ps[:, b, :].rearrange("p (h n) -> p h n", h=4)).then_inc(lfT_copied, 1)
                dve.wait_ge(lfT_copied, 4)
                link(nc.vector.tensor_reduce(quad_sum[:], lfT[:].rearrange("p h (c n) -> p h c n", n=4), AX.X, ALU.add))
                seqs = "p h (b c) -> p h b c"
                la, qs = later[:].rearrange(seqs, c=8), quad_sum[:].rearrange(seqs, c=8)
                for c in range(6, -1, -1):
                    last = nc.vector.tensor_tensor(la[:, :, :, c], la[:, :, :, c + 1], qs[:, :, :, c + 1], ALU.add)
                    if c:
                        link(last)
                last.then_inc(later_ready, 1)
                link(nc.vector.tensor_scalar(row_mod[:], row[:], DEC_S - 1, None, ALU.bitwise_and))
                link(nc.vector.tensor_scalar(row[:], row[:], R - 1, 2, ALU.bitwise_and, ALU.logical_shift_right))
                link(nc.vector.tensor_copy(row_h[:], row[:]))
                link(nc.vector.tensor_scalar(own_head[:], own_head[:], row_h[:, 0:1], None, ALU.is_equal))
                link(nc.vector.tensor_reduce(fold[:], g.ident[:].rearrange("p (j r) -> p r j", j=4), AX.X, ALU.add))
                with dve.Fori(0, DEC_B) as b:
                    def row_max(half):
                        dve.wait_ge(s_done[half], START + b + 1)
                        dve.wait_ge(kept, START + 2 * b)
                        nc.vector.tensor_reduce(nmax[:, half:half + 1], ps[:, 4 + half, :], AX.X, ALU.max,
                                                negate=True).then_inc(have_max[half], 1)

                    def values(half):
                        u = 2 * b + half
                        dve.wait_ge(prT_done, START + u + 1)
                        nc.vector.tensor_copy(prT[:], ps[:, 7, :]).then_inc(prT_copied, 1)
                        dve.wait_ge(pv_done[3], START + u + 1)
                        nc.vector.tensor_tensor(o_all[:], ps[:, 6, :], own_head[:].rearrange("p h d -> p (h d)"),
                                                ALU.mult).then_inc(o_read, 1)
                        dve.wait_ge(o_read, START + u + 1)
                        nc.vector.tensor_reduce(o_head[:, bass.ds(u, 1), :].rearrange("p a d -> p (a d)"),
                                                o_all[:].rearrange("p (h d) -> p d h", h=H), AX.X, ALU.add)\
                            .then_inc(o_masked, 1)
                        dve.wait_ge(o_masked, u + 1)

                    copy_keys(dve, nc.vector.tensor_copy, 0, b, 0)
                    row_max(0)
                    copy_keys(dve, nc.vector.tensor_copy, 0, b, 1)
                    values(0)
                    row_max(1)
                    values(1)

                link(nc.vector.tensor_copy(row_q[:], row_mod[0:R, :]))
                link(nc.vector.tensor_scalar(key_q[:], key_q[:], row_q[:, 0:1], NEG, ALU.is_gt, ALU.mult))
                dve.wait_ge(c_pe, 1)
                link(nc.vector.tensor_tensor(s_new[:], ps[0:R, 0, 0:DEC_B * NS].rearrange("r (b k) -> r b k", k=NS),
                                             key_q[:], ALU.add))
                link(nc.vector.tensor_tensor(s_new[:], s_new[:], own_seq[:], ALU.add))
                link(nc.vector.tensor_reduce(nmax_new[:], s_new[:], AX.X, ALU.max, negate=True))
                nc.vector.tensor_tensor(s_new[:], s_new[:], nmax_new[:].unsqueeze(2).to_broadcast([R, DEC_B, NS]),
                                        ALU.add).then_inc(shifted, 1)
                dve.wait_ge(c_act, 1)
                nc.vector.tensor_reduce(rsum_new[:], s_new[:], AX.X, ALU.add).then_inc(c_dve, 1)
                dve.wait_ge(c_pe, 2)
                parts = "b (n r) -> b n r"
                link(nc.vector.tensor_copy(parts_m[:], ps[0:DEC_B, 1, 0:9 * R].rearrange(parts, r=R)))
                link(nc.vector.tensor_copy(parts_l[:], ps[0:DEC_B, 2, 0:9 * R].rearrange(parts, r=R)))
                link(nc.vector.tensor_reduce(top[:], parts_m[:].rearrange("b n r -> b r n"), AX.X, ALU.min))
                nc.vector.tensor_tensor(parts_m[:], top[:].unsqueeze(1).to_broadcast([DEC_B, 9, R]), parts_m[:],
                                        ALU.subtract).then_inc(shifted, 1)
                dve.wait_ge(c_act, 2)
                link(nc.vector.tensor_tensor(parts_l[:], parts_l[:], parts_w[:], ALU.mult))
                link(nc.vector.tensor_reduce(total[:], parts_l[:].rearrange("b n r -> b r n"), AX.X, ALU.add))
                link(nc.vector.reciprocal(total[:], total[:]))
                nc.vector.tensor_tensor(parts_w[:], parts_w[:], total[:].unsqueeze(1).to_broadcast([DEC_B, 9, R]),
                                        ALU.mult).then_inc(c_dve, 1)
                dve.wait_ge(c_pe, 3)
                link(nc.vector.tensor_copy(share[:], ps[:, 3, 0:2 * DEC_B].rearrange("p (a b) -> p b a", a=2)))
                link(nc.vector.tensor_copy(share_new[:], ps[0:R, 3, 2 * DEC_B:3 * DEC_B]))
                nc.vector.tensor_tensor(s_new[:], s_new[:], share_new[:].unsqueeze(2).to_broadcast([R, DEC_B, NS]),
                                        ALU.mult).then_inc(c_dve, 1)
                o_parts = o_head[:].rearrange("p (b a) d -> p b a d", a=2)
                link(nc.vector.tensor_tensor(o_parts, o_parts, share[:].unsqueeze(3).to_broadcast([P, DEC_B, 2, HD]), ALU.mult))
                dve.wait_ge(c_pe, 4)
                nc.vector.tensor_copy(p_newT[:], ps[0:NS, 0, 0:DEC_B * R]).then_inc(c_dve, 1)
                dve.wait_ge(c_pe, 5)
                for bh in range(2):
                    link(nc.vector.tensor_tensor(o_all[:], ps[:, 4 + bh, :], own_head[:].rearrange("p h d -> p (h d)"),
                                                 ALU.mult))
                    last = nc.vector.tensor_reduce(o_new[:, bh, :], o_all[:].rearrange("p (h d) -> p d h", h=H), AX.X,
                                                   ALU.add)
                    if bh == 0:
                        link(last)
                last.then_inc(c_dve, 1)
                dve.wait_ge(c_pe, 6)
                res = ps[0:HD, 7, 0:DEC_B * R].rearrange("d (b c hh q) -> d hh c b q", b=DEC_B, c=KC, hh=2)
                for hh in range(2):
                    nc.vector.tensor_copy(g.aT[hh * HD:(hh + 1) * HD, :, SEQ:T].rearrange("d c (b q) -> d c b q", q=DEC_S),
                                          res[:, hh])

            @block.scalar
            def _(act):
                nc.scalar.preload_act_table(ACT.Exp)
                with act.Fori(0, DEC_B) as b:
                    def exps(half):
                        act.wait_ge(have_max[half], b + 1)
                        act.wait_ge(prT_done, START + 2 * b)
                        act.wait_ge(kept, START + 2 * b)
                        nc.scalar.activation(pr[:, half, :], ps[:, 4 + half, :], ACT.Exp, bias=nmax[:, half:half + 1],
                                             accum_out=rsum[:, half:half + 1]).then_inc(exped[half], 1)

                    copy_keys(act, nc.scalar.copy, 1, b, 0)
                    exps(0)
                    copy_keys(act, nc.scalar.copy, 1, b, 1)
                    exps(1)
                act.wait_ge(shifted, 1)
                nc.scalar.activation(s_new[:], s_new[:], ACT.Exp).then_inc(c_act, 1)
                act.wait_ge(shifted, 2)
                nc.scalar.activation(parts_w[:], parts_m[:], ACT.Exp).then_inc(c_act, 1)


def mix(nc, io, g, ps, mT):
    KA = DA // P
    with ExitStack() as ctx:
        m = Mem(nc, ctx, "mix")
        w_gate = [m.sb(f"w_gate{s}", [P, 2, KD, P]) for s in range(2)]
        w_out = [m.sb(f"w_out{s}", [P, 2, KA, P]) for s in range(2)]
        sg = [m.sb(f"sg{i}", [P, 2, BLK]) for i in range(2)]
        w_loaded, full, gated, used, added = (m.sems(n, 2) for n in ("w_loaded", "full", "gated", "used", "added"))
        w_used = m.sems("w_used", 2)
        gate_v = io["w_in"][0].rearrange("(k p) n -> p k n", p=P)
        out_v = [w[0].rearrange("(k p) n -> p k n", p=P) for w in (io["w_attn_out"], io["w_gmlp_out"])]
        GROUPS = 6
        USES = GROUPS // 2

        m.start(w_used + used + added)

        with nc.Block() as block:
            @block.sync
            def _(sp):
                with sp.Fori(0, KD // 2) as it:
                    for s in range(2):
                        sp.wait_ge(w_used[s], START + it)
                        for a, at in enumerate((COL_GA, COL_GG)):
                            sp.dma_start(w_gate[s][:, a], gate_v[:, :, bass.ds((2 * it + s) * P + at, P)])\
                                .then_inc(w_loaded[s], 16)
                        for a in range(2):
                            sp.dma_start(w_out[s][:, a], out_v[a][:, :, bass.ds((2 * it + s) * P, P)])\
                                .then_inc(w_loaded[s], 16)

            @block.tensor
            def _(pe):
                with pe.Fori(0, KD // 2) as it:
                    for n in range(GROUPS):
                        s, j, b = n // 3, n % 3, n % 2
                        if j == 0:
                            pe.wait_ge(w_loaded[s], 64 * it + 64)
                        pe.wait_ge(used[b], START + it * USES + n // 2)
                        at = slice(j * BLK, (j + 1) * BLK)
                        for a in range(2):
                            for k in range(KD):
                                last = nc.tensor.matmul(ps[:, 4 * b + a, 0:BLK], w_gate[s][:, a, k, :], g.hT[:, k, at],
                                                        start=(k == 0), stop=(k == KD - 1))
                        for a, src in enumerate((g.aT, g.uT)):
                            for k in range(KA):
                                last = nc.tensor.matmul(ps[:, 4 * b + 2 + a, 0:BLK], w_out[s][:, a, k, :], src[:, k, at],
                                                        start=(k == 0), stop=(k == KA - 1))
                        last.then_inc(full[b], 1)

            @block.scalar
            def _(act):
                nc.scalar.preload_act_table(ACT.Sigmoid)
                with act.Fori(0, KD // 2) as it:
                    for n in range(GROUPS):
                        b = n % 2
                        act.wait_ge(full[b], it * USES + n // 2 + 1)
                        if n % 3 == 2:
                            act.sem_inc(w_used[n // 3], 1)
                        act.wait_ge(added[b], START + it * USES + n // 2)
                        nc.scalar.activation(sg[b][:], ps[:, 4 * b:4 * b + 2, 0:BLK], ACT.Sigmoid).then_inc(gated[b], 1)

            @block.vector
            def _(dve):
                with dve.Fori(0, KD // 2) as it:
                    for n in range(GROUPS):
                        b = n % 2
                        dve.wait_ge(gated[b], it * USES + n // 2 + 1)
                        nc.vector.tensor_tensor(sg[b][:], ps[:, 4 * b + 2:4 * b + 4, 0:BLK], sg[b][:], ALU.mult)\
                            .then_inc(used[b], 1)

            @block.gpsimd
            def _(pool):
                with pool.Fori(0, KD // 2) as it:
                    for n in range(GROUPS):
                        s, j, b = n // 3, n % 3, n % 2
                        pool.wait_ge(used[b], START + it * USES + n // 2 + 1)
                        nc.gpsimd.tensor_tensor(
                            mT[:, bass.ds(2 * it + s, 1), j * BLK:(j + 1) * BLK].rearrange("p a n -> p (a n)"),
                            sg[b][:, 0, :], sg[b][:, 1, :], ALU.add).then_inc(added[b], 1)


class Norm:

    def __init__(self, m, eps, gain, bias):
        self.stats, self.mv, self.std = m.sb("ln_stats", [P, 2, 6]), m.sb("ln_mv", [P, 2]), m.sb("ln_std", [P, 1])
        self.eps, self.gain, self.bias = eps, gain, bias
        self.have_var, self.have_std = m.sem("have_var"), m.sem("have_std")

    def variance(self, nc, link, r, rows):
        for half in range(2):
            link(nc.vector.bn_stats(self.stats[0:rows, half, :], r[0:rows, half * 512:(half + 1) * 512]))
        nc.vector.bn_aggr(self.mv[0:rows, :], self.stats[0:rows].rearrange("p a n -> p (a n)")).then_inc(self.have_var, 1)

    def deviation(self, nc, act, t, rows):
        act.wait_ge(self.have_var, t + 1)
        nc.scalar.activation(self.std[0:rows, :], self.mv[0:rows, 1:2], ACT.Sqrt, bias=self.eps[0:rows, 0:1])\
            .then_inc(self.have_std, 1)

    def apply(self, nc, dve, link, t, out, r, rows):
        dve.wait_ge(self.have_std, t + 1)
        link(nc.vector.reciprocal(self.std[0:rows, :], self.std[0:rows, :]))
        link(nc.vector.scalar_tensor_tensor(out=r[0:rows, :], in0=r[0:rows, :], scalar=self.mv[0:rows, 0:1],
                                            in1=self.gain[0:rows, :], op0=ALU.subtract, op1=ALU.mult))
        return nc.vector.scalar_tensor_tensor(out=out, in0=r[0:rows, :], scalar=self.std[0:rows, 0:1],
                                              in1=self.bias[0:rows, :], op0=ALU.mult, op1=ALU.add)


def mixer_out(nc, io, g, ps, mT):
    RW = 32
    with ExitStack() as ctx:
        m = Mem(nc, ctx, "mo")
        w_o = m.sb("w_o", [P, KD, D])
        w_r = m.sb("w_r", [P, KD, RW])
        b_r = m.sb("b_r", [P, NG + NEXP])
        ln_b = m.sb("ln_b", [P, D])
        x_t, r_t, h_t = ([m.sb(f"{n}{i}", [P, D]) for i in range(2)] for n in ("x", "r", "h"))
        hT_t = m.sb("hT", [P, KD, P])
        eps, fold = m.sb("eps", [P, 1]), m.sb("fold", [P, RW])
        part = m.sb("part", [P, P])
        norm = Norm(m, eps, g.ln_g, ln_b)
        w_in, wr_in, wr_zero, rows_in, par_in = (m.sem(n) for n in ("w_in", "wr_in", "wr_zero", "rows_in", "par_in"))
        plus_one, consts = m.sem("plus_one"), m.sem("consts")
        x_in, m_full, m_read, x1_done, h2_done = (m.sems(n, 2) for n in ("x_in", "m_full", "m_read", "x1_done", "h2_done"))
        h2_out = m.sems("h2_out", 2)
        h2T_full, h2T_copied = m.sems("h2T_full", 2), m.sems("h2T_copied", 2)
        part_full, part_copied, logits_full, logits_read = (m.sem(n) for n in ("pf", "pc", "lf", "lr"))
        own, pool_own = m.sem("own"), m.sem("pool_own")
        x_rows = [io["x_prompt"][0, t * P:(t + 1) * P, :] for t in range(PT)] + [io["x_sample"].rearrange("b s d -> (b s) d")]

        def mod(which, t):
            return g.rows[which][0 if t < PT else 1]

        with nc.Block() as block:
            def store_h2(sp, t):
                rows, b = TILE_ROWS[t], t % 2
                sp.wait_ge(h2_done[b], t // 2 + 1)
                sp.dma_start(g.h2_rows[t * P:t * P + rows, :], h_t[b][0:rows, :]).then_inc(h2_out[b], 16)

            @block.sync
            def _(sp):
                sp.dma_start(w_o[:], io["w_o"][0].rearrange("(k p) n -> p k n", p=P)).then_inc(w_in, 16)
                for which, at in (("g1", 2), ("sc2", 4), ("sh2", 3), ("g2", 5)):
                    sp.dma_start(g.rows[which][0], g.ada_rows[0:1, at, :].partition_broadcast(P)
                                 .rearrange("p a n -> p (a n)")).then_inc(rows_in, 16)
                    for b in range(DEC_B):
                        sp.dma_start(g.rows[which][1][b * DEC_S:(b + 1) * DEC_S, :],
                                     g.ada_rows[1 + b:2 + b, at, :].partition_broadcast(DEC_S)
                                     .rearrange("p a n -> p (a n)")).then_inc(rows_in, 16)
                for dst, src in ((g.ln_g, io["ln1_g"]), (ln_b[:], io["ln1_b"])):
                    sp.dma_start(dst, src.partition_broadcast(P).rearrange("p a n -> p (a n)")).then_inc(par_in, 16)
                for dst, src in ((b_r[:, 0:NG], io["b_group_router"]), (b_r[:, NG:], io["b_expert_router"])):
                    sp.dma_start(dst, src.partition_broadcast(P).rearrange("p a n -> p (a n)")).then_inc(par_in, 16)
                sp.wait_ge(wr_zero, 1)
                with nc.allow_non_contiguous_dma(reason="narrow router weights"):
                    for dst, src in ((w_r[:, :, 0:NG], io["w_group_router"]), (w_r[:, :, NG:NG + NEXP], io["w_expert_router"])):
                        sp.dma_start(dst, src[0].rearrange("(k p) n -> p k n", p=P)).then_inc(wr_in, 16)
                for t in range(NT):
                    rows, b = TILE_ROWS[t], t % 2
                    if t >= 2:
                        sp.wait_ge(x1_done[b], t // 2)
                    sp.dma_start(x_t[b][0:rows, :], x_rows[t]).then_inc(x_in[b], 16)
                    if t >= 1:
                        store_h2(sp, t - 1)
                store_h2(sp, NT - 1)
                for b in range(2):
                    sp.wait_ge(h2_out[b], 16 * ((NT + 1 - b) // 2))

            @block.tensor
            def _(pe):
                pe.wait_ge(w_in, 16)

                def product(t):
                    rows, b = TILE_ROWS[t], t % 2
                    if t >= 2:
                        pe.wait_ge(m_read[b], t // 2)
                    for half in range(2):
                        for k in range(KD):
                            last = nc.tensor.matmul(ps[0:rows, 2 * b + half, :], mT[:, k, t * P:t * P + rows],
                                                    w_o[:, k, half * 512:(half + 1) * 512], start=(k == 0),
                                                    stop=(k == KD - 1))
                    last.then_inc(m_full[b], 1)

                def route(t):
                    rows, b = TILE_ROWS[t], t % 2
                    pe.wait_ge(h2_done[b], t // 2 + 1)
                    for half in range(2):
                        pe.wait_ge(h2T_copied[half], t)
                        for i in range(4):
                            k = 4 * half + i
                            last = nc.tensor.transpose(ps[:, 4 + half, i * P:i * P + rows],
                                                       h_t[b][0:rows, k * P:(k + 1) * P], g.ident[0:rows, 0:rows])
                        last.then_inc(h2T_full[half], 1)
                    for half in range(2):
                        pe.wait_ge(h2T_copied[half], t + 1)
                    pe.wait_ge(wr_in, 32)
                    pe.wait_ge(part_copied, t)
                    for k in range(KD):
                        j = k % 4
                        last = nc.tensor.matmul(ps[RW * j:RW * j + RW, 6, 0:rows], w_r[:, k, :], hT_t[:, k, 0:rows],
                                                start=(k < 4), stop=(k >= 4))
                    last.then_inc(part_full, 1)
                    pe.wait_ge(part_copied, t + 1)
                    pe.wait_ge(logits_read, t)
                    nc.tensor.matmul(ps[0:rows, 7, 0:RW], part[:, 0:rows], fold[:], start=True, stop=True)\
                        .then_inc(logits_full, 1)

                for t in range(NT + 1):
                    if t < NT:
                        product(t)
                    if t:
                        route(t - 1)

            @block.scalar
            def _(act):
                for t in range(NT + 1):
                    if t < NT:
                        norm.deviation(nc, act, t, TILE_ROWS[t])
                    if t:
                        rows = TILE_ROWS[t - 1]
                        for half in range(2):
                            act.wait_ge(h2T_full[half], t)
                            act.wait_ge(part_full, t - 1)
                            nc.scalar.copy(hT_t[:, 4 * half:4 * half + 4, 0:rows],
                                           ps[:, 4 + half, :].rearrange("p (k n) -> p k n", k=4)[:, :, 0:rows])\
                                .then_inc(h2T_copied[half], 1)
                        act.wait_ge(part_full, t)
                        act.wait_ge(logits_full, t - 1)
                        nc.scalar.copy(part[:, 0:rows], ps[:, 6, 0:rows]).then_inc(part_copied, 1)

            @block.vector
            def _(dve):
                link = Chain(dve, own)
                dve.wait_ge(rows_in, 16 * 4 * (1 + DEC_B))
                for which in ("g1", "sc2", "g2"):
                    for kind, rows in enumerate((P, NS)):
                        at = g.rows[which][kind][0:rows, :]
                        nc.vector.tensor_scalar(at, at, 1.0, None, ALU.add).then_inc(plus_one, 1)
                link(nc.vector.tensor_reduce(fold[:], g.ident[:].rearrange("p (j r) -> p r j", j=4), AX.X, ALU.add))
                dve.wait_ge(plus_one, 6)
                dve.wait_ge(par_in, 64)
                dve.wait_ge(consts, 2)

                def logits(t):
                    rows = TILE_ROWS[t]
                    dve.wait_ge(logits_full, t + 1)
                    nc.vector.tensor_tensor(g.logits[0:rows, t, :], ps[0:rows, 7, 0:NG + NEXP], b_r[0:rows, :], ALU.add)\
                        .then_inc(logits_read, 1)

                for t in range(NT):
                    rows, b = TILE_ROWS[t], t % 2
                    r = r_t[b]
                    dve.wait_ge(m_full[b], t // 2 + 1)
                    nc.vector.tensor_tensor(r[0:rows, :], ps[0:rows, 2 * b:2 * b + 2, :].rearrange("p a n -> p (a n)"),
                                            mod("g1", t)[0:rows, :], ALU.mult).then_inc(m_read[b], 1)
                    dve.wait_ge(m_read[b], t // 2 + 1)
                    dve.wait_ge(x_in[b], 16 * (t // 2 + 1))
                    link(nc.vector.scalar_tensor_tensor(out=r[0:rows, :], in0=x_t[b][0:rows, :], scalar=ALPHA,
                                                        in1=r[0:rows, :], op0=ALU.mult, op1=ALU.add))
                    norm.variance(nc, link, r, rows)
                    if t:
                        logits(t - 1)
                    norm.apply(nc, dve, link, t, g.x1[0:rows, t, :], r, rows).then_inc(x1_done[b], 1)
                logits(NT - 1)

            @block.gpsimd
            def _(pool):
                link = Chain(pool, pool_own)
                nc.gpsimd.memset(w_r[:], 0.0).then_inc(wr_zero, 1)
                nc.gpsimd.memset(eps[:], EPS).then_inc(consts, 1)
                nc.gpsimd.memset(g.logits[:], 0.0).then_inc(consts, 1)
                pool.wait_ge(plus_one, 6)
                for t in range(NT):
                    rows, b = TILE_ROWS[t], t % 2
                    pool.wait_ge(x1_done[b], t // 2 + 1)
                    pool.wait_ge(h2_out[b], 16 * (t // 2))
                    if t >= 2:
                        for half in range(2):
                            pool.wait_ge(h2T_full[half], t - 1)
                    link(nc.gpsimd.tensor_tensor(h_t[b][0:rows, :], g.x1[0:rows, t, :], mod("sc2", t)[0:rows, :], ALU.mult))
                    nc.gpsimd.tensor_tensor(h_t[b][0:rows, :], h_t[b][0:rows, :], mod("sh2", t)[0:rows, :], ALU.add)\
                        .then_inc(h2_done[b], 1)


SLOT_TILES = (2 * T - NEXP) // P + NEXP


def route(nc, io, g, ps):
    W = NG + NEXP
    with ExitStack() as ctx:
        m = Mem(nc, ctx, "rt")
        sb = m.sb
        valid = sb("valid", [P, NT])
        turn4 = sb("turn4", [P, NT, 4])
        top = sb("top", [P, NT, 1])
        grp, e1, e2 = (sb(n, [P, NT, 4]) for n in ("grp", "e1", "e2"))
        diff, el, tmp = (sb(n, [P, NT, 4]) for n in ("diff", "el", "tmp"))
        picked = sb("picked", [P, NT, NG, EPG])
        p_top, l1, l2, w_sum = (sb(n, [P, NT, 1]) for n in ("p_top", "l1", "l2", "w_sum"))
        pair = [sb(f"pair{i}", [P, NT, NEXP]) for i in range(2)]
        both, place = sb("both", [P, NT, NEXP]), sb("place", [P, NT, NEXP])
        total, tiles, ends, base = (sb(n, [P, NEXP]) for n in ("total", "tiles", "ends", "base"))
        steps, over = sb("steps", [P, NT]), sb("over", [P, NEXP, NT])
        slot_f = sb("slot_f", [P, 2, NT])
        slot_i, slot_lo = sb("slot_i", [P, 2, NT], I32), sb("slot_lo", [P, 2, NT], I32)
        token = sb("token", [P, NT], I32)
        zeros = sb("zeros", [P, SLOT_TILES], I32)
        tile_no, past, owner = sb("tile_no", [1, SLOT_TILES]), sb("past", [1, SLOT_TILES, NEXP]), sb("owner", [1, SLOT_TILES])
        consts, own = m.sem("consts"), m.sem("own")
        shifted, exped, counted, sums_read = m.sem("shifted"), m.sem("exped"), m.sem("counted"), m.sem("sums_read")
        summed = m.sem("summed")
        zeroed, have_slots, scattered, listed = m.sem("zeroed"), m.sem("have_slots"), m.sem("scattered"), m.sem("listed")

        with nc.Block() as block:
            @block.gpsimd
            def _(pool):
                nc.gpsimd.memset(zeros[:], 0).then_inc(consts, 1)
                nc.gpsimd.affine_select(out=valid[:], in_=g.ones[:, 0:NT], compare_op=ALU.is_ge, fill=0.0, base=T - 1,
                                        pattern=[[-P, NT]], channel_multiplier=-1).then_inc(consts, 1)
                nc.gpsimd.iota(turn4[:], pattern=[[0, NT], [-1, 4]], base=4, channel_multiplier=0,
                               allow_small_or_imprecise_dtypes=True).then_inc(consts, 1)
                nc.gpsimd.iota(steps[:], pattern=[[P, NT]], base=0, channel_multiplier=0,
                               allow_small_or_imprecise_dtypes=True).then_inc(consts, 1)
                nc.gpsimd.iota(tile_no[:], pattern=[[1, SLOT_TILES]], base=0, channel_multiplier=0,
                               allow_small_or_imprecise_dtypes=True).then_inc(consts, 1)
                nc.gpsimd.iota(token[:], pattern=[[P, NT]], base=0, channel_multiplier=1).then_inc(consts, 1)
                pool.wait_ge(consts, 6)
                pool.dma_start(g.slot_token.rearrange("(p n) a -> p (n a)", p=P), zeros[:]).then_inc(zeroed, 16)
                pool.wait_ge(zeroed, 16)
                pool.wait_ge(have_slots, 1)
                for t in range(NT):
                    for i in range(2):
                        rows = TILE_ROWS[t]
                        pool.indirect_dma_start(g.slot_token, bass.IndirectOffsetOnAxis(slot_lo[0:rows, i, t:t + 1], 0),
                                                token[0:rows, t:t + 1], None).then_inc(scattered, 16)
                pool.wait_ge(scattered, 32 * NT)
                pool.dma_start(g.slot_list[:], g.slot_token.rearrange("(p n) a -> p (n a)", p=P)).then_inc(listed, 16)
                pool.wait_ge(listed, 16)

            @block.scalar
            def _(act):
                act.wait_ge(shifted, 1)
                nc.scalar.activation(diff[:], diff[:], ACT.Exp).then_inc(exped, 1)
                act.wait_ge(shifted, 2)
                nc.scalar.activation(l2[:], l2[:], ACT.Exp).then_inc(exped, 1)

            @block.tensor
            def _(pe):
                pe.wait_ge(counted, 1)
                flat = both[:].rearrange("p t e -> p (t e)")
                nc.tensor.matmul(ps[:, 0, 0:NT * NEXP], g.before[:], flat, start=True, stop=True).then_inc(summed, 1)
                nc.tensor.matmul(ps[:, 1, 0:NT * NEXP], g.ones[:, 0:P], flat, start=True, stop=True).then_inc(summed, 1)

            @block.vector
            def _(dve):
                link = Chain(dve, own)
                v = nc.vector
                lg = g.logits[:, :, 0:NG]

                def first_max(out, values, maximum):
                    link(v.tensor_reduce(maximum[:], values, AX.X, ALU.max))
                    link(v.tensor_tensor(tmp[:], values, maximum[:].to_broadcast([P, NT, 4]), ALU.is_equal))
                    link(v.tensor_tensor(tmp[:], tmp[:], turn4[:], ALU.mult))
                    link(v.tensor_reduce(top[:], tmp[:], AX.X, ALU.max))
                    link(v.tensor_tensor(out[:], tmp[:], top[:].to_broadcast([P, NT, 4]), ALU.is_equal))

                dve.wait_ge(consts, 6)
                first_max(grp, lg, p_top)
                v.tensor_tensor(diff[:], lg, p_top[:].to_broadcast([P, NT, 4]), ALU.subtract).then_inc(shifted, 1)
                link(v.tensor_tensor(picked[:], g.logits[:, :, NG:W].rearrange("p t (g e) -> p t g e", g=NG),
                                     grp[:].unsqueeze(3).to_broadcast([P, NT, NG, EPG]), ALU.mult))
                link(v.tensor_reduce(el[:], picked[:].rearrange("p t g e -> p t e g"), AX.X, ALU.add))
                first_max(e1, el[:], l1)
                link(v.scalar_tensor_tensor(out=el[:], in0=e1[:], scalar=NEG, in1=el[:], op0=ALU.mult, op1=ALU.add))
                first_max(e2, el[:], l2)
                v.tensor_tensor(l2[:], l2[:], l1[:], ALU.subtract).then_inc(shifted, 1)
                dve.wait_ge(exped, 1)
                link(v.tensor_reduce(p_top[:], diff[:], AX.X, ALU.add))
                link(v.reciprocal(p_top[:], p_top[:]))
                dve.wait_ge(exped, 2)
                link(v.tensor_scalar(w_sum[:], l2[:], 1.0, None, ALU.add))
                link(v.reciprocal(w_sum[:], w_sum[:]))
                link(v.tensor_tensor(g.weight[:, 0, :].unsqueeze(2), w_sum[:], p_top[:], ALU.mult))
                link(v.tensor_tensor(g.weight[:, 1, :].unsqueeze(2), g.weight[:, 0, :].unsqueeze(2), l2[:], ALU.mult))
                link(v.tensor_tensor(grp[:], grp[:], valid[:].unsqueeze(2).to_broadcast([P, NT, 4]), ALU.mult))
                for i, e in enumerate((e1, e2)):
                    link(v.tensor_tensor(pair[i][:].rearrange("p t (g e) -> p t g e", g=NG),
                                         grp[:].unsqueeze(3).to_broadcast([P, NT, NG, EPG]),
                                         e[:].unsqueeze(2).to_broadcast([P, NT, NG, EPG]), ALU.mult))
                v.tensor_tensor(both[:], pair[0][:], pair[1][:], ALU.add).then_inc(counted, 1)
                dve.wait_ge(summed, 2)
                link(v.tensor_copy(place[:], ps[:, 0, 0:NT * NEXP].rearrange("p (t e) -> p t e", e=NEXP)))
                sums = ps[:, 1, 0:NT * NEXP].rearrange("p (t e) -> p t e", e=NEXP)
                link(v.tensor_copy(total[:], sums[:, 0, :]))
                for t in range(1, NT):
                    link(v.tensor_tensor(place[:, t, :], place[:, t, :], total[:], ALU.add))
                    link(v.tensor_tensor(total[:], sums[:, t, :], total[:], ALU.add))
                link(v.tensor_tensor(over[:], total[:].unsqueeze(2).to_broadcast([P, NEXP, NT]),
                                     steps[:].unsqueeze(1).to_broadcast([P, NEXP, NT]), ALU.is_gt))
                link(v.tensor_reduce(tiles[:], over[:], AX.X, ALU.add))
                link(v.tensor_tensor_scan(ends[:], g.ones[:, 0:NEXP], tiles[:], 0.0, ALU.mult, ALU.add))
                link(v.tensor_tensor(base[:], ends[:], tiles[:], ALU.subtract))
                link(v.tensor_scalar(base[:], base[:], float(P), None, ALU.mult))
                link(v.tensor_tensor(place[:], place[:], base[:].unsqueeze(1).to_broadcast([P, NT, NEXP]), ALU.add))
                for i in range(2):
                    link(v.tensor_tensor(pair[i][:], pair[i][:], place[:], ALU.mult))
                    link(v.tensor_reduce(slot_f[:, i, :], pair[i][:], AX.X, ALU.add))
                link(v.tensor_copy(g.slot[:], slot_f[:]))
                link(v.tensor_scalar(slot_i[:], g.slot[:], P.bit_length() - 1, None, ALU.logical_shift_right))
                link(v.tensor_scalar(slot_lo[:], g.slot[:], P - 1, None, ALU.bitwise_and))
                link(v.tensor_scalar(slot_lo[:], slot_lo[:], float(SLOT_TILES), None, ALU.mult))
                v.tensor_tensor(slot_lo[:], slot_lo[:], slot_i[:], ALU.add).then_inc(have_slots, 1)
                link(v.tensor_tensor(past[:], tile_no[:].unsqueeze(2).to_broadcast([1, SLOT_TILES, NEXP]),
                                     ends[0:1, :].unsqueeze(1).to_broadcast([1, SLOT_TILES, NEXP]), ALU.is_ge))
                link(v.tensor_reduce(owner[:], past[:], AX.X, ALU.add))
                link(v.tensor_scalar(owner[:], owner[:], float(NEXP - 1), None, ALU.min))
                link(v.tensor_copy(g.tile_expert[:], owner[:]))


def experts(nc, io, g, ps):
    KE = DE // P
    LAST = SLOT_TILES // 2 - 1
    with ExitStack() as ctx:
        m = Mem(nc, ctx, "ex")

        def two(name, shape, dt=F32):
            return [m.sb(f"{name}{s}", shape, dt) for s in range(2)]

        w_gu, w_dn = two("w_gu", [P, KD, 2 * DE]), two("w_dn", [P, KE, D])
        x, y, who = two("x", [P, D]), two("y", [P, D]), two("who", [P, 1], I32)
        xT, gate, act_in, aT = two("xT", [P, KD, P]), two("gate", [P, DE]), two("act_in", [P, DE]), two("aT", [P, KE, P])
        gu_in, dn_in, x_in, who_set = (m.sems(n, 2) for n in ("gu_in", "dn_in", "x_in", "who_set"))
        who_seen = m.sem("who_seen")
        xT_full, xT_copied, y_copied = ([m.sems(f"{n}{h}", 2) for h in range(2)] for n in ("xT_full", "xT_copied", "y_copied"))
        gu_full, gated, a_done, aT_full, aT_copied, y_full, stored = (
            m.sems(n, 2) for n in ("gu_full", "gated", "a_done", "aT_full", "aT_copied", "y_full", "stored"))
        gate_v = io["w_exp_gate"][0].rearrange("e (k p) f -> e p k f", p=P)
        up_v = io["w_exp_up"][0].rearrange("e (k p) f -> e p k f", p=P)
        down_v = io["w_exp_down"][0].rearrange("e (k p) n -> e p k n", p=P)
        y_v = g.y_rows.rearrange("(t p) n -> t p n", p=P)

        def wait_before(eng, sems, use, s):
            if s:
                eng.wait_ge(sems[0], START + use + 1)
            else:
                eng.wait_ge(sems[1], START + use)

        m.start(gu_full + y_full + xT_full[0] + xT_full[1] + xT_copied[0] + xT_copied[1] + a_done + aT_copied
                + y_copied[0] + y_copied[1] + aT_full + stored)

        with nc.Block() as block:
            @block.sync
            def _(sp):
                with sp.Fori(0, LAST + 1) as use:
                    for s in range(2):
                        e = sp.value_load(g.tile_expert[0:1, bass.ds(2 * use + s, 1)], min_val=0, max_val=NEXP - 1)
                        sp.wait_ge(gu_full[s], START + use)
                        for at, src in ((0, gate_v), (DE, up_v)):
                            sp.dma_start(w_gu[s][:, :, at:at + DE], src[bass.ds(e, 1)].rearrange("a p k f -> (a p) k f"))\
                                .then_inc(gu_in[s], 16)
                        sp.wait_ge(y_full[s], START + use)
                        sp.dma_start(w_dn[s][:], down_v[bass.ds(e, 1)].rearrange("a p k f -> (a p) k f"))\
                            .then_inc(dn_in[s], 16)

            @block.gpsimd
            def _(pool):
                with pool.Fori(0, LAST + 1) as use:
                    for s in range(2):
                        for half in range(2):
                            pool.wait_ge(xT_full[half][s], START + use)
                        nc.gpsimd.tensor_copy(who[s][:], g.slot_list[:, bass.ds(2 * use + s, 1)]).then_inc(who_set[s], 1)
                        pool.wait_ge(who_set[s], use + 1)
                        pool.sem_inc(who_seen, 1)
                        pool.indirect_dma_start(x[s][:], None, g.h2_rows, bass.IndirectOffsetOnAxis(who[s][:, 0:1], 0))\
                            .then_inc(x_in[s], 16)

            @block.tensor
            def _(pe):
                def x_transposes(use, s):
                    pe.wait_ge(x_in[s], 16 * use + 16)
                    for half in range(2):
                        wait_before(pe, xT_copied[half], use, s)
                        for k in range(4):
                            last = nc.tensor.transpose(ps[:, half, k * P:(k + 1) * P],
                                                       x[s][:, (4 * half + k) * P:(4 * half + k + 1) * P], g.ident[:])
                        last.then_inc(xT_full[half][s], 1)

                def gate_up(use, s):
                    for half in range(2):
                        pe.wait_ge(xT_copied[half][s], START + use + 1)
                    pe.wait_ge(gu_in[s], 32 * use + 32)
                    pe.wait_ge(a_done[s], START + use)
                    for k in range(KD):
                        last = nc.tensor.matmul(ps[:, 2 + s, :], xT[s][:, k, :], w_gu[s][:, k, :], start=(k == 0),
                                                stop=(k == KD - 1))
                    last.then_inc(gu_full[s], 1)

                def a_transposes(use, s):
                    pe.wait_ge(a_done[s], START + use + 1)
                    pe.wait_ge(aT_copied[s], START + use)
                    for k in range(KE):
                        last = nc.tensor.transpose(ps[:, 4 + s, k * P:(k + 1) * P], act_in[s][:, k * P:(k + 1) * P],
                                                   g.ident[:])
                    last.then_inc(aT_full[s], 1)

                def down(use, s):
                    pe.wait_ge(aT_copied[s], START + use + 1)
                    pe.wait_ge(dn_in[s], 16 * use + 16)
                    for half in range(2):
                        wait_before(pe, y_copied[half], use, s)
                    for half in range(2):
                        for k in range(KE):
                            last = nc.tensor.matmul(ps[:, 6 + half, :], aT[s][:, k, :],
                                                    w_dn[s][:, k, half * 512:(half + 1) * 512], start=(k == 0),
                                                    stop=(k == KE - 1))
                    last.then_inc(y_full[s], 1)

                x_transposes(0, 0)
                gate_up(0, 0)
                x_transposes(0, 1)
                with pe.Fori(0, LAST) as use:
                    for s in range(2):
                        gate_up(use + s, 1 - s)
                        a_transposes(use, s)
                        x_transposes(use + 1, s)
                        down(use, s)
                gate_up(LAST, 1)
                for s in range(2):
                    a_transposes(LAST, s)
                    down(LAST, s)

            def copy_x(eng, copy, half, use, s):
                eng.wait_ge(xT_full[half][s], START + use + 1)
                copy(xT[s][:, 4 * half:4 * half + 4, :], ps[:, half, :].rearrange("p (k n) -> p k n", k=4))\
                    .then_inc(xT_copied[half][s], 1)

            def copy_y(eng, copy, half, use, s):
                eng.wait_ge(y_full[s], START + use + 1)
                eng.wait_ge(stored[s], START + 16 * use)
                copy(y[s][:, half * 512:(half + 1) * 512], ps[:, 6 + half, :]).then_inc(y_copied[half][s], 1)

            @block.vector
            def _(dve):
                copy = nc.vector.tensor_copy

                def activations(use, s):
                    dve.wait_ge(gated[s], use + 1)
                    dve.wait_ge(aT_full[s], START + use)
                    nc.vector.tensor_tensor(act_in[s][:], ps[:, 2 + s, DE:2 * DE], gate[s][:], ALU.mult)\
                        .then_inc(a_done[s], 1)

                def copy_a(use, s):
                    dve.wait_ge(aT_full[s], START + use + 1)
                    copy(aT[s][:], ps[:, 4 + s, 0:KE * P].rearrange("p (k n) -> p k n", k=KE)).then_inc(aT_copied[s], 1)

                copy_x(dve, copy, 0, 0, 0)
                activations(0, 0)
                copy_x(dve, copy, 0, 0, 1)
                with dve.Fori(0, LAST) as use:
                    for s in range(2):
                        copy_a(use, s)
                        activations(use + s, 1 - s)
                        copy_x(dve, copy, 0, use + 1, s)
                        copy_y(dve, copy, 0, use, s)
                copy_a(LAST, 0)
                activations(LAST, 1)
                copy_y(dve, copy, 0, LAST, 0)
                copy_a(LAST, 1)
                copy_y(dve, copy, 0, LAST, 1)

            @block.scalar
            def _(act):
                copy = nc.scalar.copy

                def silu(use, s):
                    act.wait_ge(gu_full[s], START + use + 1)
                    act.wait_ge(a_done[s], START + use)
                    nc.scalar.activation(gate[s][:], ps[:, 2 + s, 0:DE], ACT.Silu).then_inc(gated[s], 1)

                def store(use, s):
                    for half in range(2):
                        act.wait_ge(y_copied[half][s], START + use + 1)
                    act.dma_start(y_v[bass.ds(2 * use + s, 1)].rearrange("a p n -> (a p) n"), y[s][:])\
                        .then_inc(stored[s], 16)

                nc.scalar.preload_act_table(ACT.Silu)
                copy_x(act, copy, 1, 0, 0)
                silu(0, 0)
                copy_x(act, copy, 1, 0, 1)
                with act.Fori(0, LAST) as use:
                    for s in range(2):
                        silu(use + s, 1 - s)
                        copy_x(act, copy, 1, use + 1, s)
                        copy_y(act, copy, 1, use, s)
                        store(use, s)
                silu(LAST, 1)
                for s in range(2):
                    copy_y(act, copy, 1, LAST, s)
                    store(LAST, s)
                for s in range(2):
                    act.wait_ge(stored[s], START + 16 * (LAST + 1))


def combine(nc, io, g, ps):
    with ExitStack() as ctx:
        m = Mem(nc, ctx, "cb")
        ya, yb, r_t, out_t = ([m.sb(f"{n}{i}", [P, D]) for i in range(2)] for n in ("ya", "yb", "r", "out"))
        ln_g, ln_b, eps = m.sb("ln_g", [P, D]), m.sb("ln_b", [P, D]), m.sb("eps", [P, 1])
        norm = Norm(m, eps, ln_g, ln_b)
        par_in, eps_set, own, weighted_own = m.sem("par_in"), m.sem("eps_set"), m.sem("own"), m.sem("weighted_own")
        y_in, weighted, added, scaled, summed, ready, out = (
            m.sems(n, 2) for n in ("y_in", "weighted", "added", "scaled", "summed", "ready", "out"))
        y_out = [io["y_prompt"][0, t * P:(t + 1) * P, :] for t in range(PT)] + [io["y_sample"].rearrange("b s d -> (b s) d")]

        with nc.Block() as block:
            @block.sync
            def _(sp):
                for dst, src in ((ln_g, io["ln2_g"]), (ln_b, io["ln2_b"])):
                    sp.dma_start(dst[:], src.partition_broadcast(P).rearrange("p a n -> p (a n)")).then_inc(par_in, 16)
                for t in range(NT):
                    rows, b = TILE_ROWS[t], t % 2
                    sp.wait_ge(ready[b], t // 2 + 1)
                    sp.dma_start(y_out[t], out_t[b][0:rows, :]).then_inc(out[b], 16)
                for b in range(2):
                    sp.wait_ge(out[b], 16 * ((NT + 1 - b) // 2))

            @block.gpsimd
            def _(pool):
                nc.gpsimd.memset(eps[:], EPS).then_inc(eps_set, 1)

                def gather(t):
                    rows, b = TILE_ROWS[t], t % 2
                    if t >= 2:
                        pool.wait_ge(added[b], t // 2)
                    for i, dst in enumerate((ya, yb)):
                        pool.indirect_dma_start(dst[b][0:rows, :], None, g.y_rows,
                                                bass.IndirectOffsetOnAxis(g.slot[0:rows, i, t:t + 1], 0))\
                            .then_inc(y_in[b], 16)

                gather(0)
                for t in range(NT):
                    rows, b = TILE_ROWS[t], t % 2
                    if t + 1 < NT:
                        gather(t + 1)
                    pool.wait_ge(weighted[b], 2 * (t // 2) + 2)
                    if t >= 2:
                        pool.wait_ge(ready[b], t // 2)
                    nc.gpsimd.tensor_tensor(r_t[b][0:rows, :], ya[b][0:rows, :], yb[b][0:rows, :], ALU.add)\
                        .then_inc(added[b], 1)
                    pool.wait_ge(added[b], t // 2 + 1)
                    nc.gpsimd.tensor_tensor(r_t[b][0:rows, :], r_t[b][0:rows, :],
                                            g.rows["g2"][0 if t < PT else 1][0:rows, :], ALU.mult).then_inc(scaled[b], 1)

            @block.scalar
            def _(act):
                def weigh(t):
                    rows, b = TILE_ROWS[t], t % 2
                    act.wait_ge(y_in[b], 32 * (t // 2) + 32)
                    for i, at in enumerate((ya, yb)):
                        nc.scalar.activation(at[b][0:rows, :], at[b][0:rows, :], ACT.Copy,
                                             scale=g.weight[0:rows, i, t:t + 1]).then_inc(weighted[b], 1)

                act.wait_ge(eps_set, 1)
                weigh(0)
                for t in range(NT):
                    if t + 1 < NT:
                        weigh(t + 1)
                    norm.deviation(nc, act, t, TILE_ROWS[t])

            @block.vector
            def _(dve):
                link = Chain(dve, own)
                dve.wait_ge(par_in, 32)
                for t in range(NT):
                    rows, b = TILE_ROWS[t], t % 2
                    r = r_t[b]
                    dve.wait_ge(scaled[b], t // 2 + 1)
                    link(nc.vector.scalar_tensor_tensor(out=r[0:rows, :], in0=g.x1[0:rows, t, :], scalar=ALPHA,
                                                        in1=r[0:rows, :], op0=ALU.mult, op1=ALU.add))
                    norm.variance(nc, link, r, rows)
                    if t >= 2:
                        dve.wait_ge(out[b], 16 * (t // 2))
                    norm.apply(nc, dve, link, t, out_t[b][0:rows, :], r, rows).then_inc(ready[b], 1)


class Shared:
    pass


def hybrid_decoder_step(nc, inputs, outputs):
    io = {**inputs, **outputs}
    g = Shared()
    with ExitStack() as ctx:
        m = Mem(nc, ctx, "g")

        def scratch(name, shape, dt=F32):
            return nc.dram_tensor(name, shape, dt, kind="Internal").ap()

        g.ada_rows = scratch("ada_rows", [NB, 6, D])
        g.q_rows = scratch("q_rows", [NS, DA])
        g.h2_rows = scratch("h2_rows", [T, D])
        g.slot_token = scratch("slot_token", [SLOT_TILES * P, 1], I32)
        g.y_rows = scratch("y_rows", [SLOT_TILES * P, D])
        ps = ctx.enter_context(nc.psum_tensor("ps", [P, 8, 512], F32))
        g.ident, g.before, g.causal = (m.sb(name, [P, P]) for name in ("ident", "before", "causal"))
        g.after, g.ones = m.sb("after", [P, 4 * P]), m.sb("ones", [P, 4 * P])
        g.ncum, g.ncum_new = m.sb("ncum", [P, NT, H]), m.sb("ncum_new", [H, NS])
        g.hT_odd, g.xT_odd = m.sems("hT_odd", 4), m.sems("xT_odd", 4)
        g.arena = m.sb("arena", [P, (KD + DA // P + NGRP) * T])
        part, at = {}, 0
        for name, k in (("hT", KD), ("aT", DA // P), ("uT", NGRP)):
            part[name] = g.arena[:, at:at + k * T].rearrange("p (k n) -> p k n", k=k)
            at += k * T
        g.hT, g.aT, g.uT = part["hT"], part["aT"], part["uT"]
        modulate(nc, io, g, ps)
        with ExitStack() as z_ctx:
            g.z = Mem(nc, z_ctx, "z").sb("z", [P, 2, 2, NT, 512])
            project_in(nc, io, g, ps)
            gmlp(nc, io, g, ps)
            attend_prompt(nc, io, g, ps)
        attend_sample(nc, io, g, ps)
        g.logits, g.weight = m.sb("logits", [P, NT, NG + NEXP]), m.sb("weight", [P, 2, NT])
        g.slot, g.slot_list = m.sb("slot", [P, 2, NT], I32), m.sb("slot_list", [P, SLOT_TILES], I32)
        g.tile_expert = m.sb("tile_expert", [1, SLOT_TILES], I32)
        g2 = m.sb("g2", [P, 2, D])
        with ExitStack() as m_ctx:
            mT = Mem(nc, m_ctx, "m").sb("mT", [P, KD, T])
            mix(nc, io, g, ps, mT)
            g.x1 = g.arena[:, 0:NT * D].rearrange("p (t n) -> p t n", t=NT)
            at = NT * D
            g.rows = {"g2": (g2[:, 0, :], g2[:, 1, :])}
            for name in ("g1", "sc2", "sh2"):
                g.rows[name] = (g.arena[:, at:at + D], g.arena[:, at + D:at + 2 * D])
                at += 2 * D
            g.ln_g = g.arena[:, at:at + D]
            mixer_out(nc, io, g, ps, mT)
        route(nc, io, g, ps)
        experts(nc, io, g, ps)
        combine(nc, io, g, ps)


OUTPUTS = {
    "y_prompt": (1, SEQ, D), "y_sample": (DEC_B, DEC_S, D),
    "new_k_prompt": (1, 1, SEQ, H, HD), "new_v_prompt": (1, 1, SEQ, H, HD), "new_logf_prompt": (1, 1, SEQ, H),
    "new_k_sample": (1, DEC_B, DEC_S, H, HD), "new_v_sample": (1, DEC_B, DEC_S, H, HD),
    "new_logf_sample": (1, DEC_B, DEC_S, H), "new_gmlp_v_sample": (1, DEC_B, DEC_S, DG),
}


def kernel(**inputs):
    import concourse.bacc as bacc
    from concourse.bass_utils import run_bass_kernel_spmd

    nc = bacc.Bacc("TRN2", target_bir_lowering=False, num_devices=1)
    arrays = {name: np.ascontiguousarray(a) for name, a in inputs.items()}
    ins = {name: nc.dram_tensor(name, a.shape, mybir.dt.from_np(a.dtype), kind="ExternalInput").ap()
           for name, a in arrays.items()}
    outs = {name: nc.dram_tensor(name, shape, F32, kind="ExternalOutput").ap() for name, shape in OUTPUTS.items()}
    hybrid_decoder_step(nc, ins, outs)
    result = run_bass_kernel_spmd(nc, [arrays], core_ids=[0])
    return tuple(result.results[0][name] for name in OUTPUTS)
```

```python
from contextlib import ExitStack

import numpy as np

import concourse.bass as bass
from concourse import mybir

F32 = mybir.dt.float32
I32 = mybir.dt.int32
ALU = mybir.AluOpType
ACT = mybir.ActivationFunctionType
AX = mybir.AxisListType

P = 128
D = 1024
KD = D // P
SEQ = 1024
DEC_B, DEC_S = 8, 4
NS = DEC_B * DEC_S
T = SEQ + NS
PT = SEQ // P
NT = PT + 1
BLK = T // 3
H, HD = 8, 64
DA = H * HD
DG = 512
NGRP = DG // P
PAGES = 32
NB = 1 + DEC_B
COL_Q, COL_K, COL_V = 0, DA, 2 * DA
COL_F = 3 * DA
COL_U = COL_F + H
COL_GV = COL_U + DG
COL_GA = COL_GV + DG
COL_GG = COL_GA + D
ALPHA = 2.0 ** 0.25
EPS = 1e-5
NEG = -1e30
NEXP, EPG, NG = 16, 4, 4
DE = 256
TILE_ROWS = [P] * PT + [NS]


START = 1


class Chain:

    def __init__(self, eng, sem):
        self.eng, self.sem, self.base, self.n = eng, sem, 0, 0

    def __call__(self, ins):
        ins.then_inc(self.sem, 1)
        self.n += 1
        self.eng.wait_ge(self.sem, self.base + self.n)

    def enter(self, it, per):
        self.before, self.per = self.base + self.n, per
        self.base, self.n = self.before + it * per, 0

    def leave(self, trips):
        assert self.n == self.per, (self.n, self.per)
        self.base, self.n = self.before + trips * self.per, 0


class Mem:

    def __init__(self, nc, ctx, tag):
        self.nc, self.ctx, self.tag, self.taken = nc, ctx, tag, []
        ctx.callback(self.release)

    def sb(self, name, shape, dt=F32):
        return self.ctx.enter_context(self.nc.sbuf_tensor(f"{self.tag}_{name}", shape, dt))

    def sem(self, name):
        self.taken.append(self.nc.alloc_semaphore(f"{self.tag}_{name}"))
        return self.taken[-1]

    def sems(self, name, n):
        return [self.sem(f"{name}{i}") for i in range(n)]

    def start(self, sems):
        for sem in sems:
            self.nc.gpsimd.sem_inc(sem, START)
        self.nc.all_engine_barrier()

    def release(self):
        if self.taken:
            self.nc.clear_and_free_semaphores(self.taken)
            self.nc.all_engine_barrier()


def modulate(nc, io, g, ps):
    with ExitStack() as ctx:
        m = Mem(nc, ctx, "mod")
        c_sb, cs = m.sb("c", [NB, D]), m.sb("cs", [NB, D])
        csT = g.csT
        b_bc = m.sb("b_bc", [NB, 2 * D])
        ada = m.sb("ada", [NB, 2, D])
        w = [g.arena[:, KD * T:KD * T + KD * D].rearrange("p (k n) -> p k n", k=KD), m.sb("w1", [P, KD, D])]
        x_sb, xs_sb = m.sb("x", [P, PT, D]), m.sb("xs", [NS, D])
        modT = m.sb("modT", [P, 2, KD, NB])
        hs = m.sb("hs", [P, KD, NS])
        ones = g.ones
        zero = m.sem("zero")
        consts = m.sem("consts")
        c_in, bias_in, x_in = m.sem("c_in"), m.sem("bias_in"), m.sem("x_in")
        w_in = m.sems("w_in", 2)
        silu_done, cT_done, cT_copied = m.sem("silu"), m.sem("cT_done"), m.sem("cT_copied")
        ada_mm, ada_copied = m.sems("ada_mm", 2), m.sems("ada_copied", 2)
        modT_done, modT_copied = m.sem("modT_done"), m.sem("modT_copied")
        xT_done, hT_done = m.sems("xT_done", 4), m.sems("hT_done", 4)
        own = m.sem("own")
        xsT_done = m.sem("xsT_done")
        w_v = io["w_ada"][0].rearrange("(k p) n -> p k n", p=P)

        with nc.Block() as block:
            @block.sync
            def _(sp):
                sp.dma_start(c_sb[0:1, :], io["c_prompt"]).then_inc(c_in, 16)
                sp.dma_start(c_sb[1:NB, :], io["c_sample"]).then_inc(c_in, 16)
                sp.dma_start(b_bc[:], io["b_ada"][:, 0:2 * D].partition_broadcast(NB).rearrange("p a n -> p (a n)")).then_inc(bias_in, 16)
                for s in range(2):
                    sp.dma_start(w[s][:, :, :], w_v[:, :, s * D:(s + 1) * D]).then_inc(w_in[s], 16)

            @block.gpsimd
            def _(pool):
                pool.dma_start(x_sb[:], io["x_prompt"][0].rearrange("(t p) d -> p t d", p=P)).then_inc(x_in, 16)
                pool.dma_start(xs_sb[:], io["x_sample"].rearrange("b s d -> (b s) d")).then_inc(x_in, 16)
                nc.gpsimd.memset(g.ident[:], 0.0).then_inc(zero, 1)
                nc.gpsimd.memset(ones[:], 1.0).then_inc(zero, 1)
                nc.gpsimd.memset(g.causal[:], 0.0).then_inc(zero, 1)
                pool.wait_ge(zero, 3)
                nc.gpsimd.affine_select(out=g.ident[:], in_=g.ident[:], compare_op=ALU.not_equal, fill=1.0, base=0,
                                        pattern=[[-1, P]], channel_multiplier=1).then_inc(consts, 1)
                nc.gpsimd.affine_select(out=g.before[:], in_=ones[:, 0:P], compare_op=ALU.is_gt, fill=0.0, base=0,
                                        pattern=[[1, P]], channel_multiplier=-1).then_inc(consts, 1)
                nc.gpsimd.memset(g.after[:, 0:3 * P], 1.0).then_inc(consts, 1)
                nc.gpsimd.affine_select(out=g.after[:, 3 * P:4 * P], in_=ones[:, 0:P], compare_op=ALU.is_gt, fill=0.0,
                                        base=0, pattern=[[-1, P]], channel_multiplier=1).then_inc(consts, 1)
                nc.gpsimd.affine_select(out=g.causal[:], in_=g.causal[:], compare_op=ALU.is_ge, fill=NEG, base=0,
                                        pattern=[[-1, P]], channel_multiplier=1).then_inc(consts, 1)

            @block.scalar
            def _(act):
                act.wait_ge(c_in, 32)
                nc.scalar.activation(cs[:], c_sb[:], ACT.Silu).then_inc(silu_done, 1)
                act.wait_ge(modT_copied, 2)
                for k in range(0, KD, 2):
                    for half in range(2):
                        b = 2 * ((k // 2) % 2) + half
                        act.wait_ge(xT_done[b], k // 4 + 1)
                        nc.scalar.activation(g.hT[:, k, half * 512:half * 512 + 512], ps[:, b, :], ACT.Identity,
                                             scale=modT[:, 1, k, 0:1], bias=modT[:, 0, k, 0:1]).then_inc(hT_done[b], 1)

            @block.tensor
            def _(pe):
                pe.wait_ge(silu_done, 1)
                pe.wait_ge(consts, 1)
                for k in range(KD):
                    last = nc.tensor.transpose(ps[:, 0, 16 * k:16 * k + NB], cs[:, k * P:k * P + P], g.ident[0:NB, 0:NB])
                last.then_inc(cT_done, 1)
                pe.wait_ge(cT_copied, 1)
                for s in range(2):
                    pe.wait_ge(w_in[s], 16)
                    for k in range(KD):
                        for j in range(4):
                            last = nc.tensor.matmul(ps[32 * j:32 * j + NB, 1 + s, 0:256], csT[:, k, :],
                                                    w[s][:, k, 256 * j:256 * j + 256],
                                                    start=(k == 0), stop=(k == KD - 1))
                    last.then_inc(ada_mm[s], 1)
                for s in range(2):
                    pe.wait_ge(ada_copied[s], 1)
                for r in range(2):
                    for k in range(KD):
                        last = nc.tensor.transpose(ps[:, 3, 16 * (KD * r + k):16 * (KD * r + k) + NB],
                                                   ada[:, r, k * P:k * P + P], g.ident[0:NB, 0:NB])
                last.then_inc(modT_done, 1)
                pe.wait_ge(modT_copied, 2)
                pe.wait_ge(x_in, 32)
                for k in range(KD):
                    for half in range(2):
                        b = (4 if k % 2 else 0) + 2 * ((k // 2) % 2) + half
                        if b < 4:
                            pe.wait_ge(hT_done[b], k // 4)
                        else:
                            pe.wait_ge(g.hT_odd[b - 4], k // 4)
                        for i in range(4):
                            last = nc.tensor.transpose(ps[:, b, i * P:i * P + P],
                                                       x_sb[:, 4 * half + i, k * P:k * P + P], g.ident[:])
                        last.then_inc(xT_done[b] if b < 4 else g.xT_odd[b - 4], 1)
                pe.wait_ge(hT_done[0], 2)
                for k in range(KD):
                    last = nc.tensor.transpose(ps[:, 0, NS * k:NS * k + NS], xs_sb[:, k * P:k * P + P],
                                               g.ident[0:NS, 0:NS])
                last.then_inc(xsT_done, 1)

            @block.vector
            def _(dve):
                link = Chain(dve, own)
                dve.wait_ge(cT_done, 1)
                nc.vector.tensor_copy(csT[:], ps[:, 0, 0:16 * KD].rearrange("p (k n) -> p k n", n=16)[:, :, 0:NB])\
                    .then_inc(cT_copied, 1)
                dve.wait_ge(bias_in, 16)
                for s in range(2):
                    dve.wait_ge(ada_mm[s], 1)
                    for j in range(4):
                        at = slice(256 * j, 256 * j + 256)
                        last = nc.vector.tensor_tensor(ada[:, s, at], ps[32 * j:32 * j + NB, 1 + s, 0:256],
                                                       b_bc[:, s * D + 256 * j:s * D + 256 * j + 256], ALU.add)
                    last.then_inc(ada_copied[s], 1)
                dve.wait_ge(modT_done, 1)
                mT = ps[:, 3, 0:32 * KD].rearrange("p (r k n) -> p r k n", r=2, n=16)
                nc.vector.tensor_copy(modT[:, 0], mT[:, 0, :, 0:NB]).then_inc(modT_copied, 1)
                nc.vector.tensor_scalar(modT[:, 1], mT[:, 1, :, 0:NB], 1.0, None, ALU.add).then_inc(modT_copied, 1)
                dve.wait_ge(modT_copied, 2)
                for k in range(1, KD, 2):
                    for half in range(2):
                        b = 2 * ((k // 2) % 2) + half
                        dve.wait_ge(g.xT_odd[b], k // 4 + 1)
                        nc.vector.tensor_scalar(g.hT[:, k, half * 512:half * 512 + 512], ps[:, 4 + b, :],
                                                modT[:, 1, k, 0:1], modT[:, 0, k, 0:1], ALU.mult, ALU.add)\
                            .then_inc(g.hT_odd[b], 1)
                dve.wait_ge(xsT_done, 1)
                seqs = "p k (b s) -> p k b s"
                per_seq = [modT[:, r, :, 1:NB].unsqueeze(3).to_broadcast([P, KD, DEC_B, DEC_S]) for r in range(2)]
                link(nc.vector.tensor_tensor(hs[:].rearrange(seqs, s=DEC_S),
                                             ps[:, 0, 0:NS * KD].rearrange("p (k b s) -> p k b s", k=KD, s=DEC_S),
                                             per_seq[1], ALU.mult))
                link(nc.vector.tensor_tensor(g.hT[:, :, SEQ:T].rearrange(seqs, s=DEC_S),
                                             hs[:].rearrange(seqs, s=DEC_S), per_seq[0], ALU.add))


def project_in(nc, io, g, ps, w_u, w_f, bf, u_in, f_in):
    PIECE, A = D // 4, 4
    with ExitStack() as ctx:
        m = Mem(nc, ctx, "pin")
        w = [m.sb(f"w{i}", [P, KD, 512]) for i in range(2)]
        w_in, w_used = m.sems("w_in", 2), m.sems("w_used", 2)
        full, free = m.sems("full", 6), m.sems("free", 6)
        out = m.sem("out")
        ada_w = [g.arena[:, KD * T + x * KD * PIECE:KD * T + (x + 1) * KD * PIECE].rearrange("p (k n) -> p k n", k=KD)
                 for x in range(2)]
        ada = g.arena[0:NB, KD * T + 2 * KD * PIECE:KD * T + 2 * KD * PIECE + 4 * D]
        ada_b = [m.sb(f"ada_b{x}", [NB, PIECE]) for x in range(2)]
        ada_in, ada_mm, ada_added, ada_out = m.sems("ada_in", 2), m.sems("ada_mm", 2), m.sems("ada_added", 2), m.sem("ada_out")
        ada_v = io["w_ada"][0].rearrange("(k p) n -> p k n", p=P)
        w_v = io["w_in"][0].rearrange("(k p) n -> p k n", p=P)

        def piece(it, s, a):
            return a % 2, A // 2 * (2 * it + s) + a // 2, (A * (2 * it + s) + a) * PIECE

        GROUPS = 2 * NT
        USES = GROUPS // 6

        m.start(w_used + free + ada_added)

        with nc.Block() as block:
            @block.sync
            def _(sp):
                with sp.Fori(0, 2) as it:
                    for s, (at, by) in enumerate(((COL_Q, COL_V - COL_Q), (COL_K, COL_GV - COL_K))):
                        sp.wait_ge(w_used[s], START + it)
                        sp.dma_start(w[s][:], w_v[:, :, bass.ds(it * by + at, 512)]).then_inc(w_in[s], 16)
                        for a in range(A):
                            x, use, column = piece(it, s, a)
                            sp.wait_ge(ada_added[x], START + use)
                            sp.dma_start(ada_w[x][:, :, :], ada_v[:, :, bass.ds(2 * D + column, PIECE)]).then_inc(ada_in[x], 16)
                            sp.dma_start(ada_b[x][:], io["b_ada"][:, bass.ds(2 * D + column, PIECE)].partition_broadcast(NB)
                                         .rearrange("p a n -> p (a n)")).then_inc(ada_in[x], 16)
                with nc.allow_non_contiguous_dma(reason="eight columns"):
                    sp.dma_start(w_f[:], w_v[:, :, COL_F:COL_F + H]).then_inc(f_in, 16)
                    sp.dma_start(bf[:], io["b_f"].rearrange("a h -> h a")).then_inc(f_in, 16)
                sp.dma_start(w_u[:], w_v[:, :, COL_U:COL_U + DG]).then_inc(u_in, 16)
                for x in range(2):
                    sp.wait_ge(ada_added[x], START + 2 * A)
                sp.dma_start(g.ada_rows.rearrange("b r n -> b (r n)"), ada).then_inc(ada_out, 16)
                sp.wait_ge(ada_out, 16)

            @block.tensor
            def _(pe):
                with pe.Fori(0, 2) as it:
                    for s in range(2):
                        pe.wait_ge(w_in[s], 16 * it + 16)
                        for t in range(NT):
                            n = s * NT + t
                            b, use = n % 6, n // 6
                            pe.wait_ge(free[b], START + it * USES + use)
                            for k in range(KD):
                                if t < PT:
                                    last = nc.tensor.matmul(ps[:, b, :], g.hT[:, k, t * P:(t + 1) * P], w[s][:, k, :],
                                                            start=(k == 0), stop=(k == KD - 1))
                                    continue
                                for j in range(4):
                                    last = nc.tensor.matmul(ps[NS * j:NS * j + NS, b, 0:P], g.hT[:, k, SEQ:T],
                                                            w[s][:, k, j * P:(j + 1) * P], start=(k == 0),
                                                            stop=(k == KD - 1))
                            last.then_inc(full[b], 1)
                            if t % 2:
                                x, use, _ = piece(it, s, t // 2)
                                pe.wait_ge(ada_in[x], 32 * use + 32)
                                pe.wait_ge(ada_added[x], START + use)
                                for k in range(KD):
                                    for j in range(4):
                                        last = nc.tensor.matmul(ps[32 * j:32 * j + NB, 6 + x, 0:PIECE // 4], g.csT[:, k, :],
                                                                ada_w[x][:, k, j * PIECE // 4:(j + 1) * PIECE // 4],
                                                                start=(k == 0), stop=(k == KD - 1))
                                last.then_inc(ada_mm[x], 1)

            def evacuate(eng, copy, parity, between=None):
                with eng.Fori(0, 2) as it:
                    for n in range(GROUPS):
                        b, use, s, t = n % 6, n // 6, n // NT, n % NT
                        if b % 2 == parity:
                            eng.wait_ge(full[b], it * USES + use + 1)
                            if t == NT - 1:
                                eng.sem_inc(w_used[s], 1)
                            if t < PT:
                                last = copy(g.z[:, bass.ds(it, 1), s, t, :].rearrange("p a n -> p (a n)"), ps[:, b, :])
                            else:
                                for j in range(4):
                                    last = copy(g.z[0:NS, bass.ds(it, 1), s, t, j * P:(j + 1) * P]
                                                .rearrange("p a n -> p (a n)"), ps[NS * j:NS * j + NS, b, 0:P])
                            last.then_inc(free[b], 1)
                        if between and t % 2:
                            between(it, s, t // 2)

            @block.vector
            def _(dve):
                def add_bias(it, s, a):
                    x, use, column = piece(it, s, a)
                    dve.wait_ge(ada_mm[x], use + 1)
                    for j in range(4):
                        at = j * PIECE // 4
                        last = nc.vector.tensor_tensor(ada[:, bass.ds(column + at, PIECE // 4)],
                                                       ps[32 * j:32 * j + NB, 6 + x, 0:PIECE // 4],
                                                       ada_b[x][:, at:at + PIECE // 4], ALU.add)
                    last.then_inc(ada_added[x], 1)

                evacuate(dve, nc.vector.tensor_copy, 0, add_bias)

            @block.scalar
            def _(act):
                evacuate(act, nc.scalar.copy, 1)

            @block.gpsimd
            def _(pool):
                tok = "(t p) n -> p t n"
                for dst, dst_s, src, groups in ((io["new_k_prompt"], io["new_k_sample"], g.z[:, 0, 1], GROUPS),
                                                (io["new_v_prompt"], io["new_v_sample"], g.z[:, 1, 0], GROUPS + NT)):
                    for b in range(6):
                        pool.wait_ge(free[b], START + (groups + 5 - b) // 6)
                    pool.dma_start(dst[0, 0].rearrange("s h d -> s (h d)").rearrange(tok, p=P), src[:, 0:PT, :])\
                        .then_inc(out, 16)
                    pool.dma_start(dst_s[0].rearrange("b s h d -> (b s) (h d)"), src[0:NS, PT, :]).then_inc(out, 16)
                pool.wait_ge(out, 4 * 16)


def gmlp(nc, io, g, ps, w_u, w_f, bf, u_in, f_in):
    UB = 4
    with ExitStack() as ctx:
        m = Mem(nc, ctx, "gm")
        ws, wsT = m.sb("ws", [P, NGRP, P]), m.sb("wsT", [P, NGRP, P])
        ws_new = m.sb("ws_new", [NS, NGRP, NS])
        upto = m.sb("upto", [P, P])
        bs = m.sb("bs", [P, NGRP, P])
        ln_g, ln_b = m.sb("ln_g", [P, DG]), m.sb("ln_b", [P, DG])
        stats, mv, rstd = m.sb("stats", [P, NT, 6]), m.sb("mv", [P, NT, 2]), m.sb("rstd", [P, NT])
        sp_b = [m.sb(f"sp{i}", [P, NGRP, P]) for i in range(2)]
        eps = m.sb("eps", [P, 1])
        f_x, f_e, f_u, f_l = (m.sb(n, [H, T]) for n in ("f_x", "f_e", "f_u", "f_l"))
        f_one = m.sb("f_one", [H, SEQ])
        logfT, ncumT, logf = m.sb("logfT", [H, T]), m.sb("ncumT", [H, T]), m.sb("logf", [P, NT, H])
        loaded, cleared, new_in, masked = m.sem("loaded"), m.sem("cleared"), m.sem("new_in"), m.sem("masked")
        gelu, have_var, have_std, normed = m.sem("gelu"), m.sem("have_var"), m.sem("have_std"), m.sem("normed")
        wsT_done, wsT_ready = m.sem("wsT_done"), m.sem("wsT_ready")
        sp_full, sp_free = m.sems("sp_full", 2), m.sems("sp_free", 2)
        u_full, u_done = m.sems("u_full", UB), m.sems("u_done", UB)
        f_full, f_abs, f_exp, f_log, f_cum = (m.sem(n) for n in ("f_full", "f_abs", "f_exp", "f_log", "f_cum"))
        fT_done, fT_copied = m.sem("fT_done"), m.sem("fT_copied")
        own, out, f_out, q_scaled = m.sem("own"), m.sem("out"), m.sem("f_out"), m.sem("q_scaled")
        gv = g.z[:, 1, 1]

        with nc.Block() as block:
            @block.sync
            def _(sp):
                sp.dma_start(ws[:], io["w_s"][0].rearrange("g t s -> t g s")).then_inc(loaded, 16)
                sp.dma_start(bs[:].rearrange("p g t -> p (g t)"),
                             io["b_s"].rearrange("a g t -> a (g t)").partition_broadcast(P)
                             .rearrange("p a n -> p (a n)")).then_inc(loaded, 16)
                for dst, src in ((ln_g, io["gmlp_ln_g"]), (ln_b, io["gmlp_ln_b"])):
                    sp.dma_start(dst[:], src.partition_broadcast(P).rearrange("p a n -> p (a n)")).then_inc(loaded, 16)
                sp.wait_ge(cleared, 1)
                with nc.allow_non_contiguous_dma(reason="4x4 corners of w_s, transposed"):
                    for b in range(DEC_B):
                        at = slice(b * DEC_S, (b + 1) * DEC_S)
                        for grp in range(NGRP):
                            sp.dma_start(ws_new[at, grp, at],
                                         io["w_s"][0, grp, 0:DEC_S, 0:DEC_S].rearrange("t s -> s t")).then_inc(new_in, 16)
                sp.wait_ge(q_scaled, 1)
                sp.dma_start(g.q_rows, g.z[0:NS, 0, 0, PT, :]).then_inc(out, 16)
                sp.wait_ge(normed, NT)
                sp.dma_start(io["new_gmlp_v_sample"][0].rearrange("b s n -> (b s) n"), gv[0:NS, PT, :]).then_inc(out, 16)
                sp.wait_ge(out, 32)

            @block.gpsimd
            def _(pool):
                nc.gpsimd.memset(ws_new[:], 0.0).then_inc(cleared, 1)
                nc.gpsimd.affine_select(out=upto[:], in_=g.ones[:, 0:P], compare_op=ALU.is_ge, fill=0.0, base=0,
                                        pattern=[[1, P]], channel_multiplier=-1).then_inc(masked, 1)
                nc.gpsimd.memset(mv[:], 1.0).then_inc(masked, 1)
                nc.gpsimd.memset(eps[:], EPS).then_inc(masked, 1)
                nc.gpsimd.memset(f_one[:], 1.0).then_inc(masked, 1)
                nc.gpsimd.tensor_scalar(g.z[0:NS, 0, 0, PT, :], g.z[0:NS, 0, 0, PT, :], HD ** -0.5, None, ALU.mult)\
                    .then_inc(q_scaled, 1)
                nc.gpsimd.tensor_scalar(g.z[:, 0, 0, 0:PT, :], g.z[:, 0, 0, 0:PT, :], HD ** -0.5, None, ALU.mult)
                pool.wait_ge(fT_copied, 4)
                with nc.allow_non_contiguous_dma(reason="eight columns"):
                    pool.dma_start(io["new_logf_prompt"][0, 0].rearrange("(t p) n -> p t n", p=P), logf[:, 0:PT, :])\
                        .then_inc(f_out, 16)
                    pool.dma_start(io["new_logf_sample"][0].rearrange("b s h -> (b s) h"), logf[0:NS, PT, :])\
                        .then_inc(f_out, 16)
                pool.wait_ge(f_out, 32)

            @block.scalar
            def _(act):
                for t in range(NT):
                    at = gv[0:TILE_ROWS[t], t, :]
                    nc.scalar.activation(at, at, ACT.Gelu_apprx_tanh).then_inc(gelu, 1)
                act.wait_ge(f_abs, 1)
                nc.scalar.activation(f_e[:], f_l[:], ACT.Exp, scale=-1.0).then_inc(f_exp, 1)
                act.wait_ge(have_var, 1)
                nc.scalar.activation(rstd[:], mv[:, :, 1], ACT.Sqrt, bias=eps[:, 0:1]).then_inc(have_std, 1)
                act.wait_ge(f_abs, 2)
                nc.scalar.activation(f_l[:], f_u[:], ACT.Ln).then_inc(f_log, 1)
                for n in range(3 * NGRP):
                    i, j, b = n % NGRP, n // NGRP, n % UB
                    act.wait_ge(u_full[b], n // UB + 1)
                    nc.scalar.activation(g.uT[:, i, j * BLK:(j + 1) * BLK], ps[:, b, 0:BLK], ACT.Gelu_apprx_tanh)\
                        .then_inc(u_done[b], 1)

            @block.tensor
            def _(pe):
                pe.wait_ge(f_in, 32)
                for k in range(KD):
                    for j in range(3):
                        last = nc.tensor.matmul(ps[32 * j:32 * j + H, 6, 0:BLK], w_f[:, k, :],
                                                g.hT[:, k, j * BLK:(j + 1) * BLK], start=(k == 0), stop=(k == KD - 1))
                last.then_inc(f_full, 1)
                pe.wait_ge(loaded, 64)
                for i in range(NGRP):
                    last = nc.tensor.transpose(ps[:, 7, i * P:(i + 1) * P], ws[:, i, :], g.ident[:])
                last.then_inc(wsT_done, 1)

                def product_u(j):
                    for i in range(NGRP):
                        n = NGRP * j + i
                        b = n % UB
                        pe.wait_ge(u_done[b], n // UB)
                        for k in range(KD):
                            last = nc.tensor.matmul(ps[:, b, 0:BLK], w_u[:, k, i * P:i * P + P],
                                                    g.hT[:, k, j * BLK:(j + 1) * BLK], start=(k == 0), stop=(k == KD - 1))
                        last.then_inc(u_full[b], 1)

                def product_gv(t):
                    rows, b = TILE_ROWS[t], t % 2
                    pe.wait_ge(normed, t + 1)
                    pe.wait_ge(sp_free[b], t // 2)
                    for i in range(NGRP):
                        last = nc.tensor.matmul(ps[:, 4 + b, i * rows:(i + 1) * rows], gv[0:rows, t, i * P:(i + 1) * P],
                                                wsT[:, i, :] if t < PT else ws_new[:, i, :], start=True, stop=True)
                    last.then_inc(sp_full[b], 1)

                pe.wait_ge(u_in, 16)
                product_u(0)
                product_u(1)
                pe.wait_ge(wsT_ready, 2)
                early = 2 * BLK // P
                for t in range(early):
                    product_gv(t)
                product_u(2)
                for t in range(early, NT):
                    product_gv(t)
                pe.wait_ge(f_cum, 1)
                for r, src in enumerate((logfT, ncumT)):
                    for t in range(NT):
                        rows = TILE_ROWS[t]
                        last = nc.tensor.transpose(ps[0:rows, 7, (r * NT + t) * H:(r * NT + t + 1) * H],
                                                   src[:, t * P:t * P + rows], g.ident[0:H, 0:H])
                last.then_inc(fT_done, 1)

            @block.vector
            def _(dve):
                link = Chain(dve, own)
                v = nc.vector
                dve.wait_ge(f_full, 1)
                dve.wait_ge(f_in, 32)
                for j in range(3):
                    last = v.tensor_scalar(f_x[:, j * BLK:(j + 1) * BLK], ps[32 * j:32 * j + H, 6, 0:BLK],
                                           bf[:, 0:1], None, ALU.add)
                link(last)
                v.scalar_tensor_tensor(out=f_l[:], in0=f_x[:], scalar=-1.0, in1=f_x[:], op0=ALU.mult,
                                       op1=ALU.max).then_inc(f_abs, 1)
                dve.wait_ge(masked, 4)
                for t in range(NT):
                    rows = TILE_ROWS[t]
                    dve.wait_ge(gelu, t + 1)
                    link(v.bn_stats(stats[0:rows, t, :], gv[0:rows, t, :]))
                for t in range(NT):
                    rows = TILE_ROWS[t]
                    last = v.bn_aggr(mv[0:rows, t, :], stats[0:rows, t, :])
                    if t < NT - 1:
                        link(last)
                last.then_inc(have_var, 1)
                dve.wait_ge(f_exp, 1)
                link(v.tensor_scalar(f_u[:], f_e[:], 1.0, None, ALU.add))
                v.scalar_tensor_tensor(out=f_e[:], in0=f_u[:], scalar=-1.0, in1=f_e[:], op0=ALU.add,
                                       op1=ALU.subtract).then_inc(f_abs, 1)
                dve.wait_ge(wsT_done, 1)
                v.tensor_tensor(wsT[:], ps[:, 7, :].rearrange("p (g t) -> p g t", g=NGRP),
                                upto[:].unsqueeze(1).to_broadcast([P, NGRP, P]), ALU.mult).then_inc(wsT_ready, 1)
                dve.wait_ge(have_std, 1)
                link(v.reciprocal(rstd[:], rstd[:]))
                dve.wait_ge(loaded, 64)
                for t in range(NT):
                    rows = TILE_ROWS[t]
                    at = gv[0:rows, t, :]
                    link(v.scalar_tensor_tensor(out=at, in0=at, scalar=mv[0:rows, t, 0:1], in1=ln_g[0:rows, :],
                                                op0=ALU.subtract, op1=ALU.mult))
                    v.scalar_tensor_tensor(out=at, in0=at, scalar=rstd[0:rows, t:t + 1], in1=ln_b[0:rows, :],
                                           op0=ALU.mult, op1=ALU.add).then_inc(normed, 1)
                dve.wait_ge(new_in, 16 * DEC_B * NGRP)
                v.tensor_tensor(ws_new[:], ws_new[:], upto[0:NS, 0:NS].unsqueeze(1)
                                .to_broadcast([NS, NGRP, NS]), ALU.mult).then_inc(wsT_ready, 1)
                dve.wait_ge(f_log, 1)
                dve.wait_ge(f_abs, 2)
                link(v.reciprocal(f_u[:], f_u[:]))
                link(v.tensor_tensor(f_e[:], f_e[:], f_u[:], ALU.mult))
                link(v.tensor_tensor(f_l[:], f_e[:], f_l[:], ALU.subtract))
                link(v.scalar_tensor_tensor(out=logfT[:], in0=f_x[:], scalar=0.0, in1=f_l[:], op0=ALU.min, op1=ALU.add))
                link(v.tensor_scalar(f_x[:], logfT[:], -1.0, None, ALU.mult))
                link(v.tensor_tensor_scan(ncumT[:, 0:SEQ], f_one[:], f_x[:, 0:SEQ], 0.0, ALU.mult, ALU.add))
                cs = ncumT[:, SEQ:T].rearrange("h (b s) -> h b s", s=DEC_S)
                xs = f_x[:, SEQ:T].rearrange("h (b s) -> h b s", s=DEC_S)
                link(v.tensor_copy(cs[:, :, 0], xs[:, :, 0]))
                for s in range(1, DEC_S):
                    last = v.tensor_tensor(cs[:, :, s], cs[:, :, s - 1], xs[:, :, s], ALU.add)
                    if s < DEC_S - 1:
                        link(last)
                last.then_inc(f_cum, 1)
                dve.wait_ge(f_cum, 1)
                v.tensor_copy(g.ncum_new[:], ncumT[:, SEQ:T])
                for t in range(NT):
                    b = t % 2
                    for i in range(UB):
                        dve.wait_ge(u_done[i], (t * P + TILE_ROWS[t] - 1) // BLK + 1)
                    dve.wait_ge(sp_full[b], t // 2 + 1)
                    if t < PT:
                        u = g.uT[:, :, t * P:(t + 1) * P]
                        spt = sp_b[b][:]
                        v.tensor_tensor(spt, ps[:, 4 + b, :].rearrange("p (g t) -> p g t", g=NGRP), bs[:],
                                        ALU.add).then_inc(sp_free[b], 1)
                    else:
                        u = g.uT[:, :, SEQ:T]
                        spt = sp_b[b][:, :, 0:NS]
                        v.tensor_tensor(spt.rearrange("p g (b s) -> p g b s", s=DEC_S),
                                        ps[:, 4 + b, 0:NGRP * NS].rearrange("p (g b s) -> p g b s", g=NGRP, s=DEC_S),
                                        bs[:, :, 0:DEC_S].unsqueeze(2).to_broadcast([P, NGRP, DEC_B, DEC_S]),
                                        ALU.add).then_inc(sp_free[b], 1)
                    dve.wait_ge(sp_free[b], t // 2 + 1)
                    link(v.tensor_tensor(u, spt, u, ALU.mult))
                dve.wait_ge(fT_done, 1)
                for r, dst in enumerate((logf, g.ncum)):
                    v.tensor_copy(dst[:, 0:PT, :], ps[:, 7, r * NT * H:(r * NT + PT) * H]
                                  .rearrange("p (t h) -> p t h", h=H)).then_inc(fT_copied, 1)
                    v.tensor_copy(dst[0:NS, PT, :], ps[0:NS, 7, (r * NT + PT) * H:(r + 1) * NT * H])\
                        .then_inc(fT_copied, 1)


def attend_prompt(nc, io, g, ps):
    HA = HD + 2
    LAG, NPB = 3, 4
    UNITS = 2 * PT
    QB = 4

    groups, upto = [], {}
    for hh in range(2):
        for which in range(2):
            for half in range(2):
                groups.append(("qk", hh, which, half))
    for u in range(UNITS):
        i = u // 2
        for kb in range(0, i + 1, 4):
            groups.append(("p", u, kb, min(4, i + 1 - kb)))
        upto[u] = len(groups)
    USES = len(groups) // 2
    assert len(groups) % 2 == 0

    with ExitStack() as ctx:
        m = Mem(nc, ctx, "pat")
        qa, ka = m.sb("qa", [P, PT, 2, HA]), m.sb("ka", [P, PT, 2, HA])
        va = m.sb("va", [P, PT, 2 * HD])
        qkT = m.sb("qkT", [HA, 2, 2, SEQ])
        pr = [m.sb(f"pr{i}", [P, SEQ]) for i in range(NPB)]
        prT = [m.sb("prT", [P, PT, QB * P]), g.z[:, 1, 1, 0:PT, :]]
        nmax, rsum = m.sb("nmax", [P, NPB]), m.sb("rsum", [P, NPB])
        cum = m.sb("cum", [P, PT, H])
        one_set, cum_set = m.sem("one_set"), m.sem("cum_set")
        qk_staged, v_staged = m.sem("qk_staged"), m.sem("v_staged")
        t_full, t_free = m.sems("t_full", 2), m.sems("t_free", 2)
        s_full, masked, have_max = m.sems("s_full", 2), m.sem("masked"), m.sem("have_max")
        exped = m.sems("exped", NPB)
        have_recip, scaled = m.sem("have_recip"), m.sems("scaled", NPB)
        pv_done, pv_free = m.sems("pv_done", 2), m.sems("pv_free", 2)
        seen = m.sem("seen")
        PER_BUF = UNITS // NPB

        def t_count(it, n):
            return [it * USES + (n + 1) // 2, it * USES + n // 2]

        m.start(t_full + pv_done + t_free + exped + pv_free)

        with nc.Block() as block:
            @block.gpsimd
            def _(pool):
                nc.gpsimd.memset(qa[:, :, :, HD:HD + 1], 1.0).then_inc(one_set, 1)
                nc.gpsimd.memset(ka[:, :, :, HD + 1:HA], 1.0).then_inc(one_set, 1)
                nc.gpsimd.tensor_scalar(cum[:], g.ncum[:, 0:PT, :], -1.0, None, ALU.mult).then_inc(cum_set, 1)
                pool.wait_ge(cum_set, 1)
                heads = "p t (h d) -> p t h d"

                def stage_qk(it):
                    for dst, at in ((qa, 0), (ka, 1)):
                        nc.gpsimd.tensor_copy(dst[:, :, :, 0:HD], g.z[:, 0, at, 0:PT, bass.ds(it * 2 * HD, 2 * HD)]
                                              .rearrange(heads, h=2)).then_inc(qk_staged, 1)
                    nc.gpsimd.tensor_copy(ka[:, :, :, HD], g.ncum[:, 0:PT, bass.ds(2 * it, 2)]).then_inc(qk_staged, 1)
                    nc.gpsimd.tensor_copy(qa[:, :, :, HD + 1], cum[:, :, bass.ds(2 * it, 2)]).then_inc(qk_staged, 1)

                def stage_v(it):
                    nc.gpsimd.tensor_copy(va[:], g.z[:, 1, 0, 0:PT, bass.ds(it * 2 * HD, 2 * HD)]).then_inc(v_staged, 1)

                stage_qk(0)
                stage_v(0)
                with pool.Fori(0, H // 2 - 1) as it:
                    for b in range(2):
                        pool.wait_ge(t_full[b], START + it * USES + 4)
                    pool.sem_inc(seen, 1)
                    stage_qk(it + 1)
                    pool.wait_ge(pv_done[1], START + it + 1)
                    pool.sem_inc(seen, 1)
                    stage_v(it + 1)

            @block.tensor
            def _(pe):
                pe.wait_ge(one_set, 2)

                def group(it, n):
                    b, use = n % 2, n // 2
                    pe.wait_ge(t_free[b], START + it * USES + use)
                    what, *at = groups[n]
                    if what == "qk":
                        hh, which, half = at
                        for i in range(4):
                            last = nc.tensor.transpose(ps[0:HA, 4 + b, i * P:(i + 1) * P],
                                                       (qa, ka)[which][:, 4 * half + i, hh, :], g.ident[:])
                    else:
                        u, kb, n_kb = at
                        for i in range(n_kb):
                            last = nc.tensor.transpose(ps[:, 4 + b, i * P:(i + 1) * P],
                                                       pr[u % NPB][:, (kb + i) * P:(kb + i + 1) * P], g.ident[:])
                    last.then_inc(t_full[b], 1)

                def scores(it, u):
                    i, hh = u // 2, u % 2
                    if u >= 2:
                        pe.wait_ge(exped[(u - 2) % NPB], START + it * PER_BUF + (u - 2) // NPB + 1)
                    else:
                        pe.wait_ge(exped[(u - 2) % NPB], START + it * PER_BUF)
                    for at in range(0, (i + 1) * P, 512):
                        n = min(512, (i + 1) * P - at)
                        last = nc.tensor.matmul(ps[:, 2 * (u % 2) + at // 512, 0:n], qkT[:, hh, 0, i * P:(i + 1) * P],
                                                qkT[:, hh, 1, at:at + n], start=True, stop=True)
                    last.then_inc(s_full[u % 2], 1)

                def values(it, qb, between=None):
                    for b, count in enumerate(t_count(it, upto[2 * QB * (qb + 1) - 1])):
                        pe.wait_ge(t_free[b], START + count)
                    pe.wait_ge(v_staged, it + 1)
                    pe.wait_ge(pv_free[qb], START + it)
                    for kb in range(QB * (qb + 1)):
                        q0 = max(0, kb - QB * qb) * P
                        for hh in range(2):
                            last = nc.tensor.matmul(ps[hh * HD:(hh + 1) * HD, 6 + qb, q0:QB * P],
                                                    va[:, kb, hh * HD:(hh + 1) * HD], prT[hh][:, kb, q0:QB * P],
                                                    start=(kb == 0), stop=(kb == QB * (qb + 1) - 1))
                        if kb == QB * (qb + 1) - 1:
                            last.then_inc(pv_done[qb], 1)
                        if between:
                            between(kb)

                def step(it, final):
                    for b, count in enumerate(t_count(it, 8)):
                        pe.wait_ge(t_free[b], START + count)
                    issued = 0
                    for n in range(UNITS + LAG):
                        if issued <= n < UNITS:
                            scores(it, n)
                            issued = n + 1
                        u = n - LAG
                        if u >= 0:
                            pe.wait_ge(scaled[u % NPB], it * PER_BUF + u // NPB + 1)
                            for k in range(upto[u - 1] if u else 8, upto[u]):
                                group(it, k)
                        if u == 2 * QB - 1:
                            for ahead in (n + 1, n + 2):
                                scores(it, ahead)
                            issued = n + 3
                            values(it, 0)
                    if final:
                        values(it, 1)
                    else:
                        pe.wait_ge(qk_staged, 4 * it + 8)
                        values(it, 1, lambda kb: group(it + 1, kb))

                pe.wait_ge(qk_staged, 4)
                for n in range(8):
                    group(0, n)
                with pe.Fori(0, H // 2 - 1) as it:
                    step(it, False)
                step(H // 2 - 1, True)

            def copy_group(eng, copy, it, n):
                b, use = n % 2, n // 2
                eng.wait_ge(t_full[b], START + it * USES + use + 1)
                what, *at = groups[n]
                if what == "qk":
                    hh, which, half = at
                    ins = copy(qkT[:, hh, which, half * 512:(half + 1) * 512], ps[0:HA, 4 + b, :])
                else:
                    u, kb, n_kb = at
                    i, hh = u // 2, u % 2
                    if i < QB:
                        eng.wait_ge(pv_done[1], START + it)
                    else:
                        eng.wait_ge(pv_done[0], START + it + 1)
                    ins = copy(prT[hh][:, kb:kb + n_kb, (i % QB) * P:(i % QB + 1) * P],
                               ps[:, 4 + b, 0:n_kb * P].rearrange("p (k q) -> p k q", q=P))
                ins.then_inc(t_free[b], 1)

            def copy_values(eng, copy, it, qb):
                eng.wait_ge(pv_done[qb], START + it + 1)
                copy(g.aT[:, bass.ds(it, 1), qb * 512:(qb + 1) * 512].rearrange("p a n -> p (a n)"), ps[:, 6 + qb, :])\
                    .then_inc(pv_free[qb], 1)

            @block.vector
            def _(dve):
                def row_max(it, u):
                    i, sb = u // 2, u % 2
                    keys = (i + 1) * P
                    dve.wait_ge(s_full[sb], it * (UNITS // 2) + u // 2 + 1)
                    diag = ps[:, 2 * sb + i // 4, (i % 4) * P:(i % 4 + 1) * P]
                    nc.vector.tensor_tensor(diag, diag, g.causal[:], ALU.add).then_inc(masked, 1)
                    dve.wait_ge(masked, it * UNITS + u + 1)
                    nc.vector.tensor_reduce(nmax[:, u % NPB:u % NPB + 1],
                                            ps[:, 2 * sb:2 * sb + 2, :].rearrange("p b n -> p (b n)")[:, 0:keys],
                                            AX.X, ALU.max, negate=True).then_inc(have_max, 1)

                def scale(it, u):
                    k, keys = u % NPB, (u // 2 + 1) * P
                    dve.wait_ge(exped[k], START + it * PER_BUF + u // NPB + 1)
                    nc.vector.reciprocal(rsum[:, k:k + 1], rsum[:, k:k + 1]).then_inc(have_recip, 1)
                    dve.wait_ge(have_recip, it * UNITS + u + 1)
                    nc.vector.tensor_scalar(pr[k][:, 0:keys], pr[k][:, 0:keys], rsum[:, k:k + 1], None, ALU.mult)\
                        .then_inc(scaled[k], 1)

                def step(it, final):
                    for n in range(UNITS + 1):
                        if n < UNITS:
                            row_max(it, n)
                        if n:
                            scale(it, n - 1)
                        if n == LAG + 2 * QB + 2:
                            copy_values(dve, nc.vector.tensor_copy, it, 0)
                    if not final:
                        for n in range(0, 8, 2):
                            copy_group(dve, nc.vector.tensor_copy, it + 1, n)

                for n in range(0, 8, 2):
                    copy_group(dve, nc.vector.tensor_copy, 0, n)
                with dve.Fori(0, H // 2 - 1) as it:
                    step(it, False)
                step(H // 2 - 1, True)

            @block.scalar
            def _(act):
                def exps(it, u):
                    k, keys = u % NPB, (u // 2 + 1) * P
                    act.wait_ge(have_max, it * UNITS + u + 1)
                    for b, count in enumerate(t_count(it, upto[u - NPB] if u >= NPB else 0)):
                        act.wait_ge(t_full[b], START + count)
                    nc.scalar.activation(pr[k][:, 0:keys],
                                         ps[:, 2 * (u % 2):2 * (u % 2) + 2, :].rearrange("p b n -> p (b n)")[:, 0:keys],
                                         ACT.Exp, bias=nmax[:, k:k + 1], accum_out=rsum[:, k:k + 1])\
                        .then_inc(exped[k], 1)

                def step(it, final):
                    for n in range(UNITS + LAG):
                        if n < UNITS:
                            exps(it, n)
                        u = n - LAG
                        if u >= 0:
                            for k in range(upto[u - 1] if u else 8, upto[u]):
                                copy_group(act, nc.scalar.copy, it, k)
                    if not final:
                        for n in range(1, 8, 2):
                            copy_group(act, nc.scalar.copy, it + 1, n)
                    copy_values(act, nc.scalar.copy, it, 1)

                nc.scalar.preload_act_table(ACT.Exp)
                for n in range(1, 8, 2):
                    copy_group(act, nc.scalar.copy, 0, n)
                with act.Fori(0, H // 2 - 1) as it:
                    step(it, False)
                step(H // 2 - 1, True)




def attend_sample(nc, io, g, ps):
    UP, QUADS = 16, 4
    R = H * DEC_S
    KC = DA // P
    UNITS = 2 * DEC_B
    KS = UP

    with ExitStack() as ctx:
        m = Mem(nc, ctx, "sat")
        table_in_order, table = (m.sb(n, [1, DEC_B * PAGES], I32) for n in ("table_in_order", "table"))
        page_rows = m.sb("page_rows", [P, 2], I32)
        lfT = m.sb("lfT", [P, H, DEC_B * PAGES])
        quad_sum, later = m.sb("quad_sum", [P, H, 2 * UNITS * 2]), m.sb("later", [P, H, 2 * UNITS * 2])
        qT, kT_new = m.sb("qT", [P, KC, NS]), m.sb("kT_new", [P, KC, NS])
        q_diag = m.sb("q_diag", [P, KC, DEC_B, R])
        q_now = m.sb("q_now", [P, 2, KC, R])
        lf_now, later_now = m.sb("lf_now", [P, 2, UP, R]), m.sb("later_now", [P, 2, QUADS, R])
        k_pg, v_pg = m.sb("k_pg", [P, KS, DA]), m.sb("v_pg", [P, UP, DA])
        kT = m.sb("kT", [P, 2, KC, QUADS * P])
        lf_pages = kT[:, 0].rearrange("p c n -> p (c n)").rearrange("p (a n) -> p a n", a=2)
        pr, prT = m.sb("pr", [P, 2, 512]), m.sb("prT", [P, 512])
        nmax, rsum = m.sb("nmax", [P, 2]), m.sb("rsum", [P, 2])
        nmax_all, rsum_all = m.sb("nmax_all", [P, UNITS]), m.sb("rsum_all", [P, UNITS])
        own_head = m.sb("own_head", [P, H, HD])
        o_all = m.sb("o_all", [P, 512])
        o_head = m.sb("o_head", [P, UNITS, HD])
        row, row_mod = m.sb("row", [P, 1], I32), m.sb("row_mod", [P, 1], I32)
        own_seq = m.sb("own_seq", [R, DEC_B, NS])
        row_h = m.sb("row_h", [P, 1])
        row_q, key_q = m.sb("row_q", [R, 1]), m.sb("key_q", [R, DEC_B, NS])
        head_row = m.sb("head_row", [H, R])
        fold = m.sb("fold", [P, R])
        s_new, rsum_new, nmax_new = m.sb("s_new", [R, DEC_B, NS]), m.sb("rsum_new", [R, DEC_B]), m.sb("nmax_new", [R, DEC_B])
        p_newT = m.sb("p_newT", [NS, DEC_B * R])
        q_new, k_new, v_new = (m.sb(n, [NS, DA]) for n in ("q_new", "k_new", "v_new"))
        new_in = m.sem("new_in")
        parts_m, parts_l = m.sb("parts_m", [DEC_B, 9, R]), m.sb("parts_l", [DEC_B, 9, R])
        parts_w = m.sb("parts_w", [DEC_B, 9, R])
        top, total = m.sb("top", [DEC_B, R]), m.sb("total", [DEC_B, R])
        share, share_new = m.sb("share", [P, DEC_B, 2]), m.sb("share_new", [R, DEC_B])
        o_new = m.sb("o_new", [P, 2, HD])

        table_ready = m.sem("table_ready")
        table_in, rows_in, lf_in = m.sem("table_in"), m.sem("rows_in"), m.sems("lf_in", 2)
        pool_own, own = m.sem("pool_own"), m.sem("own")
        lfT_done, lfT_copied = m.sems("lfT_done", 4), m.sem("lfT_copied")
        qk_done, qk_copied, diag_ready = m.sem("qk_done"), m.sem("qk_copied"), m.sem("diag_ready")
        later_ready, consts = m.sem("later_ready"), m.sem("consts")
        staged = m.sems("staged", 2)
        k_in, v_in = m.sems("k_in", 4), m.sems("v_in", 4)
        t_full = [m.sems(f"t_full{e}", 4) for e in range(2)]
        t_copied, kT_used = m.sems("t_copied", 4), m.sems("kT_used", 2)
        s_done, have_max, exped = m.sems("s_done", 2), m.sems("have_max", 2), m.sems("exped", 2)
        prT_done, prT_copied = m.sems("prT_done", 2), m.sems("prT_copied", 2)
        pv_done, o_read, o_masked = m.sems("pv_done", 4), m.sems("o_read", 2), m.sems("o_masked", 2)
        kept, seen = m.sems("kept", 2), m.sem("seen")
        c_pe, c_dve, c_act, shifted = m.sem("c_pe"), m.sem("c_dve"), m.sem("c_act"), m.sem("shifted")

        k_pool = io["cache_k"][0].rearrange("n p h d -> n p (h d)")
        v_pool = io["cache_v"][0].rearrange("n p h d -> n p (h d)")
        n_pool = io["cache_k"].shape[1]

        m.start(t_full[0] + t_full[1] + t_copied + kT_used + s_done + exped + prT_done + pv_done + o_read + kept)

        def pipeline(eng, unit):
            unit(0, 0, None)
            with eng.Fori(0, DEC_B - 1) as b:
                unit(b, 1, (b, 0))
                unit(b + 1, 0, (b, 1))
            unit(DEC_B - 1, 1, (DEC_B - 1, 0))

        with nc.Block() as block:
            @block.sync
            def _(sp):
                sp.dma_start(table_in_order[:], io["page_table"].rearrange("b n -> (b n)").rearrange("(a n) -> a n", a=1))\
                    .then_inc(table_in, 16)
                sp.dma_start(q_new[:], g.q_rows).then_inc(new_in, 16)
                for dst, src in ((k_new, io["new_k_sample"]), (v_new, io["new_v_sample"])):
                    sp.dma_start(dst[:], src[0].rearrange("b s h d -> (b s) (h d)")).then_inc(new_in, 16)
                sp.wait_ge(table_ready, 1)
                def page_numbers(b, half, pp):
                    return nc.values_load_multi_w_load_instructions(
                        table[0:1, bass.ds((2 * b + half) * UP + 4 * pp, 8)], engines=(mybir.EngineType.SP,), min_val=0,
                        max_val=n_pool - 1,
                        skip_runtime_bounds_check_because="the table names pages of the pool")[1]

                def load(dst, src, pages, arrived, pp):
                    for j in range(QUADS):
                        sp.dma_start(dst[:, 4 * pp + j, :], src[bass.ds(pages[j], 1)].rearrange("a p n -> (a p) n"))\
                            .then_inc(arrived[pp], 16)

                def keys(b, half, first):
                    pages = page_numbers(b, half, first)
                    for pp in (first, first + 1):
                        for e in range(2):
                            sp.wait_ge(t_full[e][pp], START + 2 * (2 * b + half))
                        load(k_pg, k_pool, pages[4 * (pp - first):], k_in, pp)

                def values(b, half, first):
                    pages = page_numbers(b, half, first)
                    for pp in (first, first + 1):
                        sp.wait_ge(pv_done[pp], START + 2 * b + half)
                        load(v_pg, v_pool, pages[4 * (pp - first):], v_in, pp)

                def unit(b, half, before):
                    for first in (0, 2):
                        keys(b, half, first)
                        if before:
                            values(*before, first)

                pipeline(sp, unit)
                for first in (0, 2):
                    values(DEC_B - 1, 1, first)

            @block.gpsimd
            def _(pool):
                link = Chain(pool, pool_own)
                with nc.allow_non_contiguous_dma(reason="a page's number a partition"):
                    pool.dma_start(page_rows[:], io["page_table"].rearrange("b n -> (b n)").rearrange("(a p) -> p a", p=P))\
                        .then_inc(rows_in, 16)
                pool.wait_ge(table_in, 16)
                nc.gpsimd.tensor_copy(table[:].rearrange("a (u q j) -> a u q j", q=4, j=QUADS),
                                      table_in_order[:].rearrange("a (u j q) -> a u q j", q=4, j=QUADS)).then_inc(table_ready, 1)
                pool.wait_ge(rows_in, 16)
                for a in range(2):
                    pool.indirect_dma_start(lf_pages[:, a, :], None, io["cache_logf"][0].rearrange("n p h -> n (p h)"),
                                            bass.IndirectOffsetOnAxis(page_rows[:, a:a + 1], 0)).then_inc(lf_in[a], 16)
                nc.gpsimd.iota(row[:], pattern=[[0, 1]], base=0, channel_multiplier=1).then_inc(consts, 1)
                nc.gpsimd.iota(own_head[:], pattern=[[1, H], [0, HD]], base=0, channel_multiplier=0,
                               allow_small_or_imprecise_dtypes=True).then_inc(consts, 1)
                nc.gpsimd.iota(key_q[:], pattern=[[0, DEC_B * DEC_B], [1, DEC_S]], base=0, channel_multiplier=0,
                               allow_small_or_imprecise_dtypes=True).then_inc(consts, 1)
                link(nc.gpsimd.affine_select(out=head_row[:], in_=g.ones[0:H, 0:R], compare_op=ALU.is_ge, fill=0.0,
                                             base=0, pattern=[[1, R]], channel_multiplier=-DEC_S))
                nc.gpsimd.affine_select(out=head_row[:], in_=head_row[:], compare_op=ALU.is_ge, fill=0.0,
                                        base=DEC_S - 1, pattern=[[-1, R]], channel_multiplier=DEC_S).then_inc(consts, 1)
                link(nc.gpsimd.memset(own_seq[:], 0.0))
                link(nc.gpsimd.affine_select(out=own_seq[:], in_=own_seq[:], compare_op=ALU.is_ge, fill=NEG, base=0,
                                             pattern=[[-DEC_S, DEC_B], [1, NS]], channel_multiplier=0))
                nc.gpsimd.affine_select(out=own_seq[:], in_=own_seq[:], compare_op=ALU.is_ge, fill=NEG, base=DEC_S - 1,
                                        pattern=[[DEC_S, DEC_B], [-1, NS]], channel_multiplier=0).then_inc(consts, 1)
                nc.gpsimd.memset(q_diag[:], 0.0).then_inc(consts, 1)
                nc.gpsimd.memset(later[:], 0.0).then_inc(consts, 1)
                pool.wait_ge(diag_ready, 2 * KC)
                pool.wait_ge(later_ready, 1)
                pool.wait_ge(lfT_copied, 4)
                rep = [P, UP, H, DEC_S]

                def stage(b, half):
                    pool.wait_ge(s_done[half], START + b)
                    pool.sem_inc(seen, 1)
                    nc.gpsimd.tensor_copy(q_now[:, half], q_diag[:, :, bass.ds(b, 1), :].rearrange("p c a r -> p c (a r)"))\
                        .then_inc(staged[half], 1)
                    for q in range(DEC_S):
                        nc.gpsimd.tensor_copy(
                            lf_now[:, half].rearrange("p n (h q) -> p n h q", q=DEC_S)[:, :, :, q],
                            lfT[:, :, bass.ds(b * PAGES + half * UP, UP)].rearrange("p h n -> p n h"))\
                            .then_inc(staged[half], 1)
                        nc.gpsimd.tensor_copy(
                            later_now[:, half].rearrange("p n (h q) -> p n h q", q=DEC_S)[:, :, :, q],
                            later[:, :, bass.ds(8 * b + 4 * half, 4)].rearrange("p h n -> p n h"))\
                            .then_inc(staged[half], 1)

                def keep(b, half):
                    pool.wait_ge(exped[half], START + b + 1)
                    pool.sem_inc(seen, 1)
                    for dst, src in ((nmax_all, nmax), (rsum_all, rsum)):
                        nc.gpsimd.tensor_copy(dst[:, bass.ds(2 * b + half, 1)], src[:, half:half + 1]).then_inc(kept[half], 1)

                for half in range(2):
                    stage(0, half)
                with pool.Fori(0, DEC_B - 1) as b:
                    for half in range(2):
                        keep(b, half)
                        stage(b + 1, half)
                for half in range(2):
                    keep(DEC_B - 1, half)

            def copy_keys(eng, copy, e, b, half, pp):
                u = 2 * b + half
                eng.wait_ge(kT_used[pp % 2], START + 2 * u + pp // 2)
                for j in range(e, QUADS, 2):
                    eng.wait_ge(t_full[e][pp], START + 2 * u + j // 2 + 1)
                    copy(kT[:, pp % 2, :, j * P:(j + 1) * P], ps[:, j, :].rearrange("p (c k) -> p c k", c=KC))\
                        .then_inc(t_copied[j], 1)

            @block.tensor
            def _(pe):
                pe.wait_ge(new_in, 48)
                for which, src in enumerate((q_new, k_new)):
                    for c in range(KC):
                        last = nc.tensor.transpose(ps[:, 7, (which * KC + c) * NS:(which * KC + c + 1) * NS],
                                                   src[:, c * P:(c + 1) * P], g.ident[0:NS, 0:NS])
                last.then_inc(qk_done, 1)
                for a in range(2):
                    pe.wait_ge(lf_in[a], 16)
                    for h0 in range(0, H, 4):
                        b = 2 * a + h0 // 4
                        for h in range(h0, h0 + 4):
                            last = nc.tensor.transpose(ps[:, b, (h - h0) * P:(h - h0 + 1) * P],
                                                       lf_pages[:, a, :].rearrange("n (k h) -> n k h", h=H)[:, :, h],
                                                       g.ident[:])
                        last.then_inc(lfT_done[b], 1)
                pe.wait_ge(lfT_copied, 4)
                quads = [(j, slice(R * j, R * j + R)) for j in range(QUADS)]

                def transposes(b, half, pp):
                    u = 2 * b + half
                    pe.wait_ge(k_in[pp], 64 * u + 64)
                    for j in range(QUADS):
                        pe.wait_ge(t_copied[j], START + 4 * u + pp)
                        for c in range(KC):
                            last = nc.tensor.transpose(ps[:, j, c * P:(c + 1) * P],
                                                       k_pg[:, 4 * pp + j, c * P:(c + 1) * P], g.ident[:])
                        last.then_inc(t_full[j % 2][pp], 1)

                def decays(b, half):
                    pe.wait_ge(staged[half], 9 * b + 9)
                    pe.wait_ge(exped[half], START + b)
                    for j, at in quads:
                        nc.tensor.matmul(ps[at, 4 + half, :], later_now[:, half, j, :], g.ones[:],
                                         start=True, stop=False, skip_group_check=True)
                    for pp in range(4):
                        for j, at in quads:
                            nc.tensor.matmul(ps[at, 4 + half, 0:(pp + 1) * P], lf_now[:, half, 4 * j + pp, :],
                                             g.after[:, (3 - pp) * P:4 * P], start=False, stop=False,
                                             skip_group_check=True)

                def scores(b, half, pp):
                    for j in range(QUADS):
                        pe.wait_ge(t_copied[j], START + 4 * (2 * b + half) + pp + 1)
                    for c in range(KC):
                        for j, at in quads:
                            last = nc.tensor.matmul(ps[at, 4 + half, pp * P:(pp + 1) * P], q_now[:, half, c, :],
                                                    kT[:, pp % 2, c, j * P:(j + 1) * P], start=False,
                                                    stop=(c == KC - 1), skip_group_check=True)
                            if c == KC - 1 and j == QUADS - 2 and pp == 3:
                                last.then_inc(s_done[half], 1)
                    last.then_inc(kT_used[pp % 2], 1)

                def turn(b, half):
                    pe.wait_ge(exped[half], START + b + 1)
                    for pp in range(4):
                        last = nc.tensor.transpose(ps[:, 7, pp * P:(pp + 1) * P], pr[:, half, pp * P:(pp + 1) * P],
                                                   g.ident[:])
                    last.then_inc(prT_done[half], 1)

                def values(b, half, pp):
                    if pp == 0:
                        pe.wait_ge(prT_copied[half], b + 1)
                        pe.wait_ge(o_read[1 - half], START + b + half)
                    pe.wait_ge(v_in[pp], 64 * (2 * b + half) + 64)
                    for j, at in quads:
                        last = nc.tensor.matmul(ps[at, 6, :], prT[:, pp * P + R * j:pp * P + R * j + R],
                                                v_pg[:, 4 * pp + j, :], start=(pp == 0), stop=(pp == 3))
                    last.then_inc(pv_done[pp], 1)

                def unit(b, half, before):
                    transposes(b, half, 0)
                    decays(b, half)
                    if before:
                        scores(*before, 3)
                    transposes(b, half, 1)
                    scores(b, half, 0)
                    if before:
                        turn(*before)
                    for pp in (2, 3):
                        transposes(b, half, pp)
                        scores(b, half, pp - 1)
                        if before:
                            values(*before, 2 * pp - 4)
                            values(*before, 2 * pp - 3)

                pipeline(pe, unit)
                final = (DEC_B - 1, 1)
                scores(*final, 3)
                turn(*final)
                for pp in range(4):
                    values(*final, pp)

                for half in range(2):
                    pe.wait_ge(o_read[half], START + DEC_B)
                pe.wait_ge(consts, 7)
                for b in range(DEC_B):
                    at = slice(b * NS, (b + 1) * NS)
                    for c in range(KC):
                        nc.tensor.matmul(ps[0:R, 0, at], q_diag[:, c, b, :], kT_new[:, c, :], start=(c == 0), stop=False,
                                         skip_group_check=True)
                    last = nc.tensor.matmul(ps[0:R, 0, at], head_row[:], g.ncum_new[:], start=False, stop=True,
                                            skip_group_check=True)
                last.then_inc(c_pe, 1)
                for half in range(2):
                    pe.wait_ge(kept[half], START + 2 * DEC_B)
                pe.wait_ge(c_dve, 1)
                for half in range(2):
                    for bank, src in ((1, nmax_all), (2, rsum_all)):
                        nc.tensor.transpose(ps[0:DEC_B, bank, half * P:(half + 1) * P],
                                            src[:].rearrange("p (b a) -> p b a", a=2)[:, :, half], g.ident[:])
                for bank, src in ((1, nmax_new), (2, rsum_new)):
                    last = nc.tensor.transpose(ps[0:DEC_B, bank, 2 * P:2 * P + R], src[:], g.ident[0:R, 0:R])
                last.then_inc(c_pe, 1)
                pe.wait_ge(c_dve, 2)
                flat = parts_w[:].rearrange("b n r -> b (n r)")
                for half in range(2):
                    nc.tensor.transpose(ps[:, 3, half * DEC_B:(half + 1) * DEC_B], flat[:, half * P:(half + 1) * P],
                                        g.ident[0:DEC_B, 0:DEC_B])
                nc.tensor.transpose(ps[0:R, 3, 2 * DEC_B:3 * DEC_B], flat[:, 2 * P:2 * P + R],
                                    g.ident[0:DEC_B, 0:DEC_B]).then_inc(c_pe, 1)
                pe.wait_ge(c_dve, 3)
                for b in range(DEC_B):
                    last = nc.tensor.transpose(ps[0:NS, 0, b * R:(b + 1) * R], s_new[:, b, :], g.ident[0:R, 0:R])
                last.then_inc(c_pe, 1)
                pe.wait_ge(c_dve, 4)
                for bh in range(2):
                    for j in range(4):
                        b = 4 * bh + j
                        last = nc.tensor.matmul(ps[R * j:R * j + R, 4 + bh, :], p_newT[:, b * R:(b + 1) * R], v_new[:],
                                                start=True, stop=True)
                last.then_inc(c_pe, 1)
                pe.wait_ge(c_dve, 5)
                for b in range(DEC_B):
                    at = slice(b * R, (b + 1) * R)
                    for half in range(2):
                        nc.tensor.matmul(ps[0:HD, 7, at], o_head[:, 2 * b + half, :], fold[:], start=(half == 0), stop=False,
                                         skip_group_check=True)
                    last = nc.tensor.matmul(ps[0:HD, 7, at], o_new[:, b // 4, :], g.ident[:, R * (b % 4):R * (b % 4) + R],
                                            start=False, stop=True, skip_group_check=True)
                last.then_inc(c_pe, 1)

            @block.vector
            def _(dve):
                link = Chain(dve, own)
                dve.wait_ge(qk_done, 1)
                qkv = ps[:, 7, 0:2 * KC * NS].rearrange("p (a c n) -> p a c n", a=2, c=KC)
                nc.vector.tensor_copy(qT[:], qkv[:, 0]).then_inc(qk_copied, 1)
                nc.vector.tensor_copy(kT_new[:], qkv[:, 1]).then_inc(qk_copied, 1)
                dve.wait_ge(qk_copied, 2)
                dve.wait_ge(consts, 7)
                for c in range(KC):
                    for hh in range(2):
                        at = slice(hh * HD, (hh + 1) * HD)
                        nc.vector.tensor_copy(
                            q_diag[at, c].rearrange("p b (h q) -> p b h q", q=DEC_S)[:, :, 2 * c + hh, :],
                            qT[at, c, :].rearrange("p (b q) -> p b q", q=DEC_S)).then_inc(diag_ready, 1)
                for b in range(4):
                    dve.wait_ge(lfT_done[b], 1)
                    nc.vector.tensor_copy(lfT[:, 4 * (b % 2):4 * (b % 2) + 4, (b // 2) * P:(b // 2 + 1) * P],
                                          ps[:, b, :].rearrange("p (h n) -> p h n", h=4)).then_inc(lfT_copied, 1)
                dve.wait_ge(lfT_copied, 4)
                link(nc.vector.tensor_reduce(quad_sum[:], lfT[:].rearrange("p h (c n) -> p h c n", n=4), AX.X, ALU.add))
                seqs = "p h (b c) -> p h b c"
                la, qs = later[:].rearrange(seqs, c=8), quad_sum[:].rearrange(seqs, c=8)
                for c in range(6, -1, -1):
                    last = nc.vector.tensor_tensor(la[:, :, :, c], la[:, :, :, c + 1], qs[:, :, :, c + 1], ALU.add)
                    if c:
                        link(last)
                last.then_inc(later_ready, 1)
                link(nc.vector.tensor_scalar(row_mod[:], row[:], DEC_S - 1, None, ALU.bitwise_and))
                link(nc.vector.tensor_scalar(row[:], row[:], R - 1, 2, ALU.bitwise_and, ALU.logical_shift_right))
                link(nc.vector.tensor_copy(row_h[:], row[:]))
                link(nc.vector.tensor_scalar(own_head[:], own_head[:], row_h[:, 0:1], None, ALU.is_equal))
                link(nc.vector.tensor_reduce(fold[:], g.ident[:].rearrange("p (j r) -> p r j", j=4), AX.X, ALU.add))

                def row_max(b, half):
                    dve.wait_ge(s_done[half], START + b + 1)
                    dve.wait_ge(kT_used[1], START + 2 * (2 * b + half) + 2)
                    dve.wait_ge(kept[half], START + 2 * b)
                    nc.vector.tensor_reduce(nmax[:, half:half + 1], ps[:, 4 + half, :], AX.X, ALU.max,
                                            negate=True).then_inc(have_max[half], 1)

                def turned(b, half):
                    dve.wait_ge(prT_done[half], START + b + 1)
                    nc.vector.tensor_copy(prT[:], ps[:, 7, :]).then_inc(prT_copied[half], 1)

                def own_heads(b, half):
                    dve.wait_ge(pv_done[3], START + 2 * b + half + 1)
                    nc.vector.tensor_tensor(o_all[:], ps[:, 6, :], own_head[:].rearrange("p h d -> p (h d)"),
                                            ALU.mult).then_inc(o_read[half], 1)
                    dve.wait_ge(o_read[half], START + b + 1)
                    nc.vector.tensor_reduce(o_head[:, bass.ds(2 * b + half, 1), :].rearrange("p a d -> p (a d)"),
                                            o_all[:].rearrange("p (h d) -> p d h", h=H), AX.X, ALU.add)\
                        .then_inc(o_masked[half], 1)
                    dve.wait_ge(o_masked[half], b + 1)

                def unit(b, half, before):
                    copy_keys(dve, nc.vector.tensor_copy, 0, b, half, 0)
                    if before:
                        row_max(*before)
                    copy_keys(dve, nc.vector.tensor_copy, 0, b, half, 1)
                    if before:
                        turned(*before)
                    for pp in (2, 3):
                        copy_keys(dve, nc.vector.tensor_copy, 0, b, half, pp)
                    if before:
                        own_heads(*before)

                pipeline(dve, unit)
                final = (DEC_B - 1, 1)
                row_max(*final)
                turned(*final)
                own_heads(*final)

                link(nc.vector.tensor_copy(row_q[:], row_mod[0:R, :]))
                link(nc.vector.tensor_scalar(key_q[:], key_q[:], row_q[:, 0:1], NEG, ALU.is_gt, ALU.mult))
                dve.wait_ge(c_pe, 1)
                link(nc.vector.tensor_tensor(s_new[:], ps[0:R, 0, 0:DEC_B * NS].rearrange("r (b k) -> r b k", k=NS),
                                             key_q[:], ALU.add))
                link(nc.vector.tensor_tensor(s_new[:], s_new[:], own_seq[:], ALU.add))
                link(nc.vector.tensor_reduce(nmax_new[:], s_new[:], AX.X, ALU.max, negate=True))
                nc.vector.tensor_tensor(s_new[:], s_new[:], nmax_new[:].unsqueeze(2).to_broadcast([R, DEC_B, NS]),
                                        ALU.add).then_inc(shifted, 1)
                dve.wait_ge(c_act, 1)
                nc.vector.tensor_reduce(rsum_new[:], s_new[:], AX.X, ALU.add).then_inc(c_dve, 1)
                dve.wait_ge(c_pe, 2)
                parts = "b (n r) -> b n r"
                link(nc.vector.tensor_copy(parts_m[:], ps[0:DEC_B, 1, 0:9 * R].rearrange(parts, r=R)))
                link(nc.vector.tensor_copy(parts_l[:], ps[0:DEC_B, 2, 0:9 * R].rearrange(parts, r=R)))
                link(nc.vector.tensor_reduce(top[:], parts_m[:].rearrange("b n r -> b r n"), AX.X, ALU.min))
                nc.vector.tensor_tensor(parts_m[:], top[:].unsqueeze(1).to_broadcast([DEC_B, 9, R]), parts_m[:],
                                        ALU.subtract).then_inc(shifted, 1)
                dve.wait_ge(c_act, 2)
                link(nc.vector.tensor_tensor(parts_l[:], parts_l[:], parts_w[:], ALU.mult))
                link(nc.vector.tensor_reduce(total[:], parts_l[:].rearrange("b n r -> b r n"), AX.X, ALU.add))
                link(nc.vector.reciprocal(total[:], total[:]))
                nc.vector.tensor_tensor(parts_w[:], parts_w[:], total[:].unsqueeze(1).to_broadcast([DEC_B, 9, R]),
                                        ALU.mult).then_inc(c_dve, 1)
                dve.wait_ge(c_pe, 3)
                link(nc.vector.tensor_copy(share[:], ps[:, 3, 0:2 * DEC_B].rearrange("p (a b) -> p b a", a=2)))
                link(nc.vector.tensor_copy(share_new[:], ps[0:R, 3, 2 * DEC_B:3 * DEC_B]))
                nc.vector.tensor_tensor(s_new[:], s_new[:], share_new[:].unsqueeze(2).to_broadcast([R, DEC_B, NS]),
                                        ALU.mult).then_inc(c_dve, 1)
                o_parts = o_head[:].rearrange("p (b a) d -> p b a d", a=2)
                link(nc.vector.tensor_tensor(o_parts, o_parts, share[:].unsqueeze(3).to_broadcast([P, DEC_B, 2, HD]), ALU.mult))
                dve.wait_ge(c_pe, 4)
                nc.vector.tensor_copy(p_newT[:], ps[0:NS, 0, 0:DEC_B * R]).then_inc(c_dve, 1)
                dve.wait_ge(c_pe, 5)
                for bh in range(2):
                    link(nc.vector.tensor_tensor(o_all[:], ps[:, 4 + bh, :], own_head[:].rearrange("p h d -> p (h d)"),
                                                 ALU.mult))
                    last = nc.vector.tensor_reduce(o_new[:, bh, :], o_all[:].rearrange("p (h d) -> p d h", h=H), AX.X,
                                                   ALU.add)
                    if bh == 0:
                        link(last)
                last.then_inc(c_dve, 1)
                dve.wait_ge(c_pe, 6)
                res = ps[0:HD, 7, 0:DEC_B * R].rearrange("d (b c hh q) -> d hh c b q", b=DEC_B, c=KC, hh=2)
                for hh in range(2):
                    nc.vector.tensor_copy(g.aT[hh * HD:(hh + 1) * HD, :, SEQ:T].rearrange("d c (b q) -> d c b q", q=DEC_S),
                                          res[:, hh])

            @block.scalar
            def _(act):
                nc.scalar.preload_act_table(ACT.Exp)

                def exps(b, half):
                    act.wait_ge(have_max[half], b + 1)
                    act.wait_ge(prT_done[half], START + b)
                    act.wait_ge(kept[half], START + 2 * b)
                    nc.scalar.activation(pr[:, half, :], ps[:, 4 + half, :], ACT.Exp, bias=nmax[:, half:half + 1],
                                         accum_out=rsum[:, half:half + 1]).then_inc(exped[half], 1)

                def unit(b, half, before):
                    copy_keys(act, nc.scalar.copy, 1, b, half, 0)
                    if before:
                        exps(*before)
                    for pp in (1, 2, 3):
                        copy_keys(act, nc.scalar.copy, 1, b, half, pp)

                pipeline(act, unit)
                exps(DEC_B - 1, 1)
                act.wait_ge(shifted, 1)
                nc.scalar.activation(s_new[:], s_new[:], ACT.Exp).then_inc(c_act, 1)
                act.wait_ge(shifted, 2)
                nc.scalar.activation(parts_w[:], parts_m[:], ACT.Exp).then_inc(c_act, 1)


def mix(nc, io, g, ps, mT):
    KA = DA // P
    LH = KD * P
    PIECES, QUARTERS, QC = 3, 4, 4
    F32R = mybir.dt.float32r
    STEPS = KD // 2
    with ExitStack() as ctx:
        m = Mem(nc, ctx, "mix")
        w_raw = [m.sb(f"w_raw{p}", [P, LH]) for p in range(PIECES)]
        w_hi, w_lo = ([m.sb(f"w_{n}{p}", [P, LH], F32R) for p in range(PIECES)] for n in ("hi", "lo"))
        x_hi, x_lo = (m.sb(f"x_{n}", [P, QUARTERS * QC, BLK], F32R) for n in ("hi", "lo"))
        sg = [m.sb(f"sg{i}", [P, 2, BLK]) for i in range(2)]
        raw_in, hi_done, lo_done, w_used = (m.sems(n, PIECES) for n in ("raw_in", "hi_done", "lo_done", "w_used"))
        x_hi_done, x_lo_done = m.sems("x_hi_done", QUARTERS), m.sems("x_lo_done", QUARTERS)
        gated, used, added = (m.sems(n, 2) for n in ("gated", "used", "added"))
        seen = m.sems("seen", QUARTERS)
        sp_seen, pool_seen = m.sem("sp_seen"), m.sem("pool_seen")
        gate_v = io["w_in"][0].rearrange("(k p) n -> p k n", p=P)
        out_v = [w[0].rearrange("(k p) n -> p k n", p=P) for w in (io["w_attn_out"], io["w_gmlp_out"])]
        mT_flat = mT[:].rearrange("p k n -> p (k n)")

        m.start(lo_done + w_used + used + added)

        def steps(eng, block_start, body):
            with eng.Fori(0, 3) as j:
                block_start(j)
                with eng.Fori(0, STEPS) as pair:
                    for b in range(2):
                        body(j, pair, b, KD * j + 2 * pair + b)

        def quarter(q, j):
            src, first = ((g.hT, 0), (g.hT, QC), (g.aT, 0), (g.uT, 0))[q]
            return src[:, first:first + QC, bass.ds(j * BLK, BLK)]

        def split_hi(eng, copy, q, j):
            eng.wait_ge(w_used[1 if q < 2 else 2], START + KD * j)
            eng.sem_inc(seen[q], 1)
            copy(x_hi[:, q * QC:(q + 1) * QC, :], quarter(q, j)).then_inc(x_hi_done[q], 1)

        def split_lo(eng, tensor_tensor, q, j):
            at = slice(q * QC, (q + 1) * QC)
            eng.wait_ge(x_hi_done[q], j + 1)
            eng.sem_inc(seen[q], 1)
            tensor_tensor(x_lo[:, at, :], quarter(q, j), x_hi[:, at, :].bitcast(F32), ALU.subtract)\
                .then_inc(x_lo_done[q], 1)

        with nc.Block() as block:
            @block.sync
            def _(sp):
                def body(j, pair, b, n):
                    column = (2 * pair + b) * P
                    for p in range(PIECES):
                        sp.wait_ge(lo_done[p], START + n)
                        sp.sem_inc(sp_seen, 1)
                        raw = w_raw[p][:].rearrange("p (k n) -> p k n", n=P)
                        if p < 2:
                            sp.dma_start(raw, gate_v[:, :, bass.ds(column + (COL_GA, COL_GG)[p], P)]).then_inc(raw_in[p], 32)
                            continue
                        for o in range(2):
                            sp.dma_start(raw[:, o * KA:(o + 1) * KA, :], out_v[o][:, :, bass.ds(column, P)])\
                                .then_inc(raw_in[p], 16)

                steps(sp, lambda j: None, body)
                sp.wait_ge(lo_done[0], START + 3 * KD)
                sp.dma_start(w_raw[0][:].rearrange("p (k n) -> p k n", n=P), gate_v[:, :, COL_GA:COL_GA + P])\
                    .then_inc(raw_in[0], 32)

            @block.tensor
            def _(pe):
                def product(out, p, w_chunks, x_first):
                    for i, c in enumerate(w_chunks):
                        at, x = slice(c * P, (c + 1) * P), x_first + i
                        for k, (w, v) in enumerate(((w_hi, x_hi), (w_hi, x_lo), (w_lo, x_hi))):
                            last = nc.tensor.matmul(out, w[p][:, at], v[:, x, :], start=(i == 0 and k == 0),
                                                    stop=(i == len(w_chunks) - 1 and k == 2))
                    return last

                def body(j, pair, b, n):
                    pe.wait_ge(used[b], START + STEPS * j + pair)
                    for p in range(2):
                        pe.wait_ge(lo_done[p], START + n + 1)
                        for q in range(2):
                            pe.wait_ge(x_lo_done[q], j + 1)
                        product(ps[:, 4 * b + p, 0:BLK], p, range(KD), 0).then_inc(w_used[p], 1)
                    pe.wait_ge(lo_done[2], START + n + 1)
                    for o in range(2):
                        pe.wait_ge(x_lo_done[2 + o], j + 1)
                        last = product(ps[:, 4 * b + 2 + o, 0:BLK], 2, range(o * KA, (o + 1) * KA), KD + o * KA)
                    last.then_inc(w_used[2], 1)

                steps(pe, lambda j: None, body)

            @block.scalar
            def _(act):
                def block_start(j):
                    for q in range(2):
                        split_hi(act, nc.scalar.copy, q, j)

                def body(j, pair, b, n):
                    for p, step in ((1, n), (2, n), (0, n + 1)):
                        act.wait_ge(raw_in[p], 32 * step + 32)
                        act.wait_ge(w_used[p], START + step)
                        nc.scalar.copy(w_hi[p][:], w_raw[p][:]).then_inc(hi_done[p], 1)
                    act.wait_ge(w_used[1], START + n + 1)
                    act.wait_ge(added[b], START + STEPS * j + pair)
                    nc.scalar.activation(sg[b][:], ps[:, 4 * b:4 * b + 2, 0:BLK], ACT.Sigmoid).then_inc(gated[b], 1)

                nc.scalar.preload_act_table(ACT.Sigmoid)
                act.wait_ge(raw_in[0], 32)
                nc.scalar.copy(w_hi[0][:], w_raw[0][:]).then_inc(hi_done[0], 1)
                steps(act, block_start, body)

            @block.vector
            def _(dve):
                def split_w(p, step):
                    dve.wait_ge(hi_done[p], step + 1)
                    nc.vector.tensor_tensor(w_lo[p][:], w_raw[p][:], w_hi[p][:].bitcast(F32), ALU.subtract)\
                        .then_inc(lo_done[p], 1)

                def block_start(j):
                    for q in range(2):
                        split_lo(dve, nc.vector.tensor_tensor, q, j)

                def body(j, pair, b, n):
                    for p, step in ((1, n), (2, n), (0, n + 1)):
                        split_w(p, step)
                    dve.wait_ge(gated[b], STEPS * j + pair + 1)
                    dve.wait_ge(w_used[2], START + n + 1)
                    nc.vector.tensor_tensor(sg[b][:], ps[:, 4 * b + 2:4 * b + 4, 0:BLK], sg[b][:], ALU.mult)\
                        .then_inc(used[b], 1)

                split_w(0, 0)
                steps(dve, block_start, body)

            @block.gpsimd
            def _(pool):
                def block_start(j):
                    for q in range(2, QUARTERS):
                        split_hi(pool, nc.gpsimd.tensor_copy, q, j)
                        split_lo(pool, nc.gpsimd.tensor_tensor, q, j)

                def body(j, pair, b, n):
                    pool.wait_ge(used[b], START + STEPS * j + pair + 1)
                    pool.sem_inc(pool_seen, 1)
                    nc.gpsimd.tensor_tensor(mT_flat[:, bass.ds((2 * pair + b) * T + j * BLK, BLK)],
                                            sg[b][:, 0, :], sg[b][:, 1, :], ALU.add).then_inc(added[b], 1)

                steps(pool, block_start, body)


class Norm:

    def __init__(self, m, eps, gain, bias):
        self.stats, self.mv, self.std = m.sb("ln_stats", [P, 2, 6]), m.sb("ln_mv", [P, 2]), m.sb("ln_std", [P, 1])
        self.eps, self.gain, self.bias = eps, gain, bias
        self.have_var, self.have_std = m.sem("have_var"), m.sem("have_std")

    def variance(self, nc, link, r, rows):
        for half in range(2):
            link(nc.vector.bn_stats(self.stats[0:rows, half, :], r[0:rows, half * 512:(half + 1) * 512]))
        nc.vector.bn_aggr(self.mv[0:rows, :], self.stats[0:rows].rearrange("p a n -> p (a n)")).then_inc(self.have_var, 1)

    def deviation(self, nc, act, t, rows):
        act.wait_ge(self.have_var, t + 1)
        nc.scalar.activation(self.std[0:rows, :], self.mv[0:rows, 1:2], ACT.Sqrt, bias=self.eps[0:rows, 0:1])\
            .then_inc(self.have_std, 1)

    def apply(self, nc, dve, link, t, out, r, rows):
        dve.wait_ge(self.have_std, t + 1)
        link(nc.vector.reciprocal(self.std[0:rows, :], self.std[0:rows, :]))
        link(nc.vector.scalar_tensor_tensor(out=r[0:rows, :], in0=r[0:rows, :], scalar=self.mv[0:rows, 0:1],
                                            in1=self.gain[0:rows, :], op0=ALU.subtract, op1=ALU.mult))
        return nc.vector.scalar_tensor_tensor(out=out, in0=r[0:rows, :], scalar=self.std[0:rows, 0:1],
                                              in1=self.bias[0:rows, :], op0=ALU.mult, op1=ALU.add)


def mixer_out(nc, io, g, ps, mT):
    RW = 32
    with ExitStack() as ctx:
        m = Mem(nc, ctx, "mo")
        w_o, w_in = m.sb("w_o", [P, KD, D]), m.sem("w_in")
        w_r = m.sb("w_r", [P, KD, RW])
        b_r = m.sb("b_r", [P, NG + NEXP])
        ln_b = m.sb("ln_b", [P, D])
        x_t, r_t, h_t = ([m.sb(f"{n}{i}", [P, D]) for i in range(2)] for n in ("x", "r", "h"))
        hT_t = m.sb("hT", [P, KD, P])
        eps, fold = m.sb("eps", [P, 1]), m.sb("fold", [P, RW])
        part = m.sb("part", [P, P])
        norm = Norm(m, eps, g.ln_g, ln_b)
        wr_in, wr_zero, rows_in, par_in = (m.sem(n) for n in ("wr_in", "wr_zero", "rows_in", "par_in"))
        plus_one, consts = m.sem("plus_one"), m.sem("consts")
        x_in, m_full, m_read, x1_done, h2_done = (m.sems(n, 2) for n in ("x_in", "m_full", "m_read", "x1_done", "h2_done"))
        h2_out = m.sems("h2_out", 2)
        h2T_full, h2T_copied = m.sems("h2T_full", 2), m.sems("h2T_copied", 2)
        part_full, part_copied, logits_full, logits_read = (m.sem(n) for n in ("pf", "pc", "lf", "lr"))
        own, pool_own = m.sem("own"), m.sem("pool_own")
        x_rows = [io["x_prompt"][0, t * P:(t + 1) * P, :] for t in range(PT)] + [io["x_sample"].rearrange("b s d -> (b s) d")]

        def mod(which, t):
            return g.rows[which][0 if t < PT else 1]

        with nc.Block() as block:
            def store_h2(sp, t):
                rows, b = TILE_ROWS[t], t % 2
                sp.wait_ge(h2_done[b], t // 2 + 1)
                sp.dma_start(g.h2_rows[t * P:t * P + rows, :], h_t[b][0:rows, :]).then_inc(h2_out[b], 16)

            @block.sync
            def _(sp):
                sp.dma_start(w_o[:], io["w_o"][0].rearrange("(k p) n -> p k n", p=P)).then_inc(w_in, 16)
                for which, at in (("g1", 0), ("sc2", 2), ("sh2", 1), ("g2", 3)):
                    sp.dma_start(g.rows[which][0], g.ada_rows[0:1, at, :].partition_broadcast(P)
                                 .rearrange("p a n -> p (a n)")).then_inc(rows_in, 16)
                    sp.dma_start(g.rows[which][1][0:NS, :],
                                 g.ada_rows[1:NB, at, :].unsqueeze(1).to_broadcast([DEC_B, DEC_S, D]))\
                        .then_inc(rows_in, 16)
                for dst, src in ((g.ln_g, io["ln1_g"]), (ln_b[:], io["ln1_b"])):
                    sp.dma_start(dst, src.partition_broadcast(P).rearrange("p a n -> p (a n)")).then_inc(par_in, 16)
                for dst, src in ((b_r[:, 0:NG], io["b_group_router"]), (b_r[:, NG:], io["b_expert_router"])):
                    sp.dma_start(dst, src.partition_broadcast(P).rearrange("p a n -> p (a n)")).then_inc(par_in, 16)
                sp.wait_ge(wr_zero, 1)
                with nc.allow_non_contiguous_dma(reason="narrow router weights"):
                    for dst, src in ((w_r[:, :, 0:NG], io["w_group_router"]), (w_r[:, :, NG:NG + NEXP], io["w_expert_router"])):
                        sp.dma_start(dst, src[0].rearrange("(k p) n -> p k n", p=P)).then_inc(wr_in, 16)
                for t in range(NT):
                    rows, b = TILE_ROWS[t], t % 2
                    if t >= 2:
                        sp.wait_ge(x1_done[b], t // 2)
                    sp.dma_start(x_t[b][0:rows, :], x_rows[t]).then_inc(x_in[b], 16)
                    if t >= 1:
                        store_h2(sp, t - 1)
                store_h2(sp, NT - 1)
                for b in range(2):
                    sp.wait_ge(h2_out[b], 16 * ((NT + 1 - b) // 2))

            @block.tensor
            def _(pe):
                pe.wait_ge(w_in, 16)

                def product(t, half):
                    b = t % 2
                    if t >= 2:
                        pe.wait_ge(m_read[b], t // 2)
                    for k in range(KD):
                        if t < PT:
                            last = nc.tensor.matmul(ps[:, 2 * b + half, :], mT[:, k, t * P:(t + 1) * P],
                                                    w_o[:, k, half * 512:(half + 1) * 512], start=(k == 0),
                                                    stop=(k == KD - 1))
                            continue
                        for j in range(4):
                            at = half * 512 + j * P
                            last = nc.tensor.matmul(ps[NS * j:NS * j + NS, 2 * b + half, 0:P], mT[:, k, SEQ:T],
                                                    w_o[:, k, at:at + P], start=(k == 0), stop=(k == KD - 1))
                    if half:
                        last.then_inc(m_full[b], 1)

                def transpose_h2(t):
                    rows, b = TILE_ROWS[t], t % 2
                    pe.wait_ge(h2_done[b], t // 2 + 1)
                    for half in range(2):
                        pe.wait_ge(h2T_copied[half], t)
                        for i in range(4):
                            k = 4 * half + i
                            last = nc.tensor.transpose(ps[:, 4 + half, i * P:i * P + rows],
                                                       h_t[b][0:rows, k * P:(k + 1) * P], g.ident[0:rows, 0:rows])
                        last.then_inc(h2T_full[half], 1)

                def route(t):
                    rows = TILE_ROWS[t]
                    for half in range(2):
                        pe.wait_ge(h2T_copied[half], t + 1)
                    pe.wait_ge(part_copied, t)
                    for k in range(KD):
                        j = k % 4
                        last = nc.tensor.matmul(ps[RW * j:RW * j + RW, 6, 0:rows], w_r[:, k, :], hT_t[:, k, 0:rows],
                                                start=(k < 4), stop=(k >= 4))
                    last.then_inc(part_full, 1)

                def add_quarters(t):
                    rows = TILE_ROWS[t]
                    pe.wait_ge(part_copied, t + 1)
                    pe.wait_ge(logits_read, t)
                    nc.tensor.matmul(ps[0:rows, 7, 0:RW], part[:, 0:rows], fold[:], start=True, stop=True)\
                        .then_inc(logits_full, 1)

                product(0, 0)
                product(0, 1)
                product(1, 0)
                pe.wait_ge(wr_in, 32)
                for t in range(NT):
                    if t + 1 < NT:
                        product(t + 1, 1)
                    transpose_h2(t)
                    if t + 2 < NT:
                        product(t + 2, 0)
                    route(t)
                    if t:
                        add_quarters(t - 1)
                add_quarters(NT - 1)

            @block.scalar
            def _(act):
                for t in range(NT + 1):
                    if t < NT:
                        norm.deviation(nc, act, t, TILE_ROWS[t])
                    if t:
                        rows = TILE_ROWS[t - 1]
                        for half in range(2):
                            act.wait_ge(h2T_full[half], t)
                            act.wait_ge(part_full, t - 1)
                            nc.scalar.copy(hT_t[:, 4 * half:4 * half + 4, 0:rows],
                                           ps[:, 4 + half, :].rearrange("p (k n) -> p k n", k=4)[:, :, 0:rows])\
                                .then_inc(h2T_copied[half], 1)
                        act.wait_ge(part_full, t)
                        act.wait_ge(logits_full, t - 1)
                        nc.scalar.copy(part[:, 0:rows], ps[:, 6, 0:rows]).then_inc(part_copied, 1)

            @block.vector
            def _(dve):
                link = Chain(dve, own)
                dve.wait_ge(rows_in, 16 * 8)
                for which in ("g1", "sc2", "g2"):
                    for kind, rows in enumerate((P, NS)):
                        at = g.rows[which][kind][0:rows, :]
                        nc.vector.tensor_scalar(at, at, 1.0, None, ALU.add).then_inc(plus_one, 1)
                link(nc.vector.tensor_reduce(fold[:], g.ident[:].rearrange("p (j r) -> p r j", j=4), AX.X, ALU.add))
                dve.wait_ge(plus_one, 6)
                dve.wait_ge(par_in, 64)
                dve.wait_ge(consts, 2)

                def logits(t):
                    rows = TILE_ROWS[t]
                    dve.wait_ge(logits_full, t + 1)
                    nc.vector.tensor_tensor(g.logits[0:rows, t, :], ps[0:rows, 7, 0:NG + NEXP], b_r[0:rows, :], ALU.add)\
                        .then_inc(logits_read, 1)

                for t in range(NT):
                    rows, b = TILE_ROWS[t], t % 2
                    r = r_t[b]
                    dve.wait_ge(m_full[b], t // 2 + 1)
                    if t < PT:
                        last = nc.vector.tensor_tensor(r[:], ps[:, 2 * b:2 * b + 2, :].rearrange("p a n -> p (a n)"),
                                                       mod("g1", t), ALU.mult)
                    else:
                        for n in range(KD):
                            half, j, at = n // 4, n % 4, slice(n * P, (n + 1) * P)
                            last = nc.vector.tensor_tensor(r[0:NS, at], ps[NS * j:NS * j + NS, 2 * b + half, 0:P],
                                                           mod("g1", t)[0:NS, at], ALU.mult)
                    last.then_inc(m_read[b], 1)
                    dve.wait_ge(m_read[b], t // 2 + 1)
                    dve.wait_ge(x_in[b], 16 * (t // 2 + 1))
                    link(nc.vector.scalar_tensor_tensor(out=r[0:rows, :], in0=x_t[b][0:rows, :], scalar=ALPHA,
                                                        in1=r[0:rows, :], op0=ALU.mult, op1=ALU.add))
                    norm.variance(nc, link, r, rows)
                    if t >= 2:
                        logits(t - 2)
                    norm.apply(nc, dve, link, t, g.x1[0:rows, t, :], r, rows).then_inc(x1_done[b], 1)
                logits(NT - 2)
                logits(NT - 1)

            @block.gpsimd
            def _(pool):
                link = Chain(pool, pool_own)
                nc.gpsimd.memset(w_r[:], 0.0).then_inc(wr_zero, 1)
                nc.gpsimd.memset(eps[:], EPS).then_inc(consts, 1)
                nc.gpsimd.memset(g.logits[:], 0.0).then_inc(consts, 1)
                pool.wait_ge(plus_one, 6)
                for t in range(NT):
                    rows, b = TILE_ROWS[t], t % 2
                    pool.wait_ge(x1_done[b], t // 2 + 1)
                    pool.wait_ge(h2_out[b], 16 * (t // 2))
                    if t >= 2:
                        for half in range(2):
                            pool.wait_ge(h2T_full[half], t - 1)
                    link(nc.gpsimd.tensor_tensor(h_t[b][0:rows, :], g.x1[0:rows, t, :], mod("sc2", t)[0:rows, :], ALU.mult))
                    nc.gpsimd.tensor_tensor(h_t[b][0:rows, :], h_t[b][0:rows, :], mod("sh2", t)[0:rows, :], ALU.add)\
                        .then_inc(h2_done[b], 1)


SLOT_TILES = (2 * T - NEXP) // P + NEXP


def route(nc, io, g, ps, load_weights):
    W = NG + NEXP
    with ExitStack() as ctx:
        m = Mem(nc, ctx, "rt")
        sb = m.sb
        valid = sb("valid", [P, NT])
        turn4 = sb("turn4", [P, NT, 4])
        top = sb("top", [P, NT, 1])
        grp, e1, e2 = (sb(n, [P, NT, 4]) for n in ("grp", "e1", "e2"))
        diff, el, tmp = (sb(n, [P, NT, 4]) for n in ("diff", "el", "tmp"))
        picked = sb("picked", [P, NT, NG, EPG])
        p_top, l1, l2, w_sum = (sb(n, [P, NT, 1]) for n in ("p_top", "l1", "l2", "w_sum"))
        pair = [sb(f"pair{i}", [P, NT, NEXP]) for i in range(2)]
        both, place = sb("both", [P, NT, NEXP]), sb("place", [P, NT, NEXP])
        total, tiles, ends, base = (sb(n, [P, NEXP]) for n in ("total", "tiles", "ends", "base"))
        steps, over = sb("steps", [P, NT]), sb("over", [P, NEXP, NT])
        slot_f = sb("slot_f", [P, 2, NT])
        slot_i, slot_lo = sb("slot_i", [P, 2, NT], I32), sb("slot_lo", [P, 2, NT], I32)
        token = sb("token", [P, NT], I32)
        zeros = sb("zeros", [P, SLOT_TILES], I32)
        tile_no, past, owner = sb("tile_no", [1, SLOT_TILES]), sb("past", [1, SLOT_TILES, NEXP]), sb("owner", [1, SLOT_TILES])
        consts, own = m.sem("consts"), m.sem("own")
        shifted, exped, counted, sums_read = m.sem("shifted"), m.sem("exped"), m.sem("counted"), m.sem("sums_read")
        summed, have_experts = m.sem("summed"), m.sem("have_experts")
        zeroed, have_slots, scattered, listed = m.sem("zeroed"), m.sem("have_slots"), m.sem("scattered"), m.sem("listed")

        with nc.Block() as block:
            @block.sync
            def _(sp):
                sp.wait_ge(have_experts, 1)
                for tile in range(2):
                    load_weights(sp, tile, tile)

            @block.gpsimd
            def _(pool):
                nc.gpsimd.memset(zeros[:], 0).then_inc(consts, 1)
                nc.gpsimd.affine_select(out=valid[:], in_=g.ones[:, 0:NT], compare_op=ALU.is_ge, fill=0.0, base=T - 1,
                                        pattern=[[-P, NT]], channel_multiplier=-1).then_inc(consts, 1)
                nc.gpsimd.iota(turn4[:], pattern=[[0, NT], [-1, 4]], base=4, channel_multiplier=0,
                               allow_small_or_imprecise_dtypes=True).then_inc(consts, 1)
                nc.gpsimd.iota(steps[:], pattern=[[P, NT]], base=0, channel_multiplier=0,
                               allow_small_or_imprecise_dtypes=True).then_inc(consts, 1)
                nc.gpsimd.iota(tile_no[:], pattern=[[1, SLOT_TILES]], base=0, channel_multiplier=0,
                               allow_small_or_imprecise_dtypes=True).then_inc(consts, 1)
                nc.gpsimd.iota(token[:], pattern=[[P, NT]], base=0, channel_multiplier=1).then_inc(consts, 1)
                pool.wait_ge(consts, 6)
                pool.dma_start(g.slot_token.rearrange("(p n) a -> p (n a)", p=P), zeros[:]).then_inc(zeroed, 16)
                pool.wait_ge(zeroed, 16)
                pool.wait_ge(have_slots, 1)
                for t in range(NT):
                    for i in range(2):
                        rows = TILE_ROWS[t]
                        pool.indirect_dma_start(g.slot_token, bass.IndirectOffsetOnAxis(slot_lo[0:rows, i, t:t + 1], 0),
                                                token[0:rows, t:t + 1], None).then_inc(scattered, 16)
                pool.wait_ge(scattered, 32 * NT)
                pool.dma_start(g.slot_list[:], g.slot_token.rearrange("(p n) a -> p (n a)", p=P)).then_inc(listed, 16)
                pool.wait_ge(listed, 16)

            @block.scalar
            def _(act):
                act.wait_ge(shifted, 1)
                nc.scalar.activation(diff[:], diff[:], ACT.Exp).then_inc(exped, 1)
                act.wait_ge(shifted, 2)
                nc.scalar.activation(l2[:], l2[:], ACT.Exp).then_inc(exped, 1)

            @block.tensor
            def _(pe):
                pe.wait_ge(counted, 1)
                flat = both[:].rearrange("p t e -> p (t e)")
                nc.tensor.matmul(ps[:, 0, 0:NT * NEXP], g.before[:], flat, start=True, stop=True).then_inc(summed, 1)
                nc.tensor.matmul(ps[:, 1, 0:NT * NEXP], g.ones[:, 0:P], flat, start=True, stop=True).then_inc(summed, 1)

            @block.vector
            def _(dve):
                link = Chain(dve, own)
                v = nc.vector
                lg = g.logits[:, :, 0:NG]

                def first_max(out, values, maximum):
                    link(v.tensor_reduce(maximum[:], values, AX.X, ALU.max))
                    link(v.tensor_tensor(tmp[:], values, maximum[:].to_broadcast([P, NT, 4]), ALU.is_equal))
                    link(v.tensor_tensor(tmp[:], tmp[:], turn4[:], ALU.mult))
                    link(v.tensor_reduce(top[:], tmp[:], AX.X, ALU.max))
                    link(v.tensor_tensor(out[:], tmp[:], top[:].to_broadcast([P, NT, 4]), ALU.is_equal))

                dve.wait_ge(consts, 6)
                first_max(grp, lg, p_top)
                v.tensor_tensor(diff[:], lg, p_top[:].to_broadcast([P, NT, 4]), ALU.subtract).then_inc(shifted, 1)
                link(v.tensor_tensor(picked[:], g.logits[:, :, NG:W].rearrange("p t (g e) -> p t g e", g=NG),
                                     grp[:].unsqueeze(3).to_broadcast([P, NT, NG, EPG]), ALU.mult))
                link(v.tensor_reduce(el[:], picked[:].rearrange("p t g e -> p t e g"), AX.X, ALU.add))
                first_max(e1, el[:], l1)
                link(v.scalar_tensor_tensor(out=el[:], in0=e1[:], scalar=NEG, in1=el[:], op0=ALU.mult, op1=ALU.add))
                first_max(e2, el[:], l2)
                v.tensor_tensor(l2[:], l2[:], l1[:], ALU.subtract).then_inc(shifted, 1)
                dve.wait_ge(exped, 1)
                link(v.tensor_reduce(p_top[:], diff[:], AX.X, ALU.add))
                link(v.reciprocal(p_top[:], p_top[:]))
                dve.wait_ge(exped, 2)
                link(v.tensor_scalar(w_sum[:], l2[:], 1.0, None, ALU.add))
                link(v.reciprocal(w_sum[:], w_sum[:]))
                link(v.tensor_tensor(g.weight[:, 0, :].unsqueeze(2), w_sum[:], p_top[:], ALU.mult))
                link(v.tensor_tensor(g.weight[:, 1, :].unsqueeze(2), g.weight[:, 0, :].unsqueeze(2), l2[:], ALU.mult))
                link(v.tensor_tensor(grp[:], grp[:], valid[:].unsqueeze(2).to_broadcast([P, NT, 4]), ALU.mult))
                for i, e in enumerate((e1, e2)):
                    link(v.tensor_tensor(pair[i][:].rearrange("p t (g e) -> p t g e", g=NG),
                                         grp[:].unsqueeze(3).to_broadcast([P, NT, NG, EPG]),
                                         e[:].unsqueeze(2).to_broadcast([P, NT, NG, EPG]), ALU.mult))
                v.tensor_tensor(both[:], pair[0][:], pair[1][:], ALU.add).then_inc(counted, 1)
                dve.wait_ge(summed, 2)
                link(v.tensor_copy(place[:], ps[:, 0, 0:NT * NEXP].rearrange("p (t e) -> p t e", e=NEXP)))
                sums = ps[:, 1, 0:NT * NEXP].rearrange("p (t e) -> p t e", e=NEXP)
                link(v.tensor_copy(total[:], sums[:, 0, :]))
                for t in range(1, NT):
                    link(v.tensor_tensor(place[:, t, :], place[:, t, :], total[:], ALU.add))
                    link(v.tensor_tensor(total[:], sums[:, t, :], total[:], ALU.add))
                link(v.tensor_tensor(over[:], total[:].unsqueeze(2).to_broadcast([P, NEXP, NT]),
                                     steps[:].unsqueeze(1).to_broadcast([P, NEXP, NT]), ALU.is_gt))
                link(v.tensor_reduce(tiles[:], over[:], AX.X, ALU.add))
                link(v.tensor_tensor_scan(ends[:], g.ones[:, 0:NEXP], tiles[:], 0.0, ALU.mult, ALU.add))
                link(v.tensor_tensor(base[:], ends[:], tiles[:], ALU.subtract))
                link(v.tensor_scalar(base[:], base[:], float(P), None, ALU.mult))
                link(v.tensor_tensor(place[:], place[:], base[:].unsqueeze(1).to_broadcast([P, NT, NEXP]), ALU.add))
                for i in range(2):
                    link(v.tensor_tensor(pair[i][:], pair[i][:], place[:], ALU.mult))
                    link(v.tensor_reduce(slot_f[:, i, :], pair[i][:], AX.X, ALU.add))
                link(v.tensor_copy(g.slot[:], slot_f[:]))
                link(v.tensor_scalar(slot_i[:], g.slot[:], P.bit_length() - 1, None, ALU.logical_shift_right))
                link(v.tensor_scalar(slot_lo[:], g.slot[:], P - 1, None, ALU.bitwise_and))
                link(v.tensor_scalar(slot_lo[:], slot_lo[:], float(SLOT_TILES), None, ALU.mult))
                v.tensor_tensor(slot_lo[:], slot_lo[:], slot_i[:], ALU.add).then_inc(have_slots, 1)
                link(v.tensor_tensor(past[:], tile_no[:].unsqueeze(2).to_broadcast([1, SLOT_TILES, NEXP]),
                                     ends[0:1, :].unsqueeze(1).to_broadcast([1, SLOT_TILES, NEXP]), ALU.is_ge))
                link(v.tensor_reduce(owner[:], past[:], AX.X, ALU.add))
                link(v.tensor_scalar(owner[:], owner[:], float(NEXP - 1), None, ALU.min))
                v.tensor_copy(g.tile_expert[:], owner[:]).then_inc(have_experts, 1)


class ExpertWeights:

    def __init__(self, nc, io, g, m):
        self.nc, self.g = nc, g
        self.gate_up = [m.sb(f"w_gu{s}", [P, KD, 2 * DE]) for s in range(2)]
        self.down = [m.sb(f"w_dn{s}", [P, DE // P, D]) for s in range(2)]
        self.gate_up_in, self.down_in = m.sems("gu_in", 2), m.sems("dn_in", 2)
        self.gate_v = io["w_exp_gate"][0].rearrange("e (k p) f -> e p k f", p=P)
        self.up_v = io["w_exp_up"][0].rearrange("e (k p) f -> e p k f", p=P)
        self.down_v = io["w_exp_down"][0].rearrange("e (k p) n -> e p k n", p=P)

    def load(self, sp, tile, s, gate_up_used=None, down_used=None):
        e = sp.value_load(self.g.tile_expert[0:1, bass.ds(tile, 1)], min_val=0, max_val=NEXP - 1)
        if gate_up_used:
            sp.wait_ge(*gate_up_used)
        for at, src in ((0, self.gate_v), (DE, self.up_v)):
            sp.dma_start(self.gate_up[s][:, :, at:at + DE], src[bass.ds(e, 1)].rearrange("a p k f -> (a p) k f"))\
                .then_inc(self.gate_up_in[s], 16)
        if down_used:
            sp.wait_ge(*down_used)
        sp.dma_start(self.down[s][:], self.down_v[bass.ds(e, 1)].rearrange("a p k f -> (a p) k f"))\
            .then_inc(self.down_in[s], 16)


def experts(nc, io, g, ps, weights):
    KE = DE // P
    LAST = SLOT_TILES // 2 - 1
    with ExitStack() as ctx:
        m = Mem(nc, ctx, "ex")

        def two(name, shape, dt=F32):
            return [m.sb(f"{name}{s}", shape, dt) for s in range(2)]

        w_gu, w_dn, gu_in, dn_in = weights.gate_up, weights.down, weights.gate_up_in, weights.down_in
        x, y, who = two("x", [P, D]), two("y", [P, D]), two("who", [P, 1], I32)
        xT, gate, act_in, aT = two("xT", [P, KD, P]), two("gate", [P, DE]), two("act_in", [P, DE]), two("aT", [P, KE, P])
        x_in, who_set = m.sems("x_in", 2), m.sems("who_set", 2)
        who_seen = m.sem("who_seen")
        xT_full, xT_copied, y_copied = ([m.sems(f"{n}{h}", 2) for h in range(2)] for n in ("xT_full", "xT_copied", "y_copied"))
        gu_full, gated, a_done, aT_full, aT_copied, y_full, stored = (
            m.sems(n, 2) for n in ("gu_full", "gated", "a_done", "aT_full", "aT_copied", "y_full", "stored"))
        y_v = g.y_rows.rearrange("(t p) n -> t p n", p=P)

        def wait_before(eng, sems, use, s):
            if s:
                eng.wait_ge(sems[0], START + use + 1)
            else:
                eng.wait_ge(sems[1], START + use)

        m.start(gu_full + y_full + xT_full[0] + xT_full[1] + xT_copied[0] + xT_copied[1] + a_done + aT_copied
                + y_copied[0] + y_copied[1] + aT_full + stored)

        with nc.Block() as block:
            @block.sync
            def _(sp):
                with sp.Fori(1, LAST + 1) as use:
                    for s in range(2):
                        weights.load(sp, 2 * use + s, s, (gu_full[s], START + use), (y_full[s], START + use))

            @block.gpsimd
            def _(pool):
                with pool.Fori(0, LAST + 1) as use:
                    for s in range(2):
                        for half in range(2):
                            pool.wait_ge(xT_full[half][s], START + use)
                        nc.gpsimd.tensor_copy(who[s][:], g.slot_list[:, bass.ds(2 * use + s, 1)]).then_inc(who_set[s], 1)
                        pool.wait_ge(who_set[s], use + 1)
                        pool.sem_inc(who_seen, 1)
                        pool.indirect_dma_start(x[s][:], None, g.h2_rows, bass.IndirectOffsetOnAxis(who[s][:, 0:1], 0))\
                            .then_inc(x_in[s], 16)

            @block.tensor
            def _(pe):
                def x_transposes(use, s):
                    pe.wait_ge(x_in[s], 16 * use + 16)
                    for half in range(2):
                        wait_before(pe, xT_copied[half], use, s)
                        for k in range(4):
                            last = nc.tensor.transpose(ps[:, half, k * P:(k + 1) * P],
                                                       x[s][:, (4 * half + k) * P:(4 * half + k + 1) * P], g.ident[:])
                        last.then_inc(xT_full[half][s], 1)

                def gate_up(use, s):
                    for half in range(2):
                        pe.wait_ge(xT_copied[half][s], START + use + 1)
                    pe.wait_ge(gu_in[s], 32 * use + 32)
                    pe.wait_ge(a_done[s], START + use)
                    for k in range(KD):
                        last = nc.tensor.matmul(ps[:, 2 + s, :], xT[s][:, k, :], w_gu[s][:, k, :], start=(k == 0),
                                                stop=(k == KD - 1))
                    last.then_inc(gu_full[s], 1)

                def a_transposes(use, s):
                    pe.wait_ge(a_done[s], START + use + 1)
                    pe.wait_ge(aT_copied[s], START + use)
                    for k in range(KE):
                        last = nc.tensor.transpose(ps[:, 4 + s, k * P:(k + 1) * P], act_in[s][:, k * P:(k + 1) * P],
                                                   g.ident[:])
                    last.then_inc(aT_full[s], 1)

                def down(use, s):
                    pe.wait_ge(aT_copied[s], START + use + 1)
                    pe.wait_ge(dn_in[s], 16 * use + 16)
                    for half in range(2):
                        wait_before(pe, y_copied[half], use, s)
                    for half in range(2):
                        for k in range(KE):
                            last = nc.tensor.matmul(ps[:, 6 + half, :], aT[s][:, k, :],
                                                    w_dn[s][:, k, half * 512:(half + 1) * 512], start=(k == 0),
                                                    stop=(k == KE - 1))
                    last.then_inc(y_full[s], 1)

                x_transposes(0, 0)
                gate_up(0, 0)
                x_transposes(0, 1)
                with pe.Fori(0, LAST) as use:
                    for s in range(2):
                        gate_up(use + s, 1 - s)
                        a_transposes(use, s)
                        x_transposes(use + 1, s)
                        down(use, s)
                gate_up(LAST, 1)
                for s in range(2):
                    a_transposes(LAST, s)
                    down(LAST, s)

            def copy_x(eng, copy, half, use, s):
                eng.wait_ge(xT_full[half][s], START + use + 1)
                copy(xT[s][:, 4 * half:4 * half + 4, :], ps[:, half, :].rearrange("p (k n) -> p k n", k=4))\
                    .then_inc(xT_copied[half][s], 1)

            def copy_y(eng, copy, half, use, s):
                eng.wait_ge(y_full[s], START + use + 1)
                eng.wait_ge(stored[s], START + 16 * use)
                copy(y[s][:, half * 512:(half + 1) * 512], ps[:, 6 + half, :]).then_inc(y_copied[half][s], 1)

            @block.vector
            def _(dve):
                copy = nc.vector.tensor_copy

                def activations(use, s):
                    dve.wait_ge(gated[s], use + 1)
                    dve.wait_ge(aT_full[s], START + use)
                    nc.vector.tensor_tensor(act_in[s][:], ps[:, 2 + s, DE:2 * DE], gate[s][:], ALU.mult)\
                        .then_inc(a_done[s], 1)

                def copy_a(use, s):
                    dve.wait_ge(aT_full[s], START + use + 1)
                    copy(aT[s][:], ps[:, 4 + s, 0:KE * P].rearrange("p (k n) -> p k n", k=KE)).then_inc(aT_copied[s], 1)

                copy_x(dve, copy, 0, 0, 0)
                activations(0, 0)
                copy_x(dve, copy, 0, 0, 1)
                with dve.Fori(0, LAST) as use:
                    for s in range(2):
                        copy_a(use, s)
                        activations(use + s, 1 - s)
                        copy_x(dve, copy, 0, use + 1, s)
                        copy_y(dve, copy, 0, use, s)
                copy_a(LAST, 0)
                activations(LAST, 1)
                copy_y(dve, copy, 0, LAST, 0)
                copy_a(LAST, 1)
                copy_y(dve, copy, 0, LAST, 1)

            @block.scalar
            def _(act):
                copy = nc.scalar.copy

                def silu(use, s):
                    act.wait_ge(gu_full[s], START + use + 1)
                    act.wait_ge(a_done[s], START + use)
                    nc.scalar.activation(gate[s][:], ps[:, 2 + s, 0:DE], ACT.Silu).then_inc(gated[s], 1)

                def store(use, s):
                    for half in range(2):
                        act.wait_ge(y_copied[half][s], START + use + 1)
                    act.dma_start(y_v[bass.ds(2 * use + s, 1)].rearrange("a p n -> (a p) n"), y[s][:])\
                        .then_inc(stored[s], 16)

                nc.scalar.preload_act_table(ACT.Silu)
                copy_x(act, copy, 1, 0, 0)
                silu(0, 0)
                copy_x(act, copy, 1, 0, 1)
                with act.Fori(0, LAST) as use:
                    for s in range(2):
                        silu(use + s, 1 - s)
                        copy_x(act, copy, 1, use + 1, s)
                        copy_y(act, copy, 1, use, s)
                        store(use, s)
                silu(LAST, 1)
                for s in range(2):
                    copy_y(act, copy, 1, LAST, s)
                    store(LAST, s)
                for s in range(2):
                    act.wait_ge(stored[s], START + 16 * (LAST + 1))


def combine(nc, io, g, ps):
    with ExitStack() as ctx:
        m = Mem(nc, ctx, "cb")
        ya, yb, r_t, out_t = ([m.sb(f"{n}{i}", [P, D]) for i in range(2)] for n in ("ya", "yb", "r", "out"))
        ln_g, ln_b, eps = m.sb("ln_g", [P, D]), m.sb("ln_b", [P, D]), m.sb("eps", [P, 1])
        norm = Norm(m, eps, ln_g, ln_b)
        par_in, eps_set, own, weighted_own = m.sem("par_in"), m.sem("eps_set"), m.sem("own"), m.sem("weighted_own")
        y_in, weighted, added, scaled, summed, ready, out = (
            m.sems(n, 2) for n in ("y_in", "weighted", "added", "scaled", "summed", "ready", "out"))
        y_out = [io["y_prompt"][0, t * P:(t + 1) * P, :] for t in range(PT)] + [io["y_sample"].rearrange("b s d -> (b s) d")]

        with nc.Block() as block:
            @block.sync
            def _(sp):
                for dst, src in ((ln_g, io["ln2_g"]), (ln_b, io["ln2_b"])):
                    sp.dma_start(dst[:], src.partition_broadcast(P).rearrange("p a n -> p (a n)")).then_inc(par_in, 16)
                for t in range(NT):
                    rows, b = TILE_ROWS[t], t % 2
                    sp.wait_ge(ready[b], t // 2 + 1)
                    sp.dma_start(y_out[t], out_t[b][0:rows, :]).then_inc(out[b], 16)
                for b in range(2):
                    sp.wait_ge(out[b], 16 * ((NT + 1 - b) // 2))

            @block.gpsimd
            def _(pool):
                nc.gpsimd.memset(eps[:], EPS).then_inc(eps_set, 1)

                def gather(t):
                    rows, b = TILE_ROWS[t], t % 2
                    if t >= 2:
                        pool.wait_ge(added[b], t // 2)
                    for i, dst in enumerate((ya, yb)):
                        pool.indirect_dma_start(dst[b][0:rows, :], None, g.y_rows,
                                                bass.IndirectOffsetOnAxis(g.slot[0:rows, i, t:t + 1], 0))\
                            .then_inc(y_in[b], 16)

                gather(0)
                for t in range(NT):
                    rows, b = TILE_ROWS[t], t % 2
                    if t + 1 < NT:
                        gather(t + 1)
                    pool.wait_ge(added[b], t // 2 + 1)
                    nc.gpsimd.tensor_tensor(r_t[b][0:rows, :], r_t[b][0:rows, :],
                                            g.rows["g2"][0 if t < PT else 1][0:rows, :], ALU.mult).then_inc(scaled[b], 1)

            @block.scalar
            def _(act):
                def weigh(t):
                    rows, b = TILE_ROWS[t], t % 2
                    act.wait_ge(y_in[b], 32 * (t // 2) + 32)
                    nc.scalar.activation(ya[b][0:rows, :], ya[b][0:rows, :], ACT.Copy,
                                         scale=g.weight[0:rows, 0, t:t + 1]).then_inc(weighted[b], 1)

                act.wait_ge(eps_set, 1)
                weigh(0)
                for t in range(NT):
                    if t + 1 < NT:
                        weigh(t + 1)
                    norm.deviation(nc, act, t, TILE_ROWS[t])

            @block.vector
            def _(dve):
                link = Chain(dve, own)
                dve.wait_ge(par_in, 32)

                def add(t):
                    rows, b = TILE_ROWS[t], t % 2
                    if t >= 2:
                        dve.wait_ge(ready[b], t // 2)
                    dve.wait_ge(weighted[b], t // 2 + 1)
                    nc.vector.scalar_tensor_tensor(out=r_t[b][0:rows, :], in0=yb[b][0:rows, :],
                                                   scalar=g.weight[0:rows, 1, t:t + 1], in1=ya[b][0:rows, :],
                                                   op0=ALU.mult, op1=ALU.add).then_inc(added[b], 1)

                add(0)
                for t in range(NT):
                    rows, b = TILE_ROWS[t], t % 2
                    r = r_t[b]
                    dve.wait_ge(scaled[b], t // 2 + 1)
                    link(nc.vector.scalar_tensor_tensor(out=r[0:rows, :], in0=g.x1[0:rows, t, :], scalar=ALPHA,
                                                        in1=r[0:rows, :], op0=ALU.mult, op1=ALU.add))
                    norm.variance(nc, link, r, rows)
                    if t + 1 < NT:
                        add(t + 1)
                    if t >= 2:
                        dve.wait_ge(out[b], 16 * (t // 2))
                    norm.apply(nc, dve, link, t, out_t[b][0:rows, :], r, rows).then_inc(ready[b], 1)


class Shared:
    pass


def hybrid_decoder_step(nc, inputs, outputs):
    io = {**inputs, **outputs}
    g = Shared()
    with ExitStack() as ctx:
        m = Mem(nc, ctx, "g")

        def scratch(name, shape, dt=F32):
            return nc.dram_tensor(name, shape, dt, kind="Internal").ap()

        g.ada_rows = scratch("ada_rows", [NB, 4, D])
        g.q_rows = scratch("q_rows", [NS, DA])
        g.h2_rows = scratch("h2_rows", [T, D])
        g.slot_token = scratch("slot_token", [SLOT_TILES * P, 1], I32)
        g.y_rows = scratch("y_rows", [SLOT_TILES * P, D])
        ps = ctx.enter_context(nc.psum_tensor("ps", [P, 8, 512], F32))
        g.ident, g.before, g.causal = (m.sb(name, [P, P]) for name in ("ident", "before", "causal"))
        g.after, g.ones = m.sb("after", [P, 4 * P]), m.sb("ones", [P, 4 * P])
        g.csT = m.sb("csT", [P, KD, NB])
        g.ncum, g.ncum_new = m.sb("ncum", [P, NT, H]), m.sb("ncum_new", [H, NS])
        g.hT_odd, g.xT_odd = m.sems("hT_odd", 4), m.sems("xT_odd", 4)
        g.arena = m.sb("arena", [P, (KD + DA // P + NGRP) * T])
        part, at = {}, 0
        for name, k in (("hT", KD), ("aT", DA // P), ("uT", NGRP)):
            part[name] = g.arena[:, at:at + k * T].rearrange("p (k n) -> p k n", k=k)
            at += k * T
        g.hT, g.aT, g.uT = part["hT"], part["aT"], part["uT"]
        modulate(nc, io, g, ps)
        with ExitStack() as z_ctx:
            z_mem = Mem(nc, z_ctx, "z")
            g.z = z_mem.sb("z", [P, 2, 2, NT, 512])
            with ExitStack() as u_ctx:
                u_mem = Mem(nc, u_ctx, "u")
                u_and_f = (u_mem.sb("w_u", [P, KD, DG]), u_mem.sb("w_f", [P, KD, H]), u_mem.sb("bf", [H, 1]),
                           u_mem.sem("u_in"), u_mem.sem("f_in"))
                project_in(nc, io, g, ps, *u_and_f)
                gmlp(nc, io, g, ps, *u_and_f)
            attend_prompt(nc, io, g, ps)
        attend_sample(nc, io, g, ps)
        g.logits, g.weight = m.sb("logits", [P, NT, NG + NEXP]), m.sb("weight", [P, 2, NT])
        g.slot, g.slot_list = m.sb("slot", [P, 2, NT], I32), m.sb("slot_list", [P, SLOT_TILES], I32)
        g.tile_expert = m.sb("tile_expert", [1, SLOT_TILES], I32)
        g2 = m.sb("g2", [P, 2, D])
        with ExitStack() as m_ctx:
            mT = Mem(nc, m_ctx, "m").sb("mT", [P, KD, T])
            mix(nc, io, g, ps, mT)
            g.x1 = g.arena[:, 0:NT * D].rearrange("p (t n) -> p t n", t=NT)
            at = NT * D
            g.rows = {"g2": (g2[:, 0, :], g2[:, 1, :])}
            for name in ("g1", "sc2", "sh2"):
                g.rows[name] = (g.arena[:, at:at + D], g.arena[:, at + D:at + 2 * D])
                at += 2 * D
            g.ln_g = g.arena[:, at:at + D]
            mixer_out(nc, io, g, ps, mT)
        with ExitStack() as w_ctx:
            weights = ExpertWeights(nc, io, g, Mem(nc, w_ctx, "w"))
            route(nc, io, g, ps, weights.load)
            experts(nc, io, g, ps, weights)
        combine(nc, io, g, ps)


OUTPUTS = {
    "y_prompt": (1, SEQ, D), "y_sample": (DEC_B, DEC_S, D),
    "new_k_prompt": (1, 1, SEQ, H, HD), "new_v_prompt": (1, 1, SEQ, H, HD), "new_logf_prompt": (1, 1, SEQ, H),
    "new_k_sample": (1, DEC_B, DEC_S, H, HD), "new_v_sample": (1, DEC_B, DEC_S, H, HD),
    "new_logf_sample": (1, DEC_B, DEC_S, H), "new_gmlp_v_sample": (1, DEC_B, DEC_S, DG),
}


def kernel(**inputs):
    import concourse.bacc as bacc
    from concourse.bass_utils import run_bass_kernel_spmd

    nc = bacc.Bacc("TRN2", target_bir_lowering=False, num_devices=1)
    arrays = {name: np.ascontiguousarray(a) for name, a in inputs.items()}
    ins = {name: nc.dram_tensor(name, a.shape, mybir.dt.from_np(a.dtype), kind="ExternalInput").ap()
           for name, a in arrays.items()}
    outs = {name: nc.dram_tensor(name, shape, F32, kind="ExternalOutput").ap() for name, shape in OUTPUTS.items()}
    hybrid_decoder_step(nc, ins, outs)
    result = run_bass_kernel_spmd(nc, [arrays], core_ids=[0])
    return tuple(result.results[0][name] for name in OUTPUTS)
```
